# Optimizing a Trainium2 kernel written in Bass

```python
import jax, jax.numpy as jnp
from jax import lax
import numpy as np

D_MODEL = 1024
BATCH = 1
SEQ = 512
DEPTH = 1

CHUNK = 64
Q_BLOCK = 128
ROPE_THETA = 500000.0
EPS = 1e-6
NEG = -1e30

MLA_HEADS = 8
MLA_Q_LORA = 384
MLA_KV_LORA = 256
MLA_NOPE = 64
MLA_ROPE = 32
MLA_V = 64

DSA_HEADS = 8
DSA_HEAD_DIM = 64
DSA_ROT = DSA_HEAD_DIM // 4
IDX_HEADS = 8
IDX_DIM = 64
IDX_ROT = IDX_DIM // 4
DSA_TOPK_MAX = 256

N_GROUPS = 8
EXPERTS_PER_GROUP = 4
N_EXPERTS = N_GROUPS * EXPERTS_PER_GROUP
EXPERT_FF = 256
TOPK_IN_GROUP = 2

IN_SIZES = (
    MLA_Q_LORA,
    MLA_KV_LORA,
    MLA_ROPE,
    DSA_HEADS * DSA_HEAD_DIM,
    DSA_HEADS * DSA_HEAD_DIM,
    DSA_HEADS * DSA_HEAD_DIM,
    IDX_HEADS * IDX_DIM,
    IDX_DIM,
    IDX_HEADS,
    D_MODEL,
    D_MODEL,
)
IN_WIDTH = sum(IN_SIZES)


def rmsnorm(x, g):
    xf = x.astype(jnp.float32)
    y = xf * lax.rsqrt(jnp.mean(xf * xf, axis=-1, keepdims=True) + EPS)
    return (y * g.astype(jnp.float32)).astype(x.dtype)

def rope(x, pos, rot_dim):
    half = rot_dim // 2
    inv_freq = ROPE_THETA ** (-jnp.arange(half, dtype=jnp.float32) * 2.0 / rot_dim)
    ang = pos.astype(jnp.float32)[:, None] * inv_freq[None, :]
    cos = jnp.cos(ang)[:, None, :]
    sin = jnp.sin(ang)[:, None, :]
    xr = x[..., :rot_dim].astype(jnp.float32)
    x1, x2 = xr[..., :half], xr[..., half:]
    rot = jnp.concatenate([x1 * cos - x2 * sin, x2 * cos + x1 * sin], axis=-1).astype(x.dtype)
    return jnp.concatenate([rot, x[..., rot_dim:]], axis=-1)

def _to_blocks(a):
    b, s = a.shape[0], a.shape[1]
    return a.reshape(b, s // Q_BLOCK, Q_BLOCK, *a.shape[2:]).swapaxes(0, 1)

def _from_blocks(a):
    a = a.swapaxes(0, 1)
    return a.reshape(a.shape[0], a.shape[1] * a.shape[2], *a.shape[3:])

def chunk_causal_attention(q, k, v, scale):
    s_len = q.shape[1]
    nb = s_len // Q_BLOCK
    key_chunk = jnp.arange(s_len) // CHUNK

    def one_block(args):
        qi, bi = args
        q_chunk = (bi * Q_BLOCK + jnp.arange(Q_BLOCK)) // CHUNK
        mask = key_chunk[None, :] <= q_chunk[:, None]
        s = jnp.einsum('bqhd,bkhd->bhqk', qi, k).astype(jnp.float32) * scale
        s = jnp.where(mask[None, None], s, NEG)
        p = jax.nn.softmax(s, axis=-1).astype(v.dtype)
        return jnp.einsum('bhqk,bkhd->bqhd', p, v)

    out = lax.map(one_block, (_to_blocks(q), jnp.arange(nb)))
    return _from_blocks(out)

def indexed_sparse_attention(q, k, v, q_idx, k_idx, w_idx, top_k):
    s_len = q.shape[1]
    nb = s_len // Q_BLOCK
    key_chunk = jnp.arange(s_len) // CHUNK
    gather = jax.vmap(lambda a, i: a[i])

    def one_block(args):
        qi, qii, wi, bi = args
        q_chunk = (bi * Q_BLOCK + jnp.arange(Q_BLOCK)) // CHUNK
        adm = key_chunk[None, :] <= q_chunk[:, None]
        logits = jnp.einsum('bqhd,bkd->bqhk', qii, k_idx).astype(jnp.float32) * (IDX_DIM ** -0.5)
        score = jnp.einsum('bqh,bqhk->bqk', wi.astype(jnp.float32), jax.nn.relu(logits))
        score = jnp.where(adm[None], score, -jnp.inf)
        _, sel = lax.top_k(score, top_k)
        sel_ok = (sel // CHUNK) <= q_chunk[None, :, None]
        k_sel = gather(k, sel)
        v_sel = gather(v, sel)
        s = jnp.einsum('bqhd,bqkhd->bhqk', qi, k_sel).astype(jnp.float32) * (DSA_HEAD_DIM ** -0.5)
        s = jnp.where(sel_ok[:, None], s, NEG)
        p = jax.nn.softmax(s, axis=-1).astype(v.dtype)
        return jnp.einsum('bhqk,bqkhd->bqhd', p, v_sel)

    out = lax.map(one_block, (_to_blocks(q), _to_blocks(q_idx), _to_blocks(w_idx), jnp.arange(nb)))
    return _from_blocks(out)

def hierarchical_moe(h, w_router_group, b_router_group, w_router_expert, b_router_expert,
                     w_gate, w_up, w_down):
    t = h.shape[0]
    group_logits = jnp.matmul(h, w_router_group).astype(jnp.float32) + b_router_group.astype(jnp.float32)
    p_group = jax.nn.softmax(group_logits, axis=-1)
    g_sel = jnp.argmax(group_logits, axis=-1)
    w_grp = jnp.take_along_axis(p_group, g_sel[:, None], axis=-1)
    exp_logits = (jnp.matmul(h, w_router_expert).astype(jnp.float32)
                  + b_router_expert.astype(jnp.float32)).reshape(t, N_GROUPS, EXPERTS_PER_GROUP)
    in_group = jnp.take_along_axis(exp_logits, g_sel[:, None, None], axis=1)[:, 0]
    top_vals, top_idx = lax.top_k(in_group, TOPK_IN_GROUP)
    w_top = jax.nn.softmax(top_vals, axis=-1) * w_grp
    expert_id = g_sel[:, None] * EXPERTS_PER_GROUP + top_idx
    combine = jnp.sum(jax.nn.one_hot(expert_id, N_EXPERTS, dtype=jnp.float32) * w_top[..., None],
                      axis=1).astype(h.dtype)
    out = jnp.zeros_like(h)
    for e in range(N_EXPERTS):
        hid = jax.nn.silu(jnp.matmul(h, w_gate[e])) * jnp.matmul(h, w_up[e])
        out = out + jnp.matmul(hid, w_down[e]) * combine[:, e:e + 1]
    return out

def hybrid_layer(x, pos, norm_mix_g, w_in, mla_q_norm_g, w_uq, mla_kv_norm_g, w_uk, w_uv,
                 w_o_a, w_o_b, w_out, norm_ffn_g, w_router_group, b_router_group,
                 w_router_expert, b_router_expert, w_gate, w_up, w_down):
    b, s, d = x.shape
    h = rmsnorm(x, norm_mix_g)
    proj = jnp.einsum('bsd,de->bse', h, w_in)
    splits = np.cumsum(IN_SIZES)[:-1].tolist()
    (c_q, c_kv, k_r, q_b, k_b, v_b, q_i, k_i, w_i, g_a, g_b) = jnp.split(proj, splits, axis=-1)

    c_q = rmsnorm(c_q, mla_q_norm_g)
    q_a = jnp.einsum('bsr,re->bse', c_q, w_uq).reshape(b, s, MLA_HEADS, MLA_NOPE + MLA_ROPE)
    q_a = jnp.concatenate([q_a[..., :MLA_NOPE], rope(q_a[..., MLA_NOPE:], pos, MLA_ROPE)], axis=-1)
    c_kv = rmsnorm(c_kv, mla_kv_norm_g)
    k_nope = jnp.einsum('bsr,re->bse', c_kv, w_uk).reshape(b, s, MLA_HEADS, MLA_NOPE)
    v_a = jnp.einsum('bsr,re->bse', c_kv, w_uv).reshape(b, s, MLA_HEADS, MLA_V)
    k_pe = rope(k_r[:, :, None, :], pos, MLA_ROPE)
    k_a = jnp.concatenate([k_nope, jnp.broadcast_to(k_pe, (b, s, MLA_HEADS, MLA_ROPE))], axis=-1)
    o_a = chunk_causal_attention(q_a, k_a, v_a, (MLA_NOPE + MLA_ROPE) ** -0.5)
    y_a = jnp.einsum('bse,ed->bsd', o_a.reshape(b, s, MLA_HEADS * MLA_V), w_o_a)

    q_b = rope(q_b.reshape(b, s, DSA_HEADS, DSA_HEAD_DIM), pos, DSA_ROT)
    k_b = rope(k_b.reshape(b, s, DSA_HEADS, DSA_HEAD_DIM), pos, DSA_ROT)
    v_b = v_b.reshape(b, s, DSA_HEADS, DSA_HEAD_DIM)
    q_i = rope(q_i.reshape(b, s, IDX_HEADS, IDX_DIM), pos, IDX_ROT)
    k_i = rope(k_i[:, :, None, :], pos, IDX_ROT)[:, :, 0, :]
    top_k = min(DSA_TOPK_MAX, s // 4)
    o_b = indexed_sparse_attention(q_b, k_b, v_b, q_i, k_i, w_i * (IDX_HEADS ** -0.5), top_k)
    y_b = jnp.einsum('bse,ed->bsd', o_b.reshape(b, s, DSA_HEADS * DSA_HEAD_DIM), w_o_b)

    y = jax.nn.sigmoid(g_a) * y_a + jax.nn.sigmoid(g_b) * y_b
    x = x + jnp.einsum('bsd,de->bse', y, w_out)

    h2 = rmsnorm(x, norm_ffn_g).reshape(b * s, d)
    m = hierarchical_moe(h2, w_router_group, b_router_group, w_router_expert, b_router_expert,
                         w_gate, w_up, w_down)
    return x + m.reshape(b, s, d)

def first_inputs(seed: int = 0) -> dict:
    key = jax.random.key(seed)
    ks = jax.random.split(key, 20)
    f32 = jnp.float32
    L = DEPTH

    def dense(k, shape, fan_in):
        return jax.random.normal(k, shape, f32) * (fan_in ** -0.5)

    def gain(k, shape):
        return 1.0 + 0.05 * jax.random.normal(k, shape, f32)

    return {
        'x': jax.random.normal(ks[0], (BATCH, SEQ, D_MODEL), f32),
        'norm_mix_g': gain(ks[1], (L, D_MODEL)),
        'w_in': dense(ks[2], (L, D_MODEL, IN_WIDTH), D_MODEL),
        'mla_q_norm_g': gain(ks[3], (L, MLA_Q_LORA)),
        'w_uq': dense(ks[4], (L, MLA_Q_LORA, MLA_HEADS * (MLA_NOPE + MLA_ROPE)), MLA_Q_LORA),
        'mla_kv_norm_g': gain(ks[5], (L, MLA_KV_LORA)),
        'w_uk': dense(ks[6], (L, MLA_KV_LORA, MLA_HEADS * MLA_NOPE), MLA_KV_LORA),
        'w_uv': dense(ks[7], (L, MLA_KV_LORA, MLA_HEADS * MLA_V), MLA_KV_LORA),
        'w_o_a': dense(ks[8], (L, MLA_HEADS * MLA_V, D_MODEL), MLA_HEADS * MLA_V),
        'w_o_b': dense(ks[9], (L, DSA_HEADS * DSA_HEAD_DIM, D_MODEL), DSA_HEADS * DSA_HEAD_DIM),
        'w_out': dense(ks[10], (L, D_MODEL, D_MODEL), D_MODEL),
        'norm_ffn_g': gain(ks[11], (L, D_MODEL)),
        'w_router_group': dense(ks[12], (L, D_MODEL, N_GROUPS), D_MODEL),
        'b_router_group': 0.01 * jax.random.normal(ks[13], (L, N_GROUPS), f32),
        'w_router_expert': dense(ks[14], (L, D_MODEL, N_EXPERTS), D_MODEL),
        'b_router_expert': 0.01 * jax.random.normal(ks[15], (L, N_EXPERTS), f32),
        'w_gate': dense(ks[16], (L, N_EXPERTS, D_MODEL, EXPERT_FF), D_MODEL),
        'w_up': dense(ks[17], (L, N_EXPERTS, D_MODEL, EXPERT_FF), D_MODEL),
        'w_down': dense(ks[18], (L, N_EXPERTS, EXPERT_FF, D_MODEL), EXPERT_FF),
        'final_norm_g': gain(ks[19], (D_MODEL,)),
    }

def first_block(x, norm_mix_g, w_in, mla_q_norm_g, w_uq, mla_kv_norm_g, w_uk, w_uv, w_o_a, w_o_b,
              w_out, norm_ffn_g, w_router_group, b_router_group, w_router_expert, b_router_expert,
              w_gate, w_up, w_down, final_norm_g):
    pos = jnp.arange(x.shape[1], dtype=jnp.int32)
    for l in range(DEPTH):
        x = hybrid_layer(x, pos, norm_mix_g[l], w_in[l], mla_q_norm_g[l], w_uq[l], mla_kv_norm_g[l],
                         w_uk[l], w_uv[l], w_o_a[l], w_o_b[l], w_out[l], norm_ffn_g[l],
                         w_router_group[l], b_router_group[l], w_router_expert[l],
                         b_router_expert[l], w_gate[l], w_up[l], w_down[l])
    return rmsnorm(x, final_norm_g)


MEM_LEN = 256
HEAD_DIM = 64
SB_HEADS = 8
SB_WIDTH = SB_HEADS * HEAD_DIM
DIL_CONFIG = ((128, 1), (512, 4), (2048, 16))
N_DIL_GROUPS = 3
DIL_HEADS_PER_GROUP = 4
DIL_HEADS = N_DIL_GROUPS * DIL_HEADS_PER_GROUP
DIL_WIDTH = DIL_HEADS * HEAD_DIM
DIL_OUT_WIDTH = DIL_HEADS_PER_GROUP * HEAD_DIM
DIL_STREAM_KEYS = 128
ALIBI_MAX_BIAS = 8.0
MEM_HEADS = 4
MEM_HEAD_DIM = 128
MEM_WIDTH = MEM_HEADS * MEM_HEAD_DIM
N_BRANCHES = 3
IN_WIDTH_2 = 3 * SB_WIDTH + 3 * DIL_WIDTH + MEM_WIDTH
IN_SPLITS = (SB_WIDTH, 2 * SB_WIDTH, 3 * SB_WIDTH,
             3 * SB_WIDTH + DIL_WIDTH, 3 * SB_WIDTH + 2 * DIL_WIDTH, 3 * SB_WIDTH + 3 * DIL_WIDTH)
PEER_HEADS = 8
PEER_KEYS = 128
PEER_EXPERTS = PEER_KEYS * PEER_KEYS
PEER_TOPK = 16
PEER_QDIM = 256
PEER_HALF = PEER_QDIM // 2
PEER_CHUNK = 128


def rms_norm(x, g):
    xf = x.astype(jnp.float32)
    y = xf * lax.rsqrt(jnp.mean(xf * xf, axis=-1, keepdims=True) + EPS)
    return (y * g.astype(jnp.float32)).astype(x.dtype)

def alibi_slopes(n):
    return jnp.exp2(-ALIBI_MAX_BIAS * jnp.arange(1, n + 1, dtype=jnp.float32) / n)

def stick_breaking_attention(q, k, v):
    B, H, S, dh = q.shape
    nb = S // Q_BLOCK
    q_blocks = q.reshape(B, H, nb, Q_BLOCK, dh).transpose(2, 0, 1, 3, 4)
    kpos = jnp.arange(S)
    scale = dh ** -0.5

    def block(args):
        q_blk, n = args
        z = jnp.einsum('bhqd,bhkd->bhqk', q_blk, k).astype(jnp.float32) * scale
        qpos = n * Q_BLOCK + jnp.arange(Q_BLOCK)
        past = kpos[None, :] < qpos[:, None]
        log_keep = jnp.where(past, jax.nn.log_sigmoid(-z), 0.0)
        between = lax.cumsum(log_keep, axis=3, reverse=True) - log_keep
        a = jnp.where(past, jnp.exp(jax.nn.log_sigmoid(z) + between), 0.0)
        return jnp.einsum('bhqk,bhkd->bhqd', a.astype(v.dtype), v)

    o = lax.map(block, (q_blocks, jnp.arange(nb)))
    return o.transpose(1, 2, 0, 3, 4).reshape(B, H, S, dh)

def dilated_group_attention(q, k, v, dilation, slopes):
    B, S, H, dh = q.shape
    L = S // dilation
    nb = -(-L // Q_BLOCK)
    Lp = nb * Q_BLOCK

    def to_streams(t):
        t = t.reshape(B, L, dilation, H, dh).transpose(0, 2, 3, 1, 4)
        t = jnp.pad(t, ((0, 0), (0, 0), (0, 0), (0, Lp - L), (0, 0)))
        return t.reshape(B, dilation, H, nb, Q_BLOCK, dh)

    qs, ks, vs = to_streams(q), to_streams(k), to_streams(v)

    def with_prev(t):
        prev = jnp.pad(t, ((0, 0), (0, 0), (0, 0), (1, 0), (0, 0), (0, 0)))[:, :, :, :nb]
        return jnp.concatenate([prev, t], axis=4)

    kc, vc = with_prev(ks), with_prev(vs)
    qi = jnp.arange(Q_BLOCK)
    kj = jnp.arange(2 * Q_BLOCK) - Q_BLOCK
    gap = qi[:, None] - kj[None, :]
    blk = jnp.arange(nb)
    valid = ((gap >= 0) & (gap <= DIL_STREAM_KEYS))[None] & \
            ((blk[:, None, None] * Q_BLOCK + kj[None, None, :]) >= 0)
    s = jnp.einsum('brhnqd,brhnkd->brhnqk', qs, kc).astype(jnp.float32) * dh ** -0.5
    s = s - slopes[:, None, None, None] * (gap * dilation).astype(jnp.float32)
    s = jnp.where(valid, s, -1e30)
    lse = jax.nn.logsumexp(s, axis=-1)
    p = jnp.exp(s - lse[..., None])
    o = jnp.einsum('brhnqk,brhnkd->brhnqd', p.astype(v.dtype), vc)
    o = o.reshape(B, dilation, H, Lp, dh)[:, :, :, :L].transpose(0, 3, 1, 2, 4).reshape(B, S, H, dh)
    lse = lse.reshape(B, dilation, H, Lp)[..., :L].transpose(0, 3, 1, 2).reshape(B, S, H)
    return o, lse

def dilated_mixture(q, k, v, g_q, g_k):
    q = rms_norm(q, g_q)
    k = rms_norm(k, g_k)
    slopes = alibi_slopes(DIL_HEADS)
    outs, lses = [], []
    for g, (window, dilation) in enumerate(DIL_CONFIG):
        hs = slice(g * DIL_HEADS_PER_GROUP, (g + 1) * DIL_HEADS_PER_GROUP)
        o, lse = dilated_group_attention(q[:, :, hs], k[:, :, hs], v[:, :, hs], dilation, slopes[hs])
        outs.append(o)
        lses.append(lse)
    w = jax.nn.softmax(jnp.stack(lses, axis=2), axis=2)
    o = jnp.stack(outs, axis=2)
    return jnp.sum(w[..., None].astype(o.dtype) * o, axis=2)

def memory_attention(q, mem_h, w_kv, g_q, g_k):
    B, M, _ = mem_h.shape
    kv = (mem_h @ w_kv).reshape(B, M, 2, MEM_HEADS, MEM_HEAD_DIM)
    k = rms_norm(kv[:, :, 0], g_k)
    v = kv[:, :, 1]
    q = rms_norm(q, g_q)
    s = jnp.einsum('bshd,bmhd->bhsm', q, k).astype(jnp.float32) * MEM_HEAD_DIM ** -0.5
    p = jax.nn.softmax(s, axis=-1)
    return jnp.einsum('bhsm,bmhd->bshd', p.astype(v.dtype), v)

def peer_ffn(h, w_q, subkeys, u, v):
    B, S, D = h.shape
    T = B * S
    hf = h.reshape(T, D)
    q = (hf @ w_q).reshape(T, PEER_HEADS, 2, PEER_HALF)
    sc = jnp.einsum('thpd,hpkd->thpk', q, subkeys).astype(jnp.float32)
    s1, i1 = lax.top_k(sc[:, :, 0], PEER_TOPK)
    s2, i2 = lax.top_k(sc[:, :, 1], PEER_TOPK)
    cand = (s1[..., :, None] + s2[..., None, :]).reshape(T, PEER_HEADS, PEER_TOPK * PEER_TOPK)
    cand_idx = (i1[..., :, None] * PEER_KEYS + i2[..., None, :]).reshape(T, PEER_HEADS, PEER_TOPK * PEER_TOPK)
    top_s, pos = lax.top_k(cand, PEER_TOPK)
    idx = jnp.take_along_axis(cand_idx, pos, axis=-1)
    gate = jax.nn.softmax(top_s, axis=-1)
    nc = T // PEER_CHUNK

    def chunk(args):
        hc, ic, gc = args
        act = jax.nn.gelu(jnp.einsum('chkd,cd->chk', u[ic], hc).astype(jnp.float32), approximate=False)
        w = (gc * act).astype(h.dtype)
        return jnp.einsum('chk,chkd->cd', w, v[ic])

    out = lax.map(chunk, (hf.reshape(nc, PEER_CHUNK, D),
                          idx.reshape(nc, PEER_CHUNK, PEER_HEADS, PEER_TOPK),
                          gate.reshape(nc, PEER_CHUNK, PEER_HEADS, PEER_TOPK)))
    return out.reshape(B, S, D)

def second_inputs(seed: int = 0) -> dict:
    key = jax.random.key(seed)
    ks = jax.random.split(key, 24)
    D = D_MODEL

    def nrm(k, shape, scale):
        return jax.random.normal(k, shape, jnp.float32) * scale

    def gain(k, n):
        return 1.0 + 0.02 * jax.random.normal(k, (DEPTH, n), jnp.float32)

    return {
        'x': nrm(ks[0], (BATCH, SEQ, D), 1.0),
        'mem': nrm(ks[1], (BATCH, MEM_LEN, D), 1.0),
        'g_mix': gain(ks[2], D),
        'g_mem': gain(ks[3], D),
        'w_in': nrm(ks[4], (DEPTH, D, IN_WIDTH_2), D ** -0.5),
        'w_mem_kv': nrm(ks[5], (DEPTH, D, 2 * MEM_WIDTH), D ** -0.5),
        'g_q_dil': gain(ks[6], HEAD_DIM),
        'g_k_dil': gain(ks[7], HEAD_DIM),
        'g_q_mem': gain(ks[8], MEM_HEAD_DIM),
        'g_k_mem': gain(ks[9], MEM_HEAD_DIM),
        'w_o_sb': nrm(ks[10], (DEPTH, SB_WIDTH, D), SB_WIDTH ** -0.5),
        'w_o_dil': nrm(ks[11], (DEPTH, DIL_OUT_WIDTH, D), DIL_OUT_WIDTH ** -0.5),
        'w_o_mem': nrm(ks[12], (DEPTH, MEM_WIDTH, D), MEM_WIDTH ** -0.5),
        'w_gate': nrm(ks[13], (DEPTH, D, N_BRANCHES * D), D ** -0.5),
        'b_gate': nrm(ks[14], (DEPTH, N_BRANCHES * D), 0.02),
        'w_out': nrm(ks[15], (DEPTH, D, D), D ** -0.5),
        'g_ffn': gain(ks[16], D),
        'w_peer_q': nrm(ks[17], (DEPTH, D, PEER_HEADS * PEER_QDIM), D ** -0.5),
        'peer_subkeys': nrm(ks[18], (DEPTH, PEER_HEADS, 2, PEER_KEYS, PEER_HALF), PEER_HALF ** -0.5),
        'peer_u': nrm(ks[19], (DEPTH, PEER_EXPERTS, D), D ** -0.5),
        'peer_v': nrm(ks[20], (DEPTH, PEER_EXPERTS, D), (PEER_HEADS * PEER_TOPK) ** -0.5),
    }

def second_block(x, mem, g_mix, g_mem, w_in, w_mem_kv, g_q_dil, g_k_dil, g_q_mem, g_k_mem,
              w_o_sb, w_o_dil, w_o_mem, w_gate, b_gate, w_out, g_ffn, w_peer_q,
              peer_subkeys, peer_u, peer_v):
    B, S, D = x.shape
    for l in range(DEPTH):
        h = rms_norm(x, g_mix[l])
        proj = h @ w_in[l]
        sb_q, sb_k, sb_v, d_q, d_k, d_v, m_q = jnp.split(proj, IN_SPLITS, axis=-1)

        def sb_heads(t):
            return t.reshape(B, S, SB_HEADS, HEAD_DIM).transpose(0, 2, 1, 3)

        y_sb = stick_breaking_attention(sb_heads(sb_q), sb_heads(sb_k), sb_heads(sb_v))
        y_sb = y_sb.transpose(0, 2, 1, 3).reshape(B, S, SB_WIDTH) @ w_o_sb[l]

        def dil_heads(t):
            return t.reshape(B, S, DIL_HEADS, HEAD_DIM)

        y_dil = dilated_mixture(dil_heads(d_q), dil_heads(d_k), dil_heads(d_v), g_q_dil[l], g_k_dil[l])
        y_dil = y_dil.reshape(B, S, DIL_OUT_WIDTH) @ w_o_dil[l]

        mem_h = rms_norm(mem, g_mem[l])
        y_mem = memory_attention(m_q.reshape(B, S, MEM_HEADS, MEM_HEAD_DIM), mem_h, w_mem_kv[l],
                                 g_q_mem[l], g_k_mem[l])
        y_mem = y_mem.reshape(B, S, MEM_WIDTH) @ w_o_mem[l]

        gates = jax.nn.sigmoid(h @ w_gate[l] + b_gate[l]).reshape(B, S, N_BRANCHES, D)
        merged = gates[:, :, 0] * y_sb + gates[:, :, 1] * y_dil + gates[:, :, 2] * y_mem
        x = x + merged @ w_out[l]

        h2 = rms_norm(x, g_ffn[l])
        x = x + peer_ffn(h2, w_peer_q[l], peer_subkeys[l], peer_u[l], peer_v[l])
    return x


def setup_inputs(seed=0):
    out = dict(first_inputs(seed))
    for name, value in second_inputs(seed + 1).items():
        if name != "x":
            out[name + "_2"] = value
    return out


def reference(
    x, norm_mix_g, w_in, mla_q_norm_g, w_uq, mla_kv_norm_g, w_uk, w_uv, w_o_a, w_o_b, w_out,
    norm_ffn_g, w_router_group, b_router_group, w_router_expert, b_router_expert, w_gate, w_up,
    w_down, final_norm_g, mem_2, g_mix_2, g_mem_2, w_in_2, w_mem_kv_2, g_q_dil_2, g_k_dil_2,
    g_q_mem_2, g_k_mem_2, w_o_sb_2, w_o_dil_2, w_o_mem_2, w_gate_2, b_gate_2, w_out_2, g_ffn_2,
    w_peer_q_2, peer_subkeys_2, peer_u_2, peer_v_2,
):
    x = first_block(
        x, norm_mix_g, w_in, mla_q_norm_g, w_uq, mla_kv_norm_g, w_uk, w_uv, w_o_a, w_o_b, w_out,
        norm_ffn_g, w_router_group, b_router_group, w_router_expert, b_router_expert, w_gate,
        w_up, w_down, final_norm_g,
    )
    return second_block(
        x, mem_2, g_mix_2, g_mem_2, w_in_2, w_mem_kv_2, g_q_dil_2, g_k_dil_2, g_q_mem_2,
        g_k_mem_2, w_o_sb_2, w_o_dil_2, w_o_mem_2, w_gate_2, b_gate_2, w_out_2, g_ffn_2,
        w_peer_q_2, peer_subkeys_2, peer_u_2, peer_v_2,
    )


_drawn_inputs = setup_inputs


def setup_inputs(seed=0):
    import zlib

    import numpy as np

    out = dict(_drawn_inputs(seed))
    spreads = {}
    factors = {'mla_q_norm_g': 4.127,
     'mla_kv_norm_g': 3.608,
     'b_router_group': 4.617,
     'b_router_expert': 5.729,
     'g_mix_2': 5.387,
     'g_mem_2': 8.0,
     'g_q_dil_2': 8.0,
     'g_k_dil_2': 8.0,
     'g_q_mem_2': 8.0,
     'g_k_mem_2': 8.0,
     'b_gate_2': 8.0,
     'g_ffn_2': 41.086}
    for name, (base, spread) in spreads.items():
        noise = np.random.default_rng([zlib.crc32(name.encode()), seed]).standard_normal(out[name].shape)
        drawn = base * np.exp(spread * noise) if base else spread * noise
        out[name] = __import__('jax').numpy.asarray(drawn.astype(out[name].dtype))
    for name, factor in factors.items():
        out[name] = (out[name] * factor).astype(out[name].dtype)
    return out
```

```python
from contextlib import ExitStack

import numpy as np

import concourse.bass as bass
from concourse import mybir

F32 = mybir.dt.float32
BF16 = mybir.dt.bfloat16
U32 = mybir.dt.uint32
ALU = mybir.AluOpType
ACT = mybir.ActivationFunctionType
AX = mybir.AxisListType
EPS = 1e-6
NEG = -1e30


class Calls:

    @staticmethod
    def activation(*a, **k):
        return lambda e: e.activation(*a, **k)

    @staticmethod
    def tensor_copy(*a, **k):
        return lambda e: e.tensor_copy(*a, **k)

    @staticmethod
    def tensor_tensor(*a, **k):
        return lambda e: e.tensor_tensor(*a, **k)

    @staticmethod
    def tensor_scalar(*a, **k):
        return lambda e: e.tensor_scalar(*a, **k)

    @staticmethod
    def scalar_tensor_tensor(*a, **k):
        return lambda e: e.scalar_tensor_tensor(*a, **k)

    @staticmethod
    def tensor_tensor_reduce(*a, **k):
        return lambda e: e.tensor_tensor_reduce(*a, **k)

    @staticmethod
    def tensor_tensor_scan(*a, **k):
        return lambda e: e.tensor_tensor_scan(*a, **k)

    @staticmethod
    def tensor_reduce(*a, **k):
        return lambda e: e.tensor_reduce(*a, **k)

    @staticmethod
    def reciprocal(*a, **k):
        return lambda e: e.reciprocal(*a, **k)

    @staticmethod
    def max(*a, **k):
        return lambda e: e.max(*a, **k)

    @staticmethod
    def max_index(*a, **k):
        return lambda e: e.max_index(*a, **k)

    @staticmethod
    def match_replace(*a, **k):
        return lambda e: e.match_replace(*a, **k)

    @staticmethod
    def matmul(*a, **k):
        return lambda e: e.matmul(*a, **k)

    @staticmethod
    def transpose(*a, **k):
        return lambda e: e.transpose(*a, **k)

    @staticmethod
    def memset(*a, **k):
        return lambda e: e.memset(*a, **k)

    @staticmethod
    def iota(*a, **k):
        return lambda e: e.iota(*a, **k)

    @staticmethod
    def affine_select(*a, **k):
        return lambda e: e.affine_select(*a, **k)

    @staticmethod
    def indirect_dma_start(*a, **k):
        return lambda e: e.indirect_dma_start(*a, **k)

    @staticmethod
    def partition_all_reduce(*a, **k):
        return lambda e: e.partition_all_reduce(*a, **k)

    @staticmethod
    def copy_predicated(*a, **k):
        return lambda e: e.copy_predicated(*a, **k)


class Queue:

    def __init__(self, sem, chained=False):
        self.sem, self.n, self.ops, self.met, self.chained = sem, 0, [], {}, chained

    def need(self, *marks):
        for m in marks:
            if m is None:
                continue
            if isinstance(m, list):
                self.need(*m)
            elif self.met.get(m[0].num, 0) < m[1]:
                self.met[m[0].num] = m[1]
                self.ops.append(lambda e, m=m: e.wait_ge(m[0], m[1]))

    def op(self, fn, *marks, mark=True, alone=False):
        self.need(*marks)
        if self.chained and not alone:
            self.need(self.last())
        call = fn(Calls)
        if not mark:
            self.ops.append(call)
            return None
        self.n += 1
        self.ops.append(lambda e: call(e).then_inc(self.sem, 1))
        return (self.sem, self.n)

    def last(self):
        return (self.sem, self.n) if self.n else None

    def dma(self, out, in_, sem, *marks):
        self.need(*marks)
        sem[1] += 16
        self.ops.append(lambda e: e.dma_start(out, in_).then_inc(sem[0], 16))
        return (sem[0], sem[1])

    def run(self, e):
        for f in self.ops:
            f(e)


class Ring:

    def __init__(self, bufs):
        self.bufs, self.idle = bufs, [(k, []) for k in range(len(bufs))]

    def take(self):
        k, marks = self.idle.pop(0)
        return k, self.bufs[k], marks

    def free(self, k, *marks):
        self.idle.append((k, list(marks)))


def stages(n, *parts):
    for step in range(n + max(lag for lag, _ in parts)):
        for lag, fn in parts:
            if 0 <= step - lag < n:
                fn(step - lag)


CONST = {}
_at = 0
for _name, _w in (("ident", 128), ("iota", 128), ("ba", 512), ("bs", 512), ("cosa", 128), ("sina", 128),
                  ("cosb", 64), ("sinb", 64), ("sel", 256)):
    CONST[_name] = (_at, _w)
    _at += _w
NCONST = _at
GAIN = {}
_at = 0
for _name, _w in (("mix", 8), ("ffn", 8), ("mix2", 8), ("mem2", 8), ("ffn2", 8), ("bg2", 24), ("cq", 3),
                  ("ckv", 2), ("final", 1024), ("qd", 64), ("kd", 64), ("qm", 128), ("km", 128), ("br", 40)):
    GAIN[_name] = (_at, _w)
    _at += _w
NGAIN = _at


def constants():
    f = np.float32
    c = np.zeros((128, NCONST), f)

    def put(name, a):
        o, w = CONST[name]
        c[:a.shape[0], o:o + w] = a.reshape(a.shape[0], w)

    p = np.arange(128)
    put("ident", np.eye(128, dtype=f))
    put("iota", np.broadcast_to(np.arange(128, dtype=f), (128, 128)))
    a = np.zeros((128, 512), f)
    a[:, 384:] = np.where((p[None, :] // 64) <= (p[:, None] // 64), 0, NEG)
    put("ba", a)
    a = np.zeros((128, 512), f)
    a[:, 384:] = np.where(p[None, :] < p[:, None], 0, NEG)
    put("bs", a)
    for name, rot in (("a", 32), ("b", 16)):
        half = rot // 2
        inv = f(500000.0) ** (-np.arange(half, dtype=f) * f(2.0) / f(rot))
        ang = np.arange(512, dtype=f)[:, None] * inv.astype(f)[None, :]
        co, si = np.cos(ang).astype(f), np.sin(ang).astype(f)
        co = np.stack([co, co], 1).reshape(4, 128, rot).transpose(1, 0, 2)
        si = np.stack([-si, si], 1).reshape(4, 128, rot).transpose(1, 0, 2)
        put("cos" + name, np.ascontiguousarray(co))
        put("sin" + name, np.ascontiguousarray(si))
    slopes = np.exp2(f(-8.0) * np.arange(1, 13, dtype=f) / f(12)).astype(f)
    bd = np.zeros((128, 2048), f)
    gap = p[:, None] - (np.arange(256)[None, :] - 128)
    for h in range(4):
        b = -(slopes[h] * gap.astype(f))
        bd[:, 256 * h:256 * h + 256] = np.where((gap >= 0) & (gap <= 128), b, f(NEG))
    gap = p[:, None] - p[None, :]
    for h in range(4):
        bd[:, 1024 + 128 * h:1152 + 128 * h] = np.where(gap >= 0, -(slopes[4 + h] * (gap * 4).astype(f)), f(NEG))
        ok = (gap >= 0) & (p[:, None] // 32 == p[None, :] // 32)
        bd[:, 1536 + 128 * h:1664 + 128 * h] = np.where(ok, -(slopes[8 + h] * (gap * 16).astype(f)), f(NEG))
    s = np.zeros((4, 256), f)
    for h in range(4):
        s[h, 64 * h:64 * h + 64] = 1
    put("sel", s)
    return c, bd


def lay(i):
    def kxn(w):
        k, n = w.shape
        return w.reshape(k // 128, 128, n).transpose(1, 0, 2)

    def flat(*parts):
        return [np.ascontiguousarray(p).reshape(-1) for p in parts]

    w = i["w_in"][0]
    cq, ckv, kr, qb, kb, vb, qi, ki, wi, ga, gb = np.split(
        w, np.cumsum([384, 256, 32, 512, 512, 512, 512, 64, 8, 1024])[:10].tolist(), axis=1)
    tiles = [kxn(np.concatenate([cq, kr, ki, wi], 1)), kxn(qi), kxn(qb), kxn(kb), kxn(vb), kxn(ckv),
             kxn(i["w_uq"][0][:, :384]), kxn(i["w_uq"][0][:, 384:]), kxn(i["w_uk"][0]), kxn(i["w_uv"][0])]
    for m in range(8):
        s = slice(128 * m, 128 * m + 128)
        tiles.append(np.concatenate([kxn(np.concatenate([ga[:, s], gb[:, s]], 1)).reshape(128, -1),
                                     kxn(i["w_o_a"][0][:, s]).reshape(128, -1),
                                     kxn(i["w_o_b"][0][:, s]).reshape(128, -1)], 1))
    tiles += [kxn(i["w_out"][0][:, :512]), kxn(i["w_out"][0][:, 512:])]
    tiles.append(kxn(np.concatenate([i["w_router_group"][0], i["w_router_expert"][0]], 1)))
    for e in range(32):
        tiles.append(kxn(np.concatenate([i["w_gate"][0, e], i["w_up"][0, e]], 1)))
        tiles.append(kxn(i["w_down"][0, e]))
    w = i["w_in_2"][0]
    for k in range(3):
        tiles.append(kxn(w[:, 512 * k:512 * k + 512]))
    for k in range(4):
        tiles.append(kxn(w[:, 1536 + 384 * k:1920 + 384 * k]))
    for k in range(3):
        tiles.append(kxn(w[:, 3072 + 256 * k:3328 + 256 * k]))
    tiles.append(kxn(w[:, 3840:4352]))
    tiles += [kxn(i["w_mem_kv_2"][0][:, :512]), kxn(i["w_mem_kv_2"][0][:, 512:])]
    wg = i["w_gate_2"][0]
    for m in range(8):
        s = slice(128 * m, 128 * m + 128)
        tiles.append(kxn(np.concatenate([wg[:, 1024 * b + 128 * m:1024 * b + 128 * m + 128] for b in range(3)], 1)))
        tiles.append(np.concatenate([kxn(i["w_o_sb_2"][0][:, s]).reshape(128, -1),
                                     kxn(i["w_o_dil_2"][0][:, s]).reshape(128, -1),
                                     kxn(i["w_o_mem_2"][0][:, s]).reshape(128, -1)], 1))
    tiles += [kxn(i["w_out_2"][0][:, :512]), kxn(i["w_out_2"][0][:, 512:])]
    for h in range(8):
        tiles.append(kxn(i["w_peer_q_2"][0][:, 256 * h:256 * h + 256]))
        tiles.append(i["peer_subkeys_2"][0, h].transpose(2, 0, 1))
    sizes = [t.size // 128 for t in tiles]
    weights = np.concatenate(flat(*tiles))
    u = i["peer_u_2"][0].reshape(128, 32, 4, 8, 128).transpose(1, 4, 2, 3, 0)
    v = i["peer_v_2"][0].reshape(128, 32, 4, 1024).transpose(1, 0, 2, 3)
    g = np.zeros((128, NGAIN), np.float32)
    consts, bd = constants()

    def put(name, a, rows):
        o, w = GAIN[name]
        g[:, o:o + w] = np.broadcast_to(a[None, :], (128, w)) if rows else a.reshape(w, 128).T

    for name, key in (("mix", "norm_mix_g"), ("ffn", "norm_ffn_g"), ("mix2", "g_mix_2"), ("mem2", "g_mem_2"),
                      ("ffn2", "g_ffn_2"), ("bg2", "b_gate_2"), ("cq", "mla_q_norm_g"), ("ckv", "mla_kv_norm_g")):
        put(name, i[key][0], False)
    put("final", i["final_norm_g"], True)
    for name, key in (("qd", "g_q_dil_2"), ("kd", "g_k_dil_2"), ("qm", "g_q_mem_2"), ("km", "g_k_mem_2")):
        put(name, i[key][0], True)
    put("br", np.concatenate([i["b_router_group"][0], i["b_router_expert"][0]]), True)
    return {"x": i["x"][0], "mem": i["mem_2"][0], "weights": weights, "u": np.ascontiguousarray(u),
            "v": np.ascontiguousarray(v), "gains": g, "consts": consts, "bd": bd}, sizes


def program(nc, d, out, sizes, stop=None, dump=None):
    ctx = ExitStack()
    with ctx:
        def sb(name, shape, dt=F32, c=ctx):
            t = c.enter_context(nc.sbuf_tensor(name, shape, dt))
            return t[(slice(None),) * len(shape)]

        def sem(name):
            return ctx.enter_context(nc.semaphore(name))

        pe, sp = Queue(sem("s_pe")), Queue(sem("s_sp"))
        dve, act, pool = (Queue(sem(n), chained=True) for n in ("s_dve", "s_act", "s_pool"))
        engines = (pe, dve, act, pool)
        banks = Ring([ctx.enter_context(nc.psum_tensor(f"bank{k}", [128, 512], F32))[:, :] for k in range(8)])
        dsem = {}

        def ds(name):
            if name not in dsem:
                dsem[name] = [sem("d_" + name), 0]
            return dsem[name]

        X = sb("X", [128, 4, 1024])
        HT = sb("HT", [128, 8, 512])
        C = sb("C", [128, NCONST])
        G = sb("G", [128, NGAIN])
        NS = 4
        wring = Ring([sb(f"W{k}", [128, 4096]) for k in range(NS)])
        cc = lambda n: C[:, CONST[n][0]:CONST[n][0] + CONST[n][1]]
        gg = lambda n: G[:, GAIN[n][0]:GAIN[n][0] + GAIN[n][1]]
        ident = cc("ident")

        offs = np.concatenate([[0], np.cumsum(np.array(sizes) * 128)])
        state = {"next": 0}
        queued = []

        def fetch():
            k, buf, marks = wring.take()
            n = state["next"]
            state["next"] += 1
            src = d["weights"][int(offs[n]):int(offs[n + 1])].rearrange("(p f) -> p f", p=128)
            m = sp.dma(buf[:, 0:sizes[n]], src, ds(f"w{k}"), marks)
            queued.append((k, buf[:, 0:sizes[n]], m))

        def weight():
            if not queued:
                fetch()
            return queued.pop(0)

        def done(k, *marks):
            wring.free(k, *marks)

        def ahead():
            while state["next"] < len(sizes) and wring.idle:
                fetch()

        m_x = sp.dma(X[:, :, :], d["x"].rearrange("(b p) n -> p b n", p=128), ds("x"))
        m_c = sp.dma(C[:, :], d["consts"], ds("c"))
        m_c = [m_c, sp.dma(G[:, :], d["gains"], ds("g"))]
        for q in (dve, act, pe, pool):
            q.need(m_c)
        ahead()

        def barrier():
            marks = [q.last() for q in engines]
            for q in engines + (sp,):
                q.need(*[m for m in marks])

        dumps = {}

        def show(name, ap, *marks):
            if dump is None or name not in dump:
                return
            barrier()
            m = sp.dma(dump[name], ap, ds("dump"), *marks)
            for q in engines:
                q.need(m)

        flip = [0]

        def copy(out_, in_, *marks, scale=None):
            flip[0] ^= 1
            if flip[0]:
                s = 1.0 if scale is None else scale
                return act.op(lambda e: e.activation(out_, in_, ACT.Copy if scale is None or isinstance(scale, float) else ACT.Copy, scale=s), *marks)
            if scale is None:
                return dve.op(lambda e: e.tensor_copy(out_, in_), *marks)
            return dve.op(lambda e: e.tensor_scalar(out_, in_, scale, None, ALU.mult), *marks)

        def mms(bank, parts, *marks):
            pe.need(*marks)
            n = len(parts)
            for j, (o, a, b) in enumerate(parts):
                m = pe.op(lambda e, o=o, a=a, b=b, j=j: e.matmul(o, a, b, start=j == 0, stop=j == n - 1),
                          mark=j == n - 1)
            return m

        def flips(parts, *marks):
            pe.need(*marks)
            for j, (o, a) in enumerate(parts):
                p = a.shape[0]
                m = pe.op(lambda e, o=o, a=a, p=p: e.transpose(o, a, ident[0:p, 0:p]), mark=j == len(parts) - 1)
            return m

        RT = sb("RT", [128, 2, 8])

        def rstd(o, ss, n, m):
            w = o.shape[1]
            v, t = RT[:, 0, 0:w], RT[:, 1, 0:w]
            m = dve.op(lambda e: e.tensor_scalar(v, ss, 1.0 / n, EPS, ALU.mult, ALU.add), m)
            m = act.op(lambda e: e.activation(o, v, ACT.Sqrt), m)
            m = dve.op(lambda e: e.reciprocal(o, o), m)
            m = dve.op(lambda e: e.tensor_tensor(t, o, o, ALU.mult), m)
            m = dve.op(lambda e: e.tensor_tensor(t, t, v, ALU.mult), m)
            m = dve.op(lambda e: e.tensor_scalar(t, t, -0.5, 1.5, ALU.mult, ALU.add), m)
            return dve.op(lambda e: e.tensor_tensor(o, o, t, ALU.mult), m)

        def norm_rows(src, dst, tmp, st, nb, width, marks):
            for b in range(nb):
                m = act.op(lambda e, b=b: e.activation(tmp, src[:, b, :], ACT.Square, accum_out=st[:, b:b + 1]), marks)
            m = rstd(st[:, 0:nb], st[:, 0:nb], width, m)
            return [dve.op(lambda e, b=b: e.tensor_scalar(dst[:, b, :], src[:, b, :], st[:, b:b + 1], None, ALU.mult), m) for b in range(nb)]

        def turn(src, dst, nb, kk, gain, marks):
            res = []
            for k in range(kk):
                kb, bank, fr = banks.take()
                m = flips([(bank[:, 128 * b:128 * b + 128], src[:, b, 128 * k:128 * k + 128]) for b in range(nb)], fr, marks)
                m = copy(dst[:, k, 0:128 * nb], bank[:, 0:128 * nb], m, scale=gain[:, k:k + 1])
                banks.free(kb, m)
                res.append(m)
            return res

        def normed(src, dst, nb, gain, marks, c):
            xn = sb("xn" + gain, [128, nb, 1024], c=c)
            sq = sb("sq" + gain, [128, 1024], c=c)
            st = sb("st" + gain, [128, nb], c=c)
            r = norm_rows(src, xn, sq, st, nb, 1024, marks)
            return turn(xn, dst, nb, 8, gg(gain), r)

        def project(w, kk, lhs, tb, n, *marks):
            kb, bank, fr = banks.take()
            m = mms(bank, [(bank[:, 0:n], lhs(k, tb), w[:, k * n:k * n + n]) for k in range(kk)], fr, *marks)
            return kb, bank, m

        ht = lambda k, tb: HT[:, k, 128 * tb:128 * tb + 128]

        def rope(x, tb, heads, half, name, t1, t2, m):
            w = 2 * half
            co = cc("cos" + name)[:, w * tb:w * tb + w]
            si = cc("sin" + name)[:, w * tb:w * tb + w]
            v = lambda a: a.rearrange("p (j f) -> p j f", j=2)
            marks = []
            x4 = x.rearrange("p h (j f) -> p h j f", j=2)
            a = t1.rearrange("p (h j f) -> p h j f", h=heads, j=2)
            b = t2.rearrange("p (h j f) -> p h j f", h=heads, j=2)
            co4 = v(co).unsqueeze(1).to_broadcast([128, heads, 2, half])
            si4 = v(si).unsqueeze(1).to_broadcast([128, heads, 2, half])
            m1 = dve.op(lambda e: e.tensor_tensor(a, x4, co4, ALU.mult), m)
            m2 = dve.op(lambda e: e.tensor_tensor(b, x4[:, :, ::-1, :], si4, ALU.mult), m)
            return dve.op(lambda e: e.tensor_tensor(x4, a, b, ALU.add), m1, m2)

        def attend(c, tag, blocks, heads, q, k, v, keys, bias, scale, width, finish, extra=None):
            P = Ring([sb(f"P{tag}{n}", [128, 512], c=c) for n in range(4)])
            PT = Ring([sb(f"PT{tag}{n}", [128, 512], c=c) for n in range(3)])
            MX = sb("MX" + tag, [128, blocks * heads], c=c)
            NM = sb("NM" + tag, [128, blocks * heads], c=c)
            RS = sb("RS" + tag, [128, blocks * heads], c=c)
            S, E, T, O = {}, {}, {}, {}

            def score(n):
                i, h = divmod(n, heads)
                kb, bank, fr = banks.take()
                S[n] = (kb, bank, mms(bank, [(bank[:, 0:keys(i)], q(i, h), k(i, h))], fr))

            def soft(n):
                i, h = divmod(n, heads)
                kb, bank, m = S.pop(n)
                pk, p, fr = P.take()
                kn = keys(i)
                b = bias(i, h)
                if b is not None:
                    m = dve.op(lambda e: e.tensor_tensor_reduce(p[:, 0:kn], bank[:, 0:kn], b[0], 1.0, -3e38, ALU.add, ALU.max, MX[:, n:n + 1]), m, fr, b[1])
                    src = p[:, 0:kn]
                    banks.free(kb, m)
                else:
                    m = dve.op(lambda e: e.tensor_reduce(MX[:, n:n + 1], bank[:, 0:kn], AX.X, ALU.max), m)
                    src = bank[:, 0:kn]
                m = dve.op(lambda e: e.tensor_scalar(NM[:, n:n + 1], MX[:, n:n + 1], -scale, None, ALU.mult), m)
                m = act.op(lambda e: e.activation(p[:, 0:kn], src, ACT.Exp, bias=NM[:, n:n + 1], scale=scale, accum_out=RS[:, n:n + 1]), m, fr)
                if b is None:
                    banks.free(kb, m)
                E[n] = (pk, p, m)

            def turned(n):
                i, h = divmod(n, heads)
                pk, p, m = E.pop(n)
                kb, bank, fr = banks.take()
                nb = keys(i) // 128
                m = flips([(bank[:, 128 * j:128 * j + 128], p[:, 128 * j:128 * j + 128]) for j in range(nb)], m, fr)
                P.free(pk, m)
                tk, t, fr = PT.take()
                m = copy(t[:, 0:keys(i)], bank[:, 0:keys(i)], m, fr)
                banks.free(kb, m)
                T[n] = (tk, t, m)

            def value(n):
                i, h = divmod(n, heads)
                tk, t, m = T.pop(n)
                if h == 0:
                    O["b"] = banks.take()
                kb, bank, fr = O["b"]
                o = bank[:, width * h:width * h + width]
                nb = keys(i) // 128
                m = mms(bank, [(o, t[:, 128 * j:128 * j + 128], v(i, h, j)) for j in range(nb)], m, fr if h == 0 else None)
                PT.free(tk, m)
                if h == heads - 1:
                    s = slice(i * heads, i * heads + heads)
                    finish(i, kb, bank, RS[:, s], MX[:, s], m)

            return [(0, score), (1, soft), (3, turned), (4, value)]

        def rows_out(c, tag, heads, width, oT, dst=None):
            RI = sb("RI" + tag, [128, heads], c=c)
            ON = Ring([sb(f"ON{tag}{n}", [128, heads * width], c=c) for n in range(2)])
            kk = heads * width // 128

            def finish(i, kb, bank, rs, mx, m):
                m1 = dve.op(lambda e: e.reciprocal(RI[:, :], rs), act.last())
                ok, on, fr = ON.take()
                o3 = on[:, :].rearrange("p (h w) -> p h w", h=heads)
                b3 = bank[:, 0:heads * width].rearrange("p (h w) -> p h w", h=heads)
                m = dve.op(lambda e: e.tensor_tensor(o3, b3, RI[:, :].unsqueeze(2).to_broadcast([128, heads, width]), ALU.mult), m, m1, fr)
                banks.free(kb, m)
                k2, bk, fr = banks.take()
                m = flips([(bk[:, 128 * j:128 * j + 128], on[:, 128 * j:128 * j + 128]) for j in range(kk)], m, fr)
                ON.free(ok, m)
                src = bk[:, 0:128 * kk].rearrange("p (k t) -> p k t", k=kk)
                if dst is None:
                    banks.free(k2, copy(oT[:, :, 128 * i:128 * i + 128], src, m))
                else:
                    ms = []
                    for j in range(kk):
                        o_, i_ = dst(i, j, bk[:, 128 * j:128 * j + 128])
                        ms.append(dve.op(lambda e, o_=o_, i_=i_: e.tensor_copy(o_, i_), m))
                    banks.free(k2, *ms)
            return finish

        def proj_out(c, tag, yT):
            for half in range(2):
                wk, w, wm = weight()
                ms = []
                for tb in range(4):
                    kb, bank, m = project(w, 8, lambda k, tb: yT[:, k, 128 * tb:128 * tb + 128], tb, 512, wm, act.last(), dve.last())
                    ms.append(m)
                    o = X[:, tb, 512 * half:512 * half + 512]
                    m2 = dve.op(lambda e, o=o, bank=bank: e.tensor_tensor(o, o, bank[:, :], ALU.add), m)
                    banks.free(kb, m2)
                done(wk, ms[-1])
                ahead()

        with ExitStack() as c0:
            with ExitStack() as c1:
                hm = normed(X, HT, 4, "mix", m_x, c1)
            show("hT", HT[:, :, :])
            pe.need(*hm)
            barrier()
            oTa = sb("oTa", [128, 4, 512], c=c0)
            oTb = sb("oTb", [128, 4, 512], c=c0)
            cqT = sb("cqT", [128, 3, 512], c=c0)
            krN = sb("krN", [128, 4, 32], c=c0)
            with ExitStack() as c1:
                qbT = sb("qbT", [128, 4, 512], c=c1)
                kbT = sb("kbT", [128, 4, 512], c=c1)
                vb = sb("vb", [128, 4, 512], c=c1)
                BI = sb("BI", [128, 4, 512], c=c1)
                c2 = c1.enter_context(ExitStack())
                wiN = sb("wiN", [128, 4, 8], c=c2)
                kiT = sb("kiT", [128, 512], c=c2)
                qiT = sb("qiT", [128, 4, 512], c=c2)
                ST = Ring([sb(f"ST{n}", [128, 512], c=c2) for n in range(3)])
                t1 = sb("t1", [128, 128], c=c2)
                t2 = sb("t2", [128, 128], c=c2)
                sq = sb("sqc", [128, 384], c=c2)
                st = sb("stc", [128, 4], c=c2)
                kiN = sb("kiN", [128, 4, 128], c=c2)
                wk, w, wm = weight()
                for tb in range(4):
                    kb, bank, m = project(w, 8, ht, tb, 488, wm)
                    wlast = m
                    sk, s, fr = ST.take()
                    m = act.op(lambda e, s=s, bank=bank: e.activation(s[:, 0:488], bank[:, 0:488], ACT.Copy), m, fr)
                    banks.free(kb, m)
                    mk = dve.op(lambda e, s=s, tb=tb: e.tensor_copy(krN[:, tb, :], s[:, 384:416]), m)
                    rope(krN[:, tb, :].unsqueeze(1), tb, 1, 16, "a", t1[:, 0:32], t2[:, 0:32], mk)
                    mk = dve.op(lambda e, s=s, tb=tb: e.tensor_copy(kiN[:, tb, 0:64], s[:, 416:480]), m)
                    mk = rope(kiN[:, tb, 0:16].unsqueeze(1), tb, 1, 8, "b", t1[:, 0:16], t2[:, 0:16], mk)
                    mk = dve.op(lambda e, tb=tb: e.tensor_copy(kiN[:, tb, 64:128], kiN[:, tb, 0:64]), mk)
                    dve.op(lambda e, s=s, tb=tb: e.tensor_scalar(wiN[:, tb, :], s[:, 480:488], float(8 ** -0.5), None, ALU.mult), m)
                    mq = act.op(lambda e, s=s, tb=tb: e.activation(sq[:, :], s[:, 0:384], ACT.Square, accum_out=st[:, tb:tb + 1]), m)
                    mq = rstd(st[:, tb:tb + 1], st[:, tb:tb + 1], 384, mq)
                    mq = dve.op(lambda e, s=s, tb=tb: e.tensor_scalar(s[:, 0:384], s[:, 0:384], st[:, tb:tb + 1], None, ALU.mult), mq)
                    kb, bank, fr = banks.take()
                    m = flips([(bank[:, 128 * j:128 * j + 128], s[:, 128 * j:128 * j + 128]) for j in range(3)]
                              + [(bank[:, 384:512], kiN[:, tb, :])], mq, mk, fr)
                    ST.free(sk, m)
                    ms = [copy(cqT[:, j, 128 * tb:128 * tb + 128], bank[:, 128 * j:128 * j + 128], m, scale=gg("cq")[:, j:j + 1]) if False else
                          dve.op(lambda e, j=j, tb=tb, bank=bank: e.tensor_scalar(cqT[:, j, 128 * tb:128 * tb + 128], bank[:, 128 * j:128 * j + 128], gg("cq")[:, j:j + 1], None, ALU.mult), m)
                          for j in range(3)]
                    ms.append(dve.op(lambda e, tb=tb, bank=bank: e.tensor_copy(kiT[:, 128 * tb:128 * tb + 128], bank[:, 384:512]), m))
                    banks.free(kb, *ms)
                done(wk, wlast)
                ahead()
                for dst, turned_ in ((qiT, True), (qbT, True), (kbT, True), (vb, False)):
                    wk, w, wm = weight()
                    for tb in range(4):
                        kb, bank, m = project(w, 8, ht, tb, 512, wm)
                        wlast = m
                        if not turned_:
                            m = copy(dst[:, tb, :], bank[:, :], m)
                            banks.free(kb, m)
                            continue
                        sk, s, fr = ST.take()
                        m = act.op(lambda e, s=s, bank=bank: e.activation(s[:, :], bank[:, :], ACT.Copy), m, fr)
                        banks.free(kb, m)
                        m = rope(s[:, :].rearrange("p (h f) -> p h f", h=8)[:, :, 0:16], tb, 8, 8, "b", t1[:, :], t2[:, :], m)
                        kb, bank, fr = banks.take()
                        m = flips([(bank[:, 128 * j:128 * j + 128], s[:, 128 * j:128 * j + 128]) for j in range(4)], m, fr)
                        ST.free(sk, m)
                        m = copy(dst[:, :, 128 * tb:128 * tb + 128], bank[:, :].rearrange("p (k t) -> p k t", k=4), m)
                        banks.free(kb, m)
                    done(wk, wlast)
                    ahead()
                barrier()
                RL = Ring([sb(f"RL{n}", [128, 512], c=c2) for n in range(2)])
                WA = sb("WA", [128, 512], c=c2)
                WB = sb("WB", [128, 512], c=c2)
                M8 = sb("M8", [128, 8], c=c2)
                L = {}

                def logits(n):
                    i, h = divmod(n, 8)
                    i += 1
                    kn = 128 * i + 128
                    kb, bank, fr = banks.take()
                    o = 64 * (h % 2)
                    m = mms(bank, [(bank[:, 0:kn], qiT[o:o + 64, h // 2, 128 * i:128 * i + 128], kiT[o:o + 64, 0:kn])], fr)
                    rk, r, fr = RL.take()
                    m = act.op(lambda e: e.activation(r[:, 0:kn], bank[:, 0:kn], ACT.Relu, scale=0.125), m, fr)
                    banks.free(kb, m)
                    L[n] = (rk, r, m)

                def summed(n):
                    i, h = divmod(n, 8)
                    i += 1
                    kn = 128 * i + 128
                    rk, r, m = L.pop(n)
                    if h == 0:
                        m = dve.op(lambda e: e.tensor_scalar(WA[:, 0:kn], r[:, 0:kn], wiN[:, i, 0:1], None, ALU.mult), m)
                    else:
                        m = dve.op(lambda e: e.scalar_tensor_tensor(WA[:, 0:kn], r[:, 0:kn], wiN[:, i, h:h + 1], WA[:, 0:kn], ALU.mult, ALU.add), m, dve.last())
                    RL.free(rk, m)
                    if h == 7:
                        m = dve.op(lambda e: e.tensor_tensor(WA[:, 0:kn], WA[:, 0:kn], cc("ba")[:, 512 - kn:512], ALU.add), m)
                        a, b = WA, WB
                        for _ in range(16):
                            m = dve.op(lambda e, a=a: e.max(M8[:, :], a[:, 0:kn]), m)
                            m = dve.op(lambda e, a=a, b=b: e.match_replace(b[:, 0:kn], M8[:, :], a[:, 0:kn], -2e30), m)
                            a, b = b, a
                        dve.op(lambda e, a=a: e.tensor_scalar(BI[:, i, 0:kn], a[:, 0:kn], -1.5e30, NEG, ALU.is_gt, ALU.mult), m)
                        dve.need(dve.last())

                stages(24, (0, logits), (1, summed))
                show("bi", BI[:, 1:4, :])
                barrier()
                c2.close()
                half = lambda h: slice(64 * (h % 2), 64 * (h % 2) + 64)
                fin = rows_out(c1, "b", 8, 64, oTb)
                stages(32, *attend(
                    c1, "b", 4, 8, lambda i, h: qbT[half(h), h // 2, 128 * i:128 * i + 128],
                    lambda i, h: kbT[half(h), h // 2, 0:128 * i + 128],
                    lambda i, h, j: vb[:, j, 64 * h:64 * h + 64], lambda i: 128 * i + 128,
                    lambda i, h: ((BI[:, i, 0:128 * i + 128] if i else cc("ba")[:, 384:512]), None), 0.125, 64, fin))
                show("oTb", oTb[:, :, :])
                barrier()
            with ExitStack() as c1:
                ckvT = sb("ckvT", [128, 2, 512], c=c1)
                qaT = sb("qaT", [96, 8, 512], c=c1)
                kaT = sb("kaT", [96, 8, 512], c=c1)
                va = sb("va", [128, 4, 512], c=c1)
                ST = Ring([sb(f"SU{n}", [128, 768], c=c1) for n in range(2)])
                t1 = sb("t1b", [128, 256], c=c1)
                t2 = sb("t2b", [128, 256], c=c1)
                sq = sb("sqd", [128, 256], c=c1)
                st = sb("std", [128, 4], c=c1)
                wk, w, wm = weight()
                for tb in range(4):
                    kb, bank, m = project(w, 8, ht, tb, 256, wm)
                    wlast = m
                    sk, s, fr = ST.take()
                    m = act.op(lambda e, s=s, bank=bank: e.activation(s[:, 0:256], bank[:, 0:256], ACT.Copy), m, fr)
                    banks.free(kb, m)
                    mq = act.op(lambda e, s=s, tb=tb: e.activation(sq[:, :], s[:, 0:256], ACT.Square, accum_out=st[:, tb:tb + 1]), m)
                    mq = rstd(st[:, tb:tb + 1], st[:, tb:tb + 1], 256, mq)
                    mq = dve.op(lambda e, s=s, tb=tb: e.tensor_scalar(s[:, 0:256], s[:, 0:256], st[:, tb:tb + 1], None, ALU.mult), mq)
                    kb, bank, fr = banks.take()
                    m = flips([(bank[:, 128 * j:128 * j + 128], s[:, 128 * j:128 * j + 128]) for j in range(2)], mq, fr)
                    ST.free(sk, m)
                    banks.free(kb, *[dve.op(lambda e, j=j, tb=tb, bank=bank: e.tensor_scalar(ckvT[:, j, 128 * tb:128 * tb + 128], bank[:, 128 * j:128 * j + 128], gg("ckv")[:, j:j + 1], None, ALU.mult), m) for j in range(2)])
                done(wk, wlast)
                ahead()
                pe.need(dve.last())
                cql = lambda k, tb: cqT[:, k, 128 * tb:128 * tb + 128]
                ckl = lambda k, tb: ckvT[:, k, 128 * tb:128 * tb + 128]

                def heads_turned(s, m, dst, tb, h0, n):
                    for g in range(n // 4):
                        kb, bank, fr = banks.take()
                        m2 = flips([(bank[0:96, 128 * j:128 * j + 128], s[:, 96 * (4 * g + j):96 * (4 * g + j) + 96]) for j in range(4)], m, fr)
                        mc = copy(dst[:, h0 + 4 * g:h0 + 4 * g + 4, 128 * tb:128 * tb + 128], bank[0:96, :].rearrange("p (h t) -> p h t", h=4), m2)
                        banks.free(kb, mc)
                    return m2

                for g in range(2):
                    wk, w, wm = weight()
                    for tb in range(4):
                        kb, bank, m = project(w, 3, cql, tb, 384, wm)
                        wlast = m
                        sk, s, fr = ST.take()
                        m = act.op(lambda e, s=s, bank=bank: e.activation(s[:, 0:384], bank[:, 0:384], ACT.Copy), m, fr)
                        banks.free(kb, m)
                        m = rope(s[:, 0:384].rearrange("p (h f) -> p h f", h=4)[:, :, 64:96], tb, 4, 16, "a", t1[:, 0:128], t2[:, 0:128], m)
                        ST.free(sk, heads_turned(s, m, qaT, tb, 4 * g, 4))
                    done(wk, wlast)
                    ahead()
                wk, w, wm = weight()
                for tb in range(4):
                    kb, bank, m = project(w, 2, ckl, tb, 512, wm)
                    wlast = m
                    sk, s, fr = ST.take()
                    s3 = s[:, :].rearrange("p (h f) -> p h f", h=8)
                    m = act.op(lambda e, s3=s3, bank=bank: e.activation(s3[:, :, 0:64], bank[:, :].rearrange("p (h f) -> p h f", h=8), ACT.Copy), m, fr)
                    banks.free(kb, m)
                    m2 = dve.op(lambda e, s3=s3, tb=tb: e.tensor_copy(s3[:, :, 64:96], krN[:, tb, :].unsqueeze(1).to_broadcast([128, 8, 32])), fr)
                    ST.free(sk, heads_turned(s, [m, m2], kaT, tb, 0, 8))
                done(wk, wlast)
                ahead()
                wk, w, wm = weight()
                for tb in range(4):
                    kb, bank, m = project(w, 2, ckl, tb, 512, wm)
                    wlast = m
                    banks.free(kb, copy(va[:, tb, :], bank[:, :], m))
                done(wk, wlast)
                ahead()
                barrier()
                fin = rows_out(c1, "a", 8, 64, oTa)
                stages(32, *attend(
                    c1, "a", 4, 8, lambda i, h: qaT[:, h, 128 * i:128 * i + 128],
                    lambda i, h: kaT[:, h, 0:128 * i + 128],
                    lambda i, h, j: va[:, j, 64 * h:64 * h + 64], lambda i: 128 * i + 128,
                    lambda i, h: (cc("ba")[:, 384 - 128 * i:512], None), float(96 ** -0.5), 64, fin))
                show("oTa", oTa[:, :, :])
                barrier()
            yT = sb("yT", [128, 8, 512], c=c0)
            with ExitStack() as c1:
                SG = Ring([sb(f"SG{n}", [128, 512], c=c1) for n in range(4)])
                for m_ in range(8):
                    wk, w, wm = weight()
                    wg = w[:, 0:2048].rearrange("p (k n) -> p k n", k=8)
                    parts = []
                    for b, (oT, off) in enumerate(((oTa, 2048), (oTb, 2560))):
                        kb, bank, fr = banks.take()
                        m = mms(bank, [(bank[:, :], wg[:, k, 128 * b:128 * b + 128], HT[:, k, :]) for k in range(8)], fr, wm)
                        gk, g, fr = SG.take()
                        m = act.op(lambda e, g=g, bank=bank: e.activation(g[:, :], bank[:, :], ACT.Sigmoid), m, fr)
                        banks.free(kb, m)
                        kb, bank, fr = banks.take()
                        mw = mms(bank, [(bank[:, :], w[:, off + 128 * k:off + 128 * k + 128], oT[:, k, :]) for k in range(4)], fr)
                        m = dve.op(lambda e, g=g, bank=bank: e.tensor_tensor(g[:, :], g[:, :], bank[:, :], ALU.mult), mw, m)
                        banks.free(kb, m)
                        parts.append((gk, g, m))
                    done(wk, mw)
                    ahead()
                    (k1, g1, m1), (k2, g2, m2) = parts
                    m = dve.op(lambda e, m_=m_, g1=g1, g2=g2: e.tensor_tensor(yT[:, m_, :], g1[:, :], g2[:, :], ALU.add), m1, m2)
                    SG.free(k1, m)
                    SG.free(k2, m)
                proj_out(c1, "1", yT)
            show("x1", X[:, :, :])
            barrier()
        if stop == "attn1":
            return finish_program(nc, ctx, (pe, dve, act, pool, sp), dsem)

        with ExitStack() as c0:
            with ExitStack() as c1:
                hm = normed(X, HT, 4, "ffn", dve.last(), c1)
            pe.need(*hm)
            barrier()
            LG = sb("LG", [128, 4, 40], c=c0)
            CB = sb("CB", [128, 4, 32], c=c0)
            g8 = sb("g8", [128, 8], c=c0)
            i8 = sb("i8", [128, 8], U32, c=c0)
            f8 = sb("f8", [128, 8], c=c0)
            oh = sb("oh", [128, 32], c=c0)
            o2 = sb("o2", [128, 32], c=c0)
            s1 = sb("s1", [128, 8], c=c0)
            wk, w, wm = weight()
            ones = []

            def dv(fn, *marks):
                return dve.op(fn, dve.last(), *marks)

            for tb in range(4):
                kb, bank, m = project(w, 8, ht, tb, 40, wm)
                wlast = m
                lg = LG[:, tb, :]
                m = dv(lambda e, lg=lg, bank=bank: e.tensor_tensor(lg, bank[:, 0:40], gg("br"), ALU.add), m)
                banks.free(kb, m)
                dv(lambda e, lg=lg: e.max(g8[:, :], lg[:, 0:8]))
                dv(lambda e, lg=lg: e.max_index(i8[:, :], g8[:, :], lg[:, 0:8]))
                dv(lambda e: e.tensor_copy(f8[:, :], i8[:, :]))
                dv(lambda e: e.tensor_scalar(s1[:, 0:1], g8[:, 0:1], -1.0, None, ALU.mult))
                m = act.op(lambda e, lg=lg: e.activation(oh[:, 0:8], lg[:, 0:8], ACT.Exp, bias=s1[:, 0:1], accum_out=s1[:, 1:2]), dve.last())
                dv(lambda e: e.reciprocal(s1[:, 1:2], s1[:, 1:2]), m)
                dv(lambda e: e.tensor_scalar(oh[:, 0:8], cc("iota")[:, 0:8], f8[:, 0:1], NEG, ALU.not_equal, ALU.mult))
                dv(lambda e, lg=lg: e.tensor_tensor(o2[:, :].rearrange("p (g x) -> p g x", g=8), lg[:, 8:40].rearrange("p (g x) -> p g x", g=8), oh[:, 0:8].unsqueeze(2).to_broadcast([128, 8, 4]), ALU.add))
                dv(lambda e: e.max(g8[:, :], o2[:, :]))
                dv(lambda e: e.max_index(i8[:, :], g8[:, :], o2[:, :]))
                dv(lambda e: e.tensor_copy(f8[:, :], i8[:, :]))
                dv(lambda e: e.tensor_tensor(s1[:, 2:3], g8[:, 1:2], g8[:, 0:1], ALU.subtract))
                m = act.op(lambda e: e.activation(s1[:, 3:4], s1[:, 2:3], ACT.Exp), dve.last())
                dv(lambda e: e.tensor_scalar(s1[:, 4:5], s1[:, 3:4], 1.0, None, ALU.add), m)
                dv(lambda e: e.reciprocal(s1[:, 4:5], s1[:, 4:5]))
                dv(lambda e: e.tensor_tensor(s1[:, 5:6], s1[:, 4:5], s1[:, 1:2], ALU.mult))
                dv(lambda e: e.tensor_tensor(s1[:, 6:7], s1[:, 5:6], s1[:, 3:4], ALU.mult))
                dv(lambda e: e.tensor_scalar(oh[:, :], cc("iota")[:, 0:32], f8[:, 0:1], s1[:, 5:6], ALU.is_equal, ALU.mult))
                dv(lambda e: e.tensor_scalar(o2[:, :], cc("iota")[:, 0:32], f8[:, 1:2], s1[:, 6:7], ALU.is_equal, ALU.mult))
                dv(lambda e, tb=tb: e.tensor_tensor(CB[:, tb, :], oh[:, :], o2[:, :], ALU.add))
            done(wk, wlast)
            ahead()
            show("cb", CB[:, :, :])
            SL = Ring([sb(f"SL{n}", [128, 256], c=c0) for n in range(4)])
            HN = Ring([sb(f"HN{n}", [128, 256], c=c0) for n in range(4)])
            HH = Ring([sb(f"HH{n}", [128, 256], c=c0) for n in range(4)])
            A, B_, W_ = {}, {}, {}
            dve.need(dve.last())

            def up(n):
                e_, tb = divmod(n, 4)
                if tb == 0:
                    W_[e_] = [weight(), weight()]
                wk, w, wm = W_[e_][0]
                kb, bank, m = project(w, 8, ht, tb, 512, wm)
                if tb == 3:
                    done(wk, m)
                    ahead()
                sk, s, fr = SL.take()
                m = act.op(lambda e: e.activation(s[:, :], bank[:, 0:256], ACT.Silu), m, fr)
                hk, hn, fr = HN.take()
                m = dve.op(lambda e: e.scalar_tensor_tensor(hn[:, :], s[:, :], CB[:, tb, e_:e_ + 1], bank[:, 256:512], ALU.mult, ALU.mult), m, fr)
                SL.free(sk, m)
                banks.free(kb, m)
                A[n] = (hk, hn, m)

            def turn_h(n):
                hk, hn, m = A.pop(n)
                kb, bank, fr = banks.take()
                m = flips([(bank[:, 128 * j:128 * j + 128], hn[:, 128 * j:128 * j + 128]) for j in range(2)], m, fr)
                HN.free(hk, m)
                tk, t, fr = HH.take()
                m = act.op(lambda e: e.activation(t[:, :], bank[:, 0:256], ACT.Copy), m, fr)
                banks.free(kb, m)
                B_[n] = (tk, t, m)

            def down(n):
                e_, tb = divmod(n, 4)
                tk, t, m = B_.pop(n)
                wk, w, wm = W_[e_][1]
                for half_ in range(2):
                    kb, bank, fr = banks.take()
                    m2 = mms(bank, [(bank[:, :], t[:, 128 * j:128 * j + 128], w[:, 1024 * j + 512 * half_:1024 * j + 512 * half_ + 512]) for j in range(2)], m, fr, wm)
                    o = X[:, tb, 512 * half_:512 * half_ + 512]
                    banks.free(kb, dve.op(lambda e, o=o, bank=bank: e.tensor_tensor(o, o, bank[:, :], ALU.add), m2))
                HH.free(tk, m2)
                if tb == 3:
                    done(wk, m2)
                    ahead()

            stages(128, (0, up), (1, turn_h), (2, down))
            show("x2", X[:, :, :])
            barrier()
        if stop == "moe":
            return finish_program(nc, ctx, (pe, dve, act, pool, sp), dsem)

        with ExitStack() as c1:
            sq = sb("sqf", [128, 1024], c=c1)
            st = sb("stf", [128, 4], c=c1)
            got = [act.op(lambda e, b=b: e.activation(sq[:, :], X[:, b, :], ACT.Square, accum_out=st[:, b:b + 1])) for b in range(4)]
            m = rstd(st[:, 0:4], st[:, 0:4], 1024, got[-1])
            ms = [dve.op(lambda e, b=b: e.scalar_tensor_tensor(X[:, b, :], X[:, b, :], st[:, b:b + 1], gg("final"), ALU.mult, ALU.mult), m) for b in range(4)]
            show("x3", X[:, :, :])
            hm = normed(X, HT, 4, "mix2", ms, c1)
        barrier()
        with ExitStack() as c0:
            oTs = sb("oTs", [128, 4, 512], c=c0)
            oTd = sb("oTd", [128, 2, 512], c=c0)
            oTm = sb("oTm", [128, 4, 512], c=c0)
            with ExitStack() as c1:
                qT = sb("sqT", [128, 4, 512], c=c1)
                kT = sb("skT", [128, 4, 512], c=c1)
                vs = sb("svs", [128, 4, 512], c=c1)
                for dst, sc in ((qT, 0.125), (kT, None)):
                    wk, w, wm = weight()
                    wv = w.rearrange("p (k n) -> p k n", k=8)
                    for j in range(4):
                        kb, bank, fr = banks.take()
                        m = mms(bank, [(bank[:, :], wv[:, k, 128 * j:128 * j + 128], HT[:, k, :]) for k in range(8)], fr, wm)
                        wlast = m
                        banks.free(kb, copy(dst[:, j, :], bank[:, :], m, scale=sc))
                    done(wk, wlast)
                    ahead()
                wk, w, wm = weight()
                for tb in range(4):
                    kb, bank, m = project(w, 8, ht, tb, 512, wm)
                    wlast = m
                    banks.free(kb, copy(vs[:, tb, :], bank[:, :], m))
                done(wk, wlast)
                ahead()
                barrier()
                Z = Ring([sb(f"Z{n}", [128, 512], c=c1) for n in range(4)])
                A1 = Ring([sb(f"A1{n}", [128, 512], c=c1) for n in range(3)])
                SPL = Ring([sb(f"SPL{n}", [128, 512], c=c1) for n in range(3)])
                PT = Ring([sb(f"PTs{n}", [128, 512], c=c1) for n in range(3)])
                ON = Ring([sb(f"ONs{n}", [128, 512], c=c1) for n in range(2)])
                S, E1, E, T, O = {}, {}, {}, {}, {}
                hs = lambda h: slice(64 * (h % 2), 64 * (h % 2) + 64)

                def score(n):
                    i, h = divmod(n, 8)
                    kn = 128 * i + 128
                    kb, bank, fr = banks.take()
                    m = mms(bank, [(bank[:, 0:kn], qT[hs(h), h // 2, 128 * i:128 * i + 128], kT[hs(h), h // 2, 0:kn])], fr)
                    zk, z, fr = Z.take()
                    m = dve.op(lambda e: e.tensor_tensor(z[:, 0:kn], bank[:, 0:kn], cc("bs")[:, 512 - kn:512], ALU.add), m, fr)
                    banks.free(kb, m)
                    S[n] = (zk, z, m)

                def keep(n):
                    i, h = divmod(n, 8)
                    kn = 128 * i + 128
                    zk, z, m = S.pop(n)
                    ak, a, fr = A1.take()
                    m1 = act.op(lambda e: e.activation(a[:, 0:kn], z[:, 0:kn], ACT.Abs), m, fr)
                    m1 = act.op(lambda e: e.activation(a[:, 0:kn], a[:, 0:kn], ACT.Exp, scale=-1.0), m1)
                    m1 = act.op(lambda e: e.activation(a[:, 0:kn], a[:, 0:kn], ACT.Ln, bias=1.0), m1)
                    pk, p, fr = SPL.take()
                    m1 = dve.op(lambda e: e.scalar_tensor_tensor(a[:, 0:kn], z[:, 0:kn], 0.0, a[:, 0:kn], ALU.max, ALU.add), m1)
                    r = a[:, 0:kn][:, ::-1]
                    m1 = dve.op(lambda e: e.tensor_tensor_scan(p[:, 0:kn][:, ::-1], r, r, 0.0, ALU.add, ALU.bypass), m1, fr)
                    m2 = dve.op(lambda e: e.tensor_tensor(z[:, 0:kn], z[:, 0:kn], p[:, 0:kn], ALU.subtract), m1)
                    A1.free(ak, m1)
                    SPL.free(pk, m2)
                    m = act.op(lambda e: e.activation(z[:, 0:kn], z[:, 0:kn], ACT.Exp), m2)
                    E[n] = (zk, z, m)

                def turned(n):
                    i, h = divmod(n, 8)
                    kn = 128 * i + 128
                    zk, z, m = E.pop(n)
                    kb, bank, fr = banks.take()
                    m = flips([(bank[:, 128 * j:128 * j + 128], z[:, 128 * j:128 * j + 128]) for j in range(i + 1)], m, fr)
                    Z.free(zk, m)
                    tk, t, fr = PT.take()
                    m = copy(t[:, 0:kn], bank[:, 0:kn], m, fr)
                    banks.free(kb, m)
                    T[n] = (tk, t, m)

                def value(n):
                    i, h = divmod(n, 8)
                    tk, t, m = T.pop(n)
                    if h == 0:
                        O["b"] = banks.take()
                    kb, bank, fr = O["b"]
                    m = mms(bank, [(bank[:, 64 * h:64 * h + 64], t[:, 128 * j:128 * j + 128], vs[:, j, 64 * h:64 * h + 64]) for j in range(i + 1)], m, fr if h == 0 else None)
                    PT.free(tk, m)
                    if h == 7:
                        ok, on, fr = ON.take()
                        m = act.op(lambda e: e.activation(on[:, :], bank[:, :], ACT.Copy), m, fr)
                        banks.free(kb, m)
                        kb, bk, fr = banks.take()
                        m = flips([(bk[:, 128 * j:128 * j + 128], on[:, 128 * j:128 * j + 128]) for j in range(4)], m, fr)
                        ON.free(ok, m)
                        banks.free(kb, copy(oTs[:, :, 128 * i:128 * i + 128], bk[:, :].rearrange("p (k t) -> p k t", k=4), m))

                stages(32, (0, score), (1, keep), (2, turned), (3, value))
                show("oTs", oTs[:, :, :])
                barrier()

            def headnorm(st3, src, heads, width, gain, scale, sq, ss, m):
                bc = lambda a: a.unsqueeze(2).to_broadcast([128, heads, width])
                m = dve.op(lambda e: e.tensor_tensor(sq, src, src, ALU.mult), m)
                m = dve.op(lambda e: e.tensor_reduce(ss, sq, AX.X, ALU.add), m)
                m = rstd(ss, ss, width, m)
                m = dve.op(lambda e: e.tensor_tensor(st3, src, bc(ss), ALU.mult), m)
                g = gg(gain).unsqueeze(1).to_broadcast([128, heads, width])
                m = dve.op(lambda e: e.tensor_tensor(st3, st3, g, ALU.mult), m)
                if scale is not None:
                    m = dve.op(lambda e: e.tensor_scalar(st3, st3, scale, None, ALU.mult), m)
                return m

            with ExitStack() as c1:
                dqT = sb("dqT", [128, 6, 512], c=c1)
                dkT = sb("dkT", [128, 6, 512], c=c1)
                dvN = sb("dvN", [128, 3, 4, 256], c=c1)
                oTg = sb("oTg", [128, 3, 2, 512], c=c1)
                LS = sb("LS", [128, 3, 4, 4], c=c1)
                with ExitStack() as c2:
                    ST = Ring([sb(f"SV{n}", [128, 384], c=c2) for n in range(3)])
                    sq = sb("sqh", [128, 6, 64], c=c2)
                    ss = sb("ssh", [128, 6], c=c2)
                    for g in range(4):
                        dst, gain, sc = ((dqT, "qd", 0.125), (dkT, "kd", None))[g // 2]
                        wk, w, wm = weight()
                        for tb in range(4):
                            kb, bank, m = project(w, 8, ht, tb, 384, wm)
                            wlast = m
                            sk, s, fr = ST.take()
                            s3 = s[:, :].rearrange("p (h f) -> p h f", h=6)
                            m = act.op(lambda e, s=s, bank=bank: e.activation(s[:, :], bank[:, 0:384], ACT.Copy), m, fr)
                            banks.free(kb, m)
                            m = headnorm(s3, s3, 6, 64, gain, sc, sq[:, :, :], ss[:, :], m)
                            kb, bank, fr = banks.take()
                            m = flips([(bank[:, 128 * j:128 * j + 128], s[:, 128 * j:128 * j + 128]) for j in range(3)], m, fr)
                            ST.free(sk, m)
                            j0 = 3 * (g % 2)
                            n = 1 if j0 else 3
                            ms = [copy(dst[:, j0:j0 + n, 128 * tb:128 * tb + 128], bank[:, 0:128 * n].rearrange("p (k t) -> p k t", k=n), m)]
                            for j in range(n, 3):
                                src = bank[:, 128 * j:128 * j + 128].rearrange("p (l b r) -> p b r l", b=4, r=4)
                                o = dst[:, j0 + j, :].rearrange("p (b r l) -> p b r l", b=4, r=4)[:, :, :, 8 * tb:8 * tb + 8]
                                ms.append(act.op(lambda e: e.activation(o, src, ACT.Copy), m, ms[0]))
                            banks.free(kb, *ms)
                        done(wk, wlast)
                        ahead()

                    def cols(a, g, b, n=1):
                        if g == 0:
                            return a[:, 128 * b:128 * b + 128]
                        if g == 1:
                            return a.rearrange("p (t b) -> p b t", b=4)[:, b, :]
                        return a.rearrange("p (l b r) -> p b r l", b=4, r=4)[:, b, :, :]

                    HP = sb("HP", [128, 8, 512], c=c2)
                    mp = []
                    for k in range(8):
                        o = HP[:, k, :].rearrange("p (b r l) -> p b r l", b=4, r=4)
                        src = HT[:, k, :].rearrange("p (l b r) -> p b r l", b=4, r=4)
                        for b in range(4):
                            mp.append(copy(o[:, b], src[:, b]))
                    for g in range(3):
                        wk, w, wm = weight()
                        for b in range(4):
                            kb, bank, fr = banks.take()
                            pe.need(*mp)
                            m = mms(bank, [(bank[:, 0:256], HP[:, k, 128 * b:128 * b + 128] if g == 2 else cols(HT[:, k, :], g, b), w[:, 256 * k:256 * k + 256]) for k in range(8)], fr, wm)
                            wlast = m
                            banks.free(kb, copy(dvN[:, g, b, :], bank[:, 0:256], m))
                        done(wk, wlast)
                        ahead()
                    barrier()
                BD = sb("BD", [128, 2048], c=c1)
                dve.need(sp.dma(BD[:, :], d["bd"], ds("bd")))
                bd = BD[:, :]
                for g in range(3):
                    with ExitStack() as c2:
                        RI = sb(f"RI{g}", [128, 4], c=c2)
                        RL2 = sb(f"RL2{g}", [128, 4], c=c2)
                        ON = Ring([sb(f"OG{g}{n}", [128, 256], c=c2) for n in range(2)])

                        def q(i, h, g=g):
                            n = 4 * g + h
                            return cols(dqT[hs(n), n // 2, :], g % 2, i)

                        def k(i, h, g=g):
                            n = 4 * g + h
                            if g == 0:
                                return dkT[hs(n), n // 2, 128 * max(i - 1, 0):128 * i + 128]
                            return cols(dkT[hs(n), n // 2, :], g % 2, i)

                        def keys(i, g=g):
                            return 256 if g == 0 and i > 0 else 128

                        def v(i, h, j, g=g):
                            b = max(i - 1, 0) + j if g == 0 else i
                            return dvN[:, g, b, 64 * h:64 * h + 64]

                        def bias(i, h, g=g):
                            if g == 0:
                                o = 256 * h
                                return (bd[:, o + (0 if i else 128):o + 256], None)
                            o = 512 + 512 * g + 128 * h
                            return (bd[:, o:o + 128], None)

                        def finish(i, kb, bank, rs, mx, m, g=g, RI=RI, RL2=RL2, ON=ON):
                            al = act.last()
                            ml = act.op(lambda e: e.activation(RL2[:, :], rs, ACT.Ln), al, dve.last())
                            dve.op(lambda e: e.tensor_tensor(LS[:, g, i, :], RL2[:, :], mx, ALU.add), ml)
                            m1 = dve.op(lambda e: e.reciprocal(RI[:, :], rs), al)
                            ok, on, fr = ON.take()
                            o3 = on[:, :].rearrange("p (h w) -> p h w", h=4)
                            b3 = bank[:, 0:256].rearrange("p (h w) -> p h w", h=4)
                            m = dve.op(lambda e: e.tensor_tensor(o3, b3, RI[:, :].unsqueeze(2).to_broadcast([128, 4, 64]), ALU.mult), m, m1, fr)
                            banks.free(kb, m)
                            k2, bk, fr = banks.take()
                            m = flips([(bk[:, 128 * j:128 * j + 128], on[:, 128 * j:128 * j + 128]) for j in range(2)], m, fr)
                            ON.free(ok, m)
                            ms = []
                            for j in range(2):
                                src = bk[:, 128 * j:128 * j + 128]
                                if g == 2:
                                    src = src.rearrange("p (r l) -> p r l", r=4)
                                ms.append(dve.op(lambda e, j=j, src=src: e.tensor_copy(cols(oTg[:, g, j, :], g, i), src), m))
                            banks.free(k2, *ms)

                        stages(16, *attend(c2, f"d{g}", 4, 4, q, k, v, keys, bias, 1.0, 64, finish))
                        barrier()
                with ExitStack() as c2:
                    LT = sb("LT", [4, 3, 512], c=c2)
                    MM = sb("MM", [4, 512], c=c2)
                    for g in range(3):
                        kb, bank, fr = banks.take()
                        m = flips([(bank[0:4, 128 * b:128 * b + 128], LS[:, g, b, :]) for b in range(4)], fr, dve.last())
                        ms = []
                        for b in range(4):
                            src = bank[0:4, 128 * b:128 * b + 128]
                            if g == 2:
                                src = src.rearrange("p (r l) -> p r l", r=4)
                            ms.append(dve.op(lambda e, g=g, b=b, src=src: e.tensor_copy(cols(LT[:, g, :], g, b), src), m))
                        banks.free(kb, *ms)
                    dv(lambda e: e.tensor_tensor(MM[:, :], LT[:, 0, :], LT[:, 1, :], ALU.max))
                    dv(lambda e: e.tensor_tensor(MM[:, :], MM[:, :], LT[:, 2, :], ALU.max))
                    dv(lambda e: e.tensor_tensor(LT[:, :, :], LT[:, :, :], MM[:, :].unsqueeze(1).to_broadcast([4, 3, 512]), ALU.subtract))
                    m = act.op(lambda e: e.activation(LT[:, :, :], LT[:, :, :], ACT.Exp), dve.last())
                    dv(lambda e: e.tensor_tensor(MM[:, :], LT[:, 0, :], LT[:, 1, :], ALU.add), m)
                    dv(lambda e: e.tensor_tensor(MM[:, :], MM[:, :], LT[:, 2, :], ALU.add))
                    dv(lambda e: e.reciprocal(MM[:, :], MM[:, :]))
                    dv(lambda e: e.tensor_tensor(LT[:, :, :], LT[:, :, :], MM[:, :].unsqueeze(1).to_broadcast([4, 3, 512]), ALU.mult))
                    for j in range(2):
                        for g in range(3):
                            kb, bank, fr = banks.take()
                            m = mms(bank, [(bank[:, :], cc("sel")[0:4, 128 * j:128 * j + 128], LT[:, g, :])], fr, dve.last())
                            dst = oTd[:, j, :] if g == 0 else oTg[:, g, j, :]
                            m = dve.op(lambda e, g=g, j=j, bank=bank, dst=dst: e.tensor_tensor(dst, oTg[:, g, j, :], bank[:, :], ALU.mult), m)
                            banks.free(kb, m)
                            if g:
                                dv(lambda e, g=g, j=j: e.tensor_tensor(oTd[:, j, :], oTd[:, j, :], oTg[:, g, j, :], ALU.add))
                    show("oTd", oTd[:, :, :])
                    barrier()
            with ExitStack() as c1:
                mqT = sb("mqT", [128, 4, 512], c=c1)
                mkT = sb("mkT", [128, 4, 256], c=c1)
                mv = sb("mv", [128, 2, 512], c=c1)
                MT = sb("MT", [128, 8, 256], c=c1)
                with ExitStack() as c2:
                    ME = sb("ME", [128, 2, 1024], c=c2)
                    m = sp.dma(ME[:, :, :], d["mem"].rearrange("(b p) n -> p b n", p=128), ds("mem"))
                    normed(ME, MT, 2, "mem2", m, c2)
                    barrier()
                with ExitStack() as c2:
                    ST = Ring([sb(f"SM{n}", [128, 512], c=c2) for n in range(3)])
                    sq = sb("sqm", [128, 4, 128], c=c2)
                    ss = sb("ssm", [128, 4], c=c2)
                    for dst, gain, lhs, nb in ((mqT, "qm", ht, 4), (mkT, "km", lambda k, tb: MT[:, k, 128 * tb:128 * tb + 128], 2)):
                        wk, w, wm = weight()
                        for tb in range(nb):
                            kb, bank, m = project(w, 8, lhs, tb, 512, wm)
                            wlast = m
                            sk, s, fr = ST.take()
                            s3 = s[:, :].rearrange("p (h f) -> p h f", h=4)
                            m = act.op(lambda e, s=s, bank=bank: e.activation(s[:, :], bank[:, :], ACT.Copy), m, fr)
                            banks.free(kb, m)
                            m = headnorm(s3, s3, 4, 128, gain, None, sq[:, :, :], ss[:, :], m)
                            kb, bank, fr = banks.take()
                            m = flips([(bank[:, 128 * j:128 * j + 128], s[:, 128 * j:128 * j + 128]) for j in range(4)], m, fr)
                            ST.free(sk, m)
                            banks.free(kb, copy(dst[:, :, 128 * tb:128 * tb + 128], bank[:, :].rearrange("p (k t) -> p k t", k=4), m))
                        done(wk, wlast)
                        ahead()
                    wk, w, wm = weight()
                    for tb in range(2):
                        kb, bank, m = project(w, 8, lambda k, tb: MT[:, k, 128 * tb:128 * tb + 128], tb, 512, wm)
                        wlast = m
                        banks.free(kb, copy(mv[:, tb, :], bank[:, :], m))
                    done(wk, wlast)
                    ahead()
                    barrier()
                fin = rows_out(c1, "m", 4, 128, oTm)
                stages(16, *attend(
                    c1, "m", 4, 4, lambda i, h: mqT[:, h, 128 * i:128 * i + 128], lambda i, h: mkT[:, h, :],
                    lambda i, h, j: mv[:, j, 128 * h:128 * h + 128], lambda i: 256, lambda i, h: None,
                    float(128 ** -0.5), 128, fin))
                show("oTm", oTm[:, :, :])
                barrier()
            yT = sb("yT2", [128, 8, 512], c=c0)
            with ExitStack() as c1:
                SG = Ring([sb(f"SH{n}", [128, 512], c=c1) for n in range(6)])
                for m_ in range(8):
                    wk, w, wm = weight()
                    ok, wo, om = weight()
                    wg = w.rearrange("p (k n) -> p k n", k=8)
                    parts = []
                    for b, (oT, off, kk) in enumerate(((oTs, 0, 4), (oTd, 512, 2), (oTm, 768, 4))):
                        kb, bank, fr = banks.take()
                        mg = mms(bank, [(bank[:, :], wg[:, k, 128 * b:128 * b + 128], HT[:, k, :]) for k in range(8)], fr, wm)
                        gk, g, fr = SG.take()
                        m = act.op(lambda e, g=g, bank=bank, b=b, m_=m_: e.activation(g[:, :], bank[:, :], ACT.Sigmoid, bias=gg("bg2")[:, 8 * b + m_:8 * b + m_ + 1]), mg, fr)
                        banks.free(kb, m)
                        kb, bank, fr = banks.take()
                        mw = mms(bank, [(bank[:, :], wo[:, off + 128 * k:off + 128 * k + 128], oT[:, k, :]) for k in range(kk)], fr, om)
                        m = dve.op(lambda e, g=g, bank=bank: e.tensor_tensor(g[:, :], g[:, :], bank[:, :], ALU.mult), mw, m)
                        banks.free(kb, m)
                        parts.append((gk, g, m))
                    done(wk, mw)
                    done(ok, mw)
                    ahead()
                    (k1, g1, m1), (k2, g2, m2), (k3, g3, m3) = parts
                    m = dve.op(lambda e, g1=g1, g2=g2: e.tensor_tensor(g1[:, :], g1[:, :], g2[:, :], ALU.add), m1, m2)
                    m = dve.op(lambda e, m_=m_, g1=g1, g3=g3: e.tensor_tensor(yT[:, m_, :], g1[:, :], g3[:, :], ALU.add), m, m3)
                    for kx in (k1, k2, k3):
                        SG.free(kx, m)
                proj_out(c1, "2", yT)
            show("x4", X[:, :, :])
            barrier()
        if stop == "attn2":
            return finish_program(nc, ctx, (pe, dve, act, pool, sp), dsem)

        WD = d["wspill"]
        with ExitStack() as c0:
            with ExitStack() as c1:
                normed(X, HT, 4, "ffn2", dve.last(), c1)
            barrier()
            IA = sb("IA", [128, 3, 512], c=c0)
            with ExitStack() as c1:
                QT = Ring([sb(f"QT{n}", [128, 2, 512], c=c1) for n in range(2)])
                SC = Ring([sb(f"SC{n}", [128, 2, 128], c=c1) for n in range(3)])
                TS = sb("TS", [128, 4, 8, 2, 16], c=c1)
                TI = sb("TI", [128, 4, 8, 2, 16], U32, c=c1)
                TF = sb("TF", [128, 4, 8, 2, 16], c=c1)
                SEL = sb("SEL", [128, 3, 4, 8, 16], c=c1)
                Qm = {}

                def queries(h):
                    wk, w, wm = weight()
                    sk, sub, sm = weight()
                    wv = w.rearrange("p (k n) -> p k n", k=8)
                    qk, q, qf = QT.take()
                    ms = []
                    for p in range(2):
                        kb, bank, fr = banks.take()
                        m = mms(bank, [(bank[:, :], wv[:, k, 128 * p:128 * p + 128], HT[:, k, :]) for k in range(8)], fr, wm)
                        m2 = act.op(lambda e, p=p, q=q, bank=bank: e.activation(q[:, p, :], bank[:, :], ACT.Copy), m, qf)
                        banks.free(kb, m2)
                        ms.append(m2)
                    done(wk, m)
                    Qm[h] = (qk, q, ms, sk, sub, sm)

                def tops(h):
                    qk, q, ms, sk, sub, sm = Qm.pop(h)
                    for tb in range(4):
                        kb, bank, fr = banks.take()
                        pe.need(fr, sm, *ms)
                        for p in range(2):
                            m = mms(bank, [(bank[:, 128 * p:128 * p + 128], q[:, p, 128 * tb:128 * tb + 128], sub[:, 128 * p:128 * p + 128])])
                        ck, s, fr = SC.take()
                        mc = act.op(lambda e, s=s, bank=bank: e.activation(s[:, :, :].rearrange("p a b -> p (a b)"), bank[:, 0:256], ACT.Copy), m, fr)
                        banks.free(kb, mc)
                        a1, a2, b1, b2 = [], [], [], []
                        for p in range(2):
                            a1.append(dve.op(lambda e, s=s, p=p, tb=tb: e.max(TS[:, tb, h, p, 0:8], s[:, p, :]), mc))
                        for p in range(2):
                            a2.append(dve.op(lambda e, s=s, p=p, tb=tb: e.max_index(TI[:, tb, h, p, 0:8], TS[:, tb, h, p, 0:8], s[:, p, :]), a1[p]))
                        for p in range(2):
                            b1.append(dve.op(lambda e, s=s, p=p, tb=tb: e.match_replace(s[:, p, :], TS[:, tb, h, p, 0:8], s[:, p, :], -3e38), a2[p]))
                        for p in range(2):
                            b2.append(dve.op(lambda e, s=s, p=p, tb=tb: e.max(TS[:, tb, h, p, 8:16], s[:, p, :]), b1[p]))
                        for p in range(2):
                            m2 = dve.op(lambda e, s=s, p=p, tb=tb: e.max_index(TI[:, tb, h, p, 8:16], TS[:, tb, h, p, 8:16], s[:, p, :]), b2[p])
                        SC.free(ck, m2)
                    QT.free(qk, m)
                    done(sk, m)
                    ahead()

                stages(8, (0, queries), (1, tops))
                dv(lambda e: e.tensor_copy(TF[:, :, :, :, :], TI[:, :, :, :, :]))
                CD = sb("CD", [128, 8, 256], c=c1)
                C2 = sb("C2", [128, 8, 256], c=c1)
                S16 = sb("S16", [128, 8, 16], c=c1)
                P16 = sb("P16", [128, 8, 16], U32, c=c1)
                A16 = sb("A16", [128, 8, 16], U32, c=c1)
                PF = sb("PF", [128, 2, 8, 16], c=c1)
                SM = sb("SM", [128, 8], c=c1)
                for tb in range(4):
                    s1_, s2_ = TS[:, tb, :, 0, :], TS[:, tb, :, 1, :]
                    for h in range(8):
                        c3 = CD[:, h, :].rearrange("p (a b) -> p a b", a=16)
                        a_ = TS[:, tb, h, 0, :].unsqueeze(2).to_broadcast([128, 16, 16])
                        b_ = TS[:, tb, h, 1, :].unsqueeze(1).to_broadcast([128, 16, 16])
                        m = dve.op(lambda e, c3=c3, a_=a_, b_=b_: e.tensor_tensor(c3, a_, b_, ALU.add), dve.last() if h == 0 else None)
                    dve.need(m)
                    for h in range(8):
                        m = dve.op(lambda e, h=h: e.max(S16[:, h, 0:8], CD[:, h, :]))
                    dve.need(m)
                    for h in range(8):
                        dve.op(lambda e, h=h: e.max_index(P16[:, h, 0:8], S16[:, h, 0:8], CD[:, h, :]))
                    for h in range(8):
                        m = dve.op(lambda e, h=h: e.match_replace(C2[:, h, :], S16[:, h, 0:8], CD[:, h, :], -3e38))
                    dve.need(m)
                    for h in range(8):
                        m = dve.op(lambda e, h=h: e.max(S16[:, h, 8:16], C2[:, h, :]))
                    dve.need(m)
                    for h in range(8):
                        m = dve.op(lambda e, h=h: e.max_index(P16[:, h, 8:16], S16[:, h, 8:16], C2[:, h, :]))
                    dv(lambda e: e.tensor_scalar(A16[:, :, :], P16[:, :, :], 4, None, ALU.logical_shift_right))
                    dv(lambda e: e.tensor_copy(PF[:, 0, :, :], A16[:, :, :]))
                    dv(lambda e: e.tensor_scalar(A16[:, :, :], P16[:, :, :], 15, None, ALU.bitwise_and))
                    dv(lambda e: e.tensor_copy(PF[:, 1, :, :], A16[:, :, :]))
                    for p in range(2):
                        for h in range(8):
                            c3 = CD[:, h, :].rearrange("p (a b) -> p a b", a=16)
                            pos = PF[:, p, h, :].unsqueeze(2).to_broadcast([128, 16, 16])
                            io = cc("iota")[:, 0:16].unsqueeze(1).to_broadcast([128, 16, 16])
                            m = dve.op(lambda e, c3=c3, pos=pos, io=io: e.tensor_tensor(c3, pos, io, ALU.is_equal), dve.last() if h == 0 else None)
                        dve.need(m)
                        for h in range(8):
                            c3 = CD[:, h, :].rearrange("p (a b) -> p a b", a=16)
                            f_ = TF[:, tb, h, p, :].unsqueeze(1).to_broadcast([128, 16, 16])
                            m = dve.op(lambda e, c3=c3, f_=f_: e.tensor_tensor(c3, c3, f_, ALU.mult))
                        dv(lambda e, p=p, tb=tb: e.tensor_reduce(SEL[:, p, tb, :, :], CD[:, :, :].rearrange("p h (a b) -> p h a b", a=16), AX.X, ALU.add))
                    dv(lambda e: e.tensor_tensor(PF[:, 0, :, :], S16[:, :, :], S16[:, :, 0:1].to_broadcast([128, 8, 16]), ALU.subtract))
                    m = act.op(lambda e: e.activation(PF[:, 1, :, :], PF[:, 0, :, :], ACT.Exp), dve.last())
                    dv(lambda e: e.tensor_reduce(SM[:, :], PF[:, 1, :, :], AX.X, ALU.add), m)
                    dv(lambda e: e.reciprocal(SM[:, :], SM[:, :]))
                    dv(lambda e, tb=tb: e.tensor_tensor(SEL[:, 2, tb, :, :], PF[:, 1, :, :], SM[:, :].unsqueeze(2).to_broadcast([128, 8, 16]), ALU.mult))
                for a in range(3):
                    kb, bank, fr = banks.take()
                    m = flips([(bank[:, 128 * tb:128 * tb + 128], SEL[:, a, tb, :, :].rearrange("p h s -> p (h s)")) for tb in range(4)], fr, dve.last())
                    banks.free(kb, copy(IA[:, a, :], bank[:, :], m))
                show("sel", IA[:, :, :])
                barrier()
            with ExitStack() as c1:
                OA = Ring([sb(f"OA{n}", [128, 4, 128], c=c1) for n in range(3)])
                OB = Ring([sb(f"OB{n}", [128, 4, 128], c=c1) for n in range(3)])
                TW = 32
                WS = Ring([sb(f"WS{n}", [128, 128, TW], c=c1) for n in range(2)])
                wsem = [ds("ws0"), ds("ws1")]
                cur = {}
                H4 = {}
                spilled = []

                def hot(n):
                    ak, a, fa = OA.take()
                    bk, b, fb = OB.take()
                    for j in range(4):
                        t = 4 * n + j
                        dve.op(lambda e, j=j, t=t: e.tensor_scalar(a[:, j, :], cc("iota"), IA[:, 0, t:t + 1], None, ALU.is_equal), fa if j == 0 else None)
                        m = dve.op(lambda e, j=j, t=t: e.tensor_scalar(b[:, j, :], cc("iota"), IA[:, 1, t:t + 1], IA[:, 2, t:t + 1], ALU.is_equal, ALU.mult), fb if j == 0 else None)
                    H4[n] = (ak, a, bk, b, m)

                def outer(n):
                    ak, a, bk, b, m = H4.pop(n)
                    if (4 * n) % TW == 0:
                        cur["w"] = WS.take()
                    wk, ws, fw = cur["w"]
                    kb, bank, fr = banks.take()
                    pe.need(m, fr)
                    for j in range(4):
                        m = mms(bank, [(bank[:, 128 * j:128 * j + 128], a[:, j, :], b[:, j, :])])
                    OA.free(ak, m)
                    OB.free(bk, m)
                    t0 = (4 * n) % TW
                    o = ws[:, :, t0:t0 + 4].rearrange("p i t -> p t i")
                    mc = act.op(lambda e: e.activation(o, bank[:, :].rearrange("p (t i) -> p t i", t=4), ACT.Copy), m, fw)
                    banks.free(kb, mc)
                    if t0 + 4 == TW:
                        c = 4 * n // TW
                        m = sp.dma(WD[:, :, c * TW:(c + 1) * TW].rearrange("i p t -> p i t"), ws[:, :, :], wsem[c % 2], mc)
                        WS.free(wk, m)
                        spilled.append(m)

                stages(128, (0, hot), (1, outer))
                sp.need(*spilled[-2:])
                barrier()
            with ExitStack() as c1:
                assert state["next"] == len(sizes) and not queued
                GR = Ring([sb(f"GR{n}", [128, 4, 512], c=c1) for n in range(2)])
                GA = Ring([sb(f"GA{n}", [128, 512], c=c1) for n in range(2)])
                WW = Ring([sb(f"WW{n}", [128, 4, 512], c=c1) for n in range(2)])
                U_, V_, Wg, Gs = {}, {}, {}, {}

                def load(g):
                    uk, ub, fu = wring.take()
                    U_[g] = (uk, ub, sp.dma(ub[:, :], d["u"][g].rearrange("p a k n -> p (a k n)"), ds(f"w{uk}"), fu))
                    vk, vb_, fv = wring.take()
                    V_[g] = (vk, vb_, sp.dma(vb_[:, :], d["v"][g].rearrange("p a n -> p (a n)"), ds(f"w{vk}"), fv))
                    wk, wb, fw = WW.take()
                    Wg[g] = (wk, wb, sp.dma(wb[:, :, :], WD[4 * g:4 * g + 4, :, :].rearrange("i p t -> p i t"), ds(f"ww{wk}"), fw))

                def first(g):
                    uk, ub, um = U_.pop(g)
                    wk, wb, wm = Wg.pop(g)
                    uv = ub[:, :].rearrange("p (a k n) -> p a k n", a=4, k=8)
                    gk, gr, fg = GR.take()
                    for a in range(4):
                        kb, bank, fr = banks.take()
                        m = mms(bank, [(bank[:, :], uv[:, a, k, :], HT[:, k, :]) for k in range(8)], fr, um)
                        ak, ga, fa = GA.take()
                        m2 = act.op(lambda e, ga=ga, bank=bank: e.activation(ga[:, :], bank[:, :], ACT.Gelu), m, fa)
                        banks.free(kb, m2)
                        m3 = dve.op(lambda e, ga=ga, a=a: e.tensor_tensor(gr[:, a, :], ga[:, :], wb[:, a, :], ALU.mult), m2, wm, fg)
                        GA.free(ak, m3)
                    wring.free(uk, m)
                    WW.free(wk, m3)
                    Gs[g] = (gk, gr, m3)

                def second(g):
                    gk, gr, gm = Gs.pop(g)
                    vk, vb_, vm = V_.pop(g)
                    vv = vb_[:, :].rearrange("p (a n) -> p a n", a=4)
                    for tb in range(4):
                        for half_ in range(2):
                            kb, bank, fr = banks.take()
                            m = mms(bank, [(bank[:, :], gr[:, a, 128 * tb:128 * tb + 128], vv[:, a, 512 * half_:512 * half_ + 512]) for a in range(4)], fr, gm, vm)
                            o = X[:, tb, 512 * half_:512 * half_ + 512]
                            ma = dve.op(lambda e, o=o, bank=bank: e.tensor_tensor(o, o, bank[:, :], ALU.add), m)
                            banks.free(kb, ma)
                    GR.free(gk, m)
                    wring.free(vk, m)

                for g in range(33):
                    if g == 0:
                        load(0)
                    if g < 32:
                        first(g)
                    if g + 1 < 32:
                        load(g + 1)
                    if g >= 1:
                        second(g - 1)
            m = sp.dma(out.rearrange("(b p) n -> p b n", p=128), X[:, :, :], ds("out"), dve.last())
            sp.need(m)
        finish_program(nc, ctx, (pe, dve, act, pool, sp), dsem)


def finish_program(nc, ctx, queues, dsem):
    pe, dve, act, pool, sp = queues
    for s, n in dsem.values():
        sp.need((s, n))
    with nc.Block() as block:
        block.tensor(lambda e: pe.run(e))
        block.vector(lambda e: dve.run(e))
        block.scalar(lambda e: act.run(e))
        block.gpsimd(lambda e: pool.run(e))
        block.sync(lambda e: sp.run(e))


def kernel(**inputs):
    import concourse.bacc as bacc
    from concourse.bass_utils import run_bass_kernel_spmd

    nc = bacc.Bacc("TRN2", target_bir_lowering=False, num_devices=1)
    arrays, sizes = lay({k: np.asarray(v) for k, v in inputs.items()})
    d = {n: nc.dram_tensor("in_" + n, a.shape, F32, kind="ExternalInput").ap() for n, a in arrays.items()}
    d["wspill"] = nc.dram_tensor("wspill", (128, 128, 512), F32, kind="Internal").ap()
    out = nc.dram_tensor("out_0", (512, 1024), F32, kind="ExternalOutput").ap()
    program(nc, d, out, sizes)
    r = run_bass_kernel_spmd(nc, [{"in_" + n: a for n, a in arrays.items()}], core_ids=[0])
    return r.results[0]["out_0"].reshape(1, 512, 1024)
```

```python
from contextlib import ExitStack

import numpy as np

import concourse.bass as bass
from concourse import mybir

F32 = mybir.dt.float32
F32R = mybir.dt.float32r
U32 = mybir.dt.uint32
I32 = mybir.dt.int32
ALU = mybir.AluOpType
ACT = mybir.ActivationFunctionType
AX = mybir.AxisListType
EPS = 1e-6
NEG = -1e30


class Calls:

    @staticmethod
    def activation(*a, **k):
        return lambda e: e.activation(*a, **k)

    @staticmethod
    def tensor_copy(*a, **k):
        return lambda e: e.tensor_copy(*a, **k)

    @staticmethod
    def tensor_tensor(*a, **k):
        return lambda e: e.tensor_tensor(*a, **k)

    @staticmethod
    def tensor_scalar(*a, **k):
        return lambda e: e.tensor_scalar(*a, **k)

    @staticmethod
    def scalar_tensor_tensor(*a, **k):
        return lambda e: e.scalar_tensor_tensor(*a, **k)

    @staticmethod
    def tensor_tensor_reduce(*a, **k):
        return lambda e: e.tensor_tensor_reduce(*a, **k)

    @staticmethod
    def tensor_tensor_scan(*a, **k):
        return lambda e: e.tensor_tensor_scan(*a, **k)

    @staticmethod
    def tensor_reduce(*a, **k):
        return lambda e: e.tensor_reduce(*a, **k)

    @staticmethod
    def reciprocal(*a, **k):
        return lambda e: e.reciprocal(*a, **k)

    @staticmethod
    def max(*a, **k):
        return lambda e: e.max(*a, **k)

    @staticmethod
    def max_index(*a, **k):
        return lambda e: e.max_index(*a, **k)

    @staticmethod
    def match_replace(*a, **k):
        return lambda e: e.match_replace(*a, **k)

    @staticmethod
    def matmul(*a, **k):
        return lambda e: e.matmul(*a, **k)

    @staticmethod
    def transpose(*a, **k):
        return lambda e: e.transpose(*a, **k)

    @staticmethod
    def memset(*a, **k):
        return lambda e: e.memset(*a, **k)

    @staticmethod
    def indirect_dma_start(*a, **k):
        return lambda e: e.indirect_dma_start(*a, **k)


class Queue:

    def __init__(self, sem, chained=False):
        self.sem, self.n, self.ops, self.met, self.chained = sem, 0, [], {}, chained

    def need(self, *marks):
        for m in marks:
            if m is None:
                continue
            if isinstance(m, list):
                self.need(*m)
            elif self.met.get(m[0].num, 0) < m[1]:
                self.met[m[0].num] = m[1]
                self.ops.append(lambda e, m=m: e.wait_ge(m[0], m[1]))

    def op(self, fn, *marks, mark=True, alone=False):
        self.need(*marks)
        if self.chained and not alone:
            self.need(self.last())
        call = fn(Calls)
        if not mark:
            self.ops.append(call)
            return None
        self.n += 1
        self.ops.append(lambda e: call(e).then_inc(self.sem, 1))
        return (self.sem, self.n)

    def last(self):
        return (self.sem, self.n) if self.n else None

    def dma(self, out, in_, sem, *marks):
        self.need(*marks)
        sem[1] += 16
        self.ops.append(lambda e: e.dma_start(out, in_).then_inc(sem[0], 16))
        return (sem[0], sem[1])

    def idma(self, out, out_offset, in_, in_offset, sem, *marks):
        self.need(*marks)
        sem[1] += 16
        self.ops.append(lambda e: e.indirect_dma_start(out, out_offset, in_, in_offset).then_inc(sem[0], 16))
        return (sem[0], sem[1])

    def run(self, e):
        for f in self.ops:
            f(e)


class Stream:

    def __init__(self, q):
        self.q, self.at = q, None

    def op(self, fn, *marks):
        self.at = self.q.op(fn, self.at, *marks, alone=True)
        return self.at


def weave(*parts):
    state = [[g, n, 0] for g, n in parts]
    while state:
        s = min(state, key=lambda s: s[2] / s[1])
        s[2] += 1
        try:
            next(s[0])
        except StopIteration:
            state.remove(s)


class Ring:

    def __init__(self, bufs):
        self.bufs, self.idle = bufs, [(k, []) for k in range(len(bufs))]

    def take(self):
        k, marks = self.idle.pop(0)
        return k, self.bufs[k], marks

    def free(self, k, *marks):
        self.idle.append((k, list(marks)))


def stages(n, *parts):
    for _ in staged(n, *parts):
        pass


def staged(n, *parts):
    for step in range(n + max(lag for lag, _ in parts)):
        for lag, fn in parts:
            if 0 <= step - lag < n:
                fn(step - lag)
        yield


CONST = {}
_at = 0
for _name, _w in (("ident", 128), ("iota", 128), ("ba", 512), ("bs", 512), ("cosa", 128), ("sina", 128),
                  ("cosb", 64), ("sinb", 64), ("sel", 256),
                  ("ones", 128), ("before", 128), ("rows", 4)):
    CONST[_name] = (_at, _w)
    _at += _w
NCONST = -(-_at // 8) * 8
GAIN = {}
_at = 0
for _name, _w in (("mix", 8), ("ffn", 8), ("mix2", 8), ("mem2", 8), ("ffn2", 8), ("bg2", 24), ("cq", 3),
                  ("ckv", 2), ("final", 1024), ("qd", 64), ("kd", 64), ("qm", 128), ("km", 128), ("br", 40)):
    GAIN[_name] = (_at, _w)
    _at += _w
NGAIN = -(-_at // 8) * 8


def constants():
    f = np.float32
    c = np.zeros((128, NCONST), f)

    def put(name, a):
        o, w = CONST[name]
        c[:a.shape[0], o:o + w] = a.reshape(a.shape[0], w)

    p = np.arange(128)
    put("ident", np.eye(128, dtype=f))
    put("iota", np.broadcast_to(np.arange(128, dtype=f), (128, 128)))
    a = np.zeros((128, 512), f)
    a[:, 384:] = np.where((p[None, :] // 64) <= (p[:, None] // 64), 0, NEG)
    put("ba", a)
    a = np.zeros((128, 512), f)
    a[:, 384:] = np.where(p[None, :] < p[:, None], 0, NEG)
    put("bs", a)
    for name, rot in (("a", 32), ("b", 16)):
        half = rot // 2
        inv = f(500000.0) ** (-np.arange(half, dtype=f) * f(2.0) / f(rot))
        ang = np.arange(512, dtype=f)[:, None] * inv.astype(f)[None, :]
        co, si = np.cos(ang).astype(f), np.sin(ang).astype(f)
        co = np.stack([co, co], 1).reshape(4, 128, rot).transpose(1, 0, 2)
        si = np.stack([-si, si], 1).reshape(4, 128, rot).transpose(1, 0, 2)
        put("cos" + name, np.ascontiguousarray(co))
        put("sin" + name, np.ascontiguousarray(si))
    slopes = np.exp2(f(-8.0) * np.arange(1, 13, dtype=f) / f(12)).astype(f)
    bd = np.zeros((128, 2048), f)
    gap = p[:, None] - (np.arange(256)[None, :] - 128)
    for h in range(4):
        b = -(slopes[h] * gap.astype(f))
        bd[:, 256 * h:256 * h + 256] = np.where((gap >= 0) & (gap <= 128), b, f(NEG))
    gap = p[:, None] - p[None, :]
    for h in range(4):
        bd[:, 1024 + 128 * h:1152 + 128 * h] = np.where(gap >= 0, -(slopes[4 + h] * (gap * 4).astype(f)), f(NEG))
        ok = (gap >= 0) & (p[:, None] // 32 == p[None, :] // 32)
        bd[:, 1536 + 128 * h:1664 + 128 * h] = np.where(ok, -(slopes[8 + h] * (gap * 16).astype(f)), f(NEG))
    s = np.zeros((4, 256), f)
    for h in range(4):
        s[h, 64 * h:64 * h + 64] = 1
    put("sel", s)
    put("ones", np.ones((128, 128), f))
    put("before", (p[:, None] < p[None, :]).astype(f))
    put("rows", (np.arange(4)[None, :] * 128 + p[:, None]).astype(f))
    return c, bd


def lay(i):
    def kxn(w):
        k, n = w.shape
        return w.reshape(k // 128, 128, n).transpose(1, 0, 2)

    def flat(*parts):
        return [np.ascontiguousarray(p).reshape(-1) for p in parts]

    w = i["w_in"][0]
    cq, ckv, kr, qb, kb, vb, qi, ki, wi, ga, gb = np.split(
        w, np.cumsum([384, 256, 32, 512, 512, 512, 512, 64, 8, 1024])[:10].tolist(), axis=1)
    tiles = [kxn(np.concatenate([cq, kr, ki, wi], 1)), kxn(qi), kxn(qb), kxn(kb), kxn(vb), kxn(ckv),
             kxn(i["w_uq"][0][:, :384]), kxn(i["w_uq"][0][:, 384:]), kxn(i["w_uk"][0]), kxn(i["w_uv"][0])]
    for m in range(8):
        s = slice(128 * m, 128 * m + 128)
        tiles.append(np.concatenate([kxn(np.concatenate([ga[:, s], gb[:, s]], 1)).reshape(128, -1),
                                     kxn(i["w_o_a"][0][:, s]).reshape(128, -1),
                                     kxn(i["w_o_b"][0][:, s]).reshape(128, -1)], 1))
    tiles += [kxn(i["w_out"][0][:, :512]), kxn(i["w_out"][0][:, 512:])]
    tiles.append(kxn(np.concatenate([i["w_router_group"][0], i["w_router_expert"][0]], 1)))
    w = i["w_in_2"][0]
    for k in range(3):
        tiles.append(kxn(w[:, 512 * k:512 * k + 512]))
    for k in range(4):
        tiles.append(kxn(w[:, 1536 + 384 * k:1920 + 384 * k]))
    for k in range(3):
        tiles.append(kxn(w[:, 3072 + 256 * k:3328 + 256 * k]))
    tiles.append(kxn(w[:, 3840:4352]))
    tiles += [kxn(i["w_mem_kv_2"][0][:, :512]), kxn(i["w_mem_kv_2"][0][:, 512:])]
    wg = i["w_gate_2"][0]
    for m in range(8):
        s = slice(128 * m, 128 * m + 128)
        tiles.append(kxn(np.concatenate([wg[:, 1024 * b + 128 * m:1024 * b + 128 * m + 128] for b in range(3)], 1)))
        tiles.append(np.concatenate([kxn(i["w_o_sb_2"][0][:, s]).reshape(128, -1),
                                     kxn(i["w_o_dil_2"][0][:, s]).reshape(128, -1),
                                     kxn(i["w_o_mem_2"][0][:, s]).reshape(128, -1)], 1))
    tiles += [kxn(i["w_out_2"][0][:, :512]), kxn(i["w_out_2"][0][:, 512:])]
    for h in range(8):
        tiles.append(kxn(i["w_peer_q_2"][0][:, 256 * h:256 * h + 256]))
        tiles.append(i["peer_subkeys_2"][0, h].transpose(2, 0, 1))
    sizes = [t.size // 128 for t in tiles]
    weights = np.concatenate(flat(*tiles))
    u = i["peer_u_2"][0].reshape(128, 32, 4, 8, 128).transpose(1, 4, 2, 3, 0)
    v = i["peer_v_2"][0].reshape(128, 32, 4, 1024).transpose(1, 0, 2, 3)
    g = np.zeros((128, NGAIN), np.float32)
    consts, bd = constants()

    def put(name, a, rows):
        o, w = GAIN[name]
        g[:, o:o + w] = np.broadcast_to(a[None, :], (128, w)) if rows else a.reshape(w, 128).T

    for name, key in (("mix", "norm_mix_g"), ("ffn", "norm_ffn_g"), ("mix2", "g_mix_2"), ("mem2", "g_mem_2"),
                      ("ffn2", "g_ffn_2"), ("bg2", "b_gate_2"), ("cq", "mla_q_norm_g"), ("ckv", "mla_kv_norm_g")):
        put(name, i[key][0], False)
    put("final", i["final_norm_g"], True)
    for name, key in (("qd", "g_q_dil_2"), ("kd", "g_k_dil_2"), ("qm", "g_q_mem_2"), ("km", "g_k_mem_2")):
        put(name, i[key][0], True)
    put("br", np.concatenate([i["b_router_group"][0], i["b_router_expert"][0]]), True)
    wup = np.concatenate([i["w_gate"][0], i["w_up"][0]], 2).reshape(32, 8, 128, 512).transpose(0, 2, 1, 3)
    wdn = i["w_down"][0].reshape(32, 2, 128, 1024).transpose(0, 2, 1, 3)
    return {"wup": np.ascontiguousarray(wup).reshape(4096, 4096), "wdn": np.ascontiguousarray(wdn).reshape(4096, 2048),
            "x": i["x"][0], "mem": i["mem_2"][0], "weights": weights, "u": np.ascontiguousarray(u),
            "v": np.ascontiguousarray(v), "gains": g, "consts": consts, "bd": bd}, sizes


def program(nc, d, out, sizes, stop=None, dump=None):
    ctx = ExitStack()
    with ctx:
        def sb(name, shape, dt=F32, c=ctx):
            t = c.enter_context(nc.sbuf_tensor(name, shape, dt))
            return t[(slice(None),) * len(shape)]

        def sb2(name, shape, c):
            at = nc.sbuf_base
            a = sb(name, shape, c=c)
            assert at % 32 == 0 and nc.sbuf_base - at == 4 * int(np.prod(shape[1:]))
            t = nc.alloc_sbuf_tensor_at(name + "r", shape, F32, offset=at)
            return a, t[(slice(None),) * len(shape)]

        def sem(name):
            return ctx.enter_context(nc.semaphore(name))

        pe, sp = Queue(sem("s_pe")), Queue(sem("s_sp"))
        dve, act, pool = (Queue(sem(n), chained=True) for n in ("s_dve", "s_act", "s_pool"))
        engines = (pe, dve, act, pool)
        banks = Ring([ctx.enter_context(nc.psum_tensor(f"bank{k}", [128, 512], F32))[:, :] for k in range(8)])
        dsem = {}

        def ds(name):
            if name not in dsem:
                dsem[name] = [sem("d_" + name), 0]
            return dsem[name]

        X = sb("X", [128, 4, 1024])
        C = sb("C", [128, NCONST])
        G = sb("G", [128, NGAIN])
        RT = sb("RT", [128, 2, 8])
        cw = ctx.enter_context(ExitStack())
        HT, HTl = sb2("HT", [128, 8, 512], cw)
        NS = 3
        W2 = [sb2(f"W{k}", [128, 4096], cw) for k in range(NS)]
        state = {"next": 0, "ring": Ring([a for a, _ in W2])}
        cc = lambda n: C[:, CONST[n][0]:CONST[n][0] + CONST[n][1]]
        gg = lambda n: G[:, GAIN[n][0]:GAIN[n][0] + GAIN[n][1]]
        ident = cc("ident")

        def dv(fn, *marks):
            return dve.op(fn, *marks)

        offs = np.concatenate([[0], np.cumsum(np.array(sizes) * 128)])
        queued = []

        def fetch():
            k, buf, marks = state["ring"].take()
            n = state["next"]
            state["next"] += 1
            src = d["weights"][int(offs[n]):int(offs[n + 1])].rearrange("(p f) -> p f", p=128)
            m = sp.dma(buf[:, 0:sizes[n]], src, ds(f"w{k}"), marks)
            queued.append((k, buf[:, 0:sizes[n]], m))

        def weight():
            if not queued:
                fetch()
            return queued.pop(0)

        def done(k, *marks):
            state["ring"].free(k, *marks)

        def ahead():
            while state["next"] < state.get("stop", len(sizes)) and state["ring"].idle:
                fetch()

        m_x = sp.dma(X[:, :, :], d["x"].rearrange("(b p) n -> p b n", p=128), ds("x"))
        m_c = sp.dma(C[:, :], d["consts"], ds("c"))
        ZR = sb("ZR", [128, 257], c=cw)
        m_zr = dve.op(lambda e: e.memset(ZR, 0.0))
        m_c = [m_c, sp.dma(G[:, :], d["gains"], ds("g"))]
        state["stop"] = len(sizes) - 16
        for q in (dve, act, pe, pool):
            q.need(m_c)
        ahead()

        def barrier():
            marks = [q.last() for q in engines]
            for q in engines + (sp,):
                q.need(*[m for m in marks])

        sp.need(m_zr)
        for j in range(11):
            m_zero = sp.dma(d["hs"][128 * j:128 * j + 128, :].rearrange("p (r c) -> p r c", r=4), ZR.unsqueeze(1).to_broadcast([128, 4, 257]), ds("zero"))
        dumps = {}

        def show(name, ap, *marks):
            if dump is None or name not in dump:
                return
            barrier()
            m = sp.dma(dump[name], ap, ds("dump"), *marks)
            for q in engines:
                q.need(m)

        flip = [0]

        def copy(out_, in_, *marks, scale=None):
            flip[0] ^= 1
            if flip[0]:
                s = 1.0 if scale is None else scale
                return act.op(lambda e: e.activation(out_, in_, ACT.Copy, scale=s), *marks)
            if scale is None:
                return dve.op(lambda e: e.tensor_copy(out_, in_), *marks)
            return dve.op(lambda e: e.tensor_scalar(out_, in_, scale, None, ALU.mult), *marks)

        def mms(bank, parts, *marks):
            pe.need(*marks)
            n = len(parts)
            for j, (o, a, b) in enumerate(parts):
                m = pe.op(lambda e, o=o, a=a, b=b, j=j: e.matmul(o, a, b, start=j == 0, stop=j == n - 1),
                          mark=j == n - 1)
            return m

        def split(x, hi, lo, *marks):
            m = act.op(lambda e: e.activation(hi.bitcast(F32R), x, ACT.Copy), *marks, alone=True)
            return dve.op(lambda e: e.tensor_tensor(lo.bitcast(F32R), x, hi, ALU.subtract), m, alone=True)

        def mm3(bank, parts, *marks):
            r = lambda a: a.bitcast(F32R)
            return mms(bank, [p for o, (ah, al), (bh, bl) in parts
                              for p in ((o, r(al), r(bh)), (o, r(ah), r(bl)), (o, r(ah), r(bh)))], *marks)

        def flips(parts, *marks):
            pe.need(*marks)
            for j, (o, a) in enumerate(parts):
                p = a.shape[0]
                m = pe.op(lambda e, o=o, a=a, p=p: e.transpose(o, a, ident[0:p, 0:p]), mark=j == len(parts) - 1)
            return m

        def rstd(o, ss, n, m):
            w = o.shape[1]
            v, t = RT[:, 0, 0:w], RT[:, 1, 0:w]
            m = dve.op(lambda e: e.tensor_scalar(v, ss, 1.0 / n, EPS, ALU.mult, ALU.add), m)
            m = act.op(lambda e: e.activation(o, v, ACT.Sqrt), m)
            m = dve.op(lambda e: e.reciprocal(o, o), m)
            m = dve.op(lambda e: e.tensor_tensor(t, o, o, ALU.mult), m)
            m = dve.op(lambda e: e.tensor_tensor(t, t, v, ALU.mult), m)
            m = dve.op(lambda e: e.tensor_scalar(t, t, -0.5, 1.5, ALU.mult, ALU.add), m)
            return dve.op(lambda e: e.tensor_tensor(o, o, t, ALU.mult), m)

        def norm_rows(src, dst, tmp, st, nb, width, marks):
            for b in range(nb):
                m = act.op(lambda e, b=b: e.activation(tmp, src[:, b, :], ACT.Square, accum_out=st[:, b:b + 1]), marks)
            m = rstd(st[:, 0:nb], st[:, 0:nb], width, m)
            return [dve.op(lambda e, b=b: e.tensor_scalar(dst[:, b, :], src[:, b, :], st[:, b:b + 1], None, ALU.mult), m) for b in range(nb)]

        def turn(src, dst, nb, kk, gain, marks):
            res = []
            for k in range(kk):
                kb, bank, fr = banks.take()
                m = flips([(bank[:, 128 * b:128 * b + 128], src[:, b, 128 * k:128 * k + 128]) for b in range(nb)], fr, marks)
                if isinstance(dst, tuple):
                    hi, lo = (x[:, k, 0:128 * nb] for x in dst)
                    b_, g_ = bank[:, 0:128 * nb], gain[:, k:k + 1]
                    m = act.op(lambda e: e.activation(hi.bitcast(F32R), b_, ACT.Copy, scale=g_), m, alone=True)
                    m = dve.op(lambda e: e.scalar_tensor_tensor(lo.bitcast(F32R), b_, g_, hi, ALU.mult, ALU.subtract), m, alone=True)
                    banks.free(kb, m)
                    res.append(m)
                    continue
                m = copy(dst[:, k, 0:128 * nb], bank[:, 0:128 * nb], m, scale=gain[:, k:k + 1])
                banks.free(kb, m)
                res.append(m)
            return res

        def normed(src, dst, nb, gain, marks, c):
            xn = sb("xn" + gain, [128, nb, 1024], c=c)
            sq = sb("sq" + gain, [128, 1024], c=c)
            st = sb("st" + gain, [128, nb], c=c)
            r = norm_rows(src, xn, sq, st, nb, 1024, marks)
            return turn(xn, dst, nb, 8, gg(gain), r)

        def project(w, kk, lhs, tb, n, *marks):
            kb, bank, fr = banks.take()
            m = mms(bank, [(bank[:, 0:n], lhs(k, tb), w[:, k * n:k * n + n]) for k in range(kk)], fr, *marks)
            return kb, bank, m

        ht = lambda k, tb: HT[:, k, 128 * tb:128 * tb + 128]

        def rope(x, tb, heads, half, name, t1, t2, m):
            w = 2 * half
            co = cc("cos" + name)[:, w * tb:w * tb + w]
            si = cc("sin" + name)[:, w * tb:w * tb + w]
            v = lambda a: a.rearrange("p (j f) -> p j f", j=2)
            marks = []
            x4 = x.rearrange("p h (j f) -> p h j f", j=2)
            a = t1.rearrange("p (h j f) -> p h j f", h=heads, j=2)
            b = t2.rearrange("p (h j f) -> p h j f", h=heads, j=2)
            co4 = v(co).unsqueeze(1).to_broadcast([128, heads, 2, half])
            si4 = v(si).unsqueeze(1).to_broadcast([128, heads, 2, half])
            m1 = dve.op(lambda e: e.tensor_tensor(a, x4, co4, ALU.mult), m)
            m2 = dve.op(lambda e: e.tensor_tensor(b, x4[:, :, ::-1, :], si4, ALU.mult), m)
            return dve.op(lambda e: e.tensor_tensor(x4, a, b, ALU.add), m1, m2)

        def attend(c, tag, blocks, heads, q, k, v, keys, bias, scale, width, finish, share=None):
            P, PT = share or (Ring([sb(f"P{tag}{n}", [128, 512], c=c) for n in range(4)]),
                              Ring([sb(f"PT{tag}{n}", [128, 512], c=c) for n in range(3)]))
            MX = sb("MX" + tag, [128, blocks * heads], c=c)
            NM = sb("NM" + tag, [128, blocks * heads], c=c)
            RS = sb("RS" + tag, [128, blocks * heads], c=c)
            S, E, F, T, O = {}, {}, {}, {}, {}

            def score(n):
                i, h = divmod(n, heads)
                kb, bank, fr = banks.take()
                S[n] = (kb, bank, mms(bank, [(bank[:, 0:keys(i)], q(i, h), k(i, h))], fr))

            def soft(n):
                i, h = divmod(n, heads)
                kb, bank, m = S.pop(n)
                pk, p, fr = P.take()
                kn = keys(i)
                b = bias(i, h)
                if b is not None:
                    m = dve.op(lambda e: e.tensor_tensor_reduce(p[:, 0:kn], bank[:, 0:kn], b[0], 1.0, -3e38, ALU.add, ALU.max, MX[:, n:n + 1]), m, fr, b[1])
                    src = p[:, 0:kn]
                    banks.free(kb, m)
                else:
                    m = dve.op(lambda e: e.tensor_reduce(MX[:, n:n + 1], bank[:, 0:kn], AX.X, ALU.max), m)
                    src = bank[:, 0:kn]
                m = dve.op(lambda e: e.tensor_scalar(NM[:, n:n + 1], MX[:, n:n + 1], -scale, None, ALU.mult), m)
                m = act.op(lambda e: e.activation(p[:, 0:kn], src, ACT.Exp, bias=NM[:, n:n + 1], scale=scale, accum_out=RS[:, n:n + 1]), m, fr)
                if b is None:
                    banks.free(kb, m)
                E[n] = (pk, p, m)

            def turned(n):
                i, h = divmod(n, heads)
                pk, p, m = E.pop(n)
                kb, bank, fr = banks.take()
                nb = keys(i) // 128
                m = flips([(bank[:, 128 * j:128 * j + 128], p[:, 128 * j:128 * j + 128]) for j in range(nb)], m, fr)
                P.free(pk, m)
                F[n] = (kb, bank, m)

            def kept(n):
                i, h = divmod(n, heads)
                kb, bank, m = F.pop(n)
                tk, t, fr = PT.take()
                m = copy(t[:, 0:keys(i)], bank[:, 0:keys(i)], m, fr)
                banks.free(kb, m)
                T[n] = (tk, t, m)

            def value(n):
                i, h = divmod(n, heads)
                tk, t, m = T.pop(n)
                if h == 0:
                    O["b"] = banks.take()
                kb, bank, fr = O["b"]
                o = bank[:, width * h:width * h + width]
                nb = keys(i) // 128
                m = mms(bank, [(o, t[:, 128 * j:128 * j + 128], v(i, h, j)) for j in range(nb)], m, fr if h == 0 else None)
                PT.free(tk, m)
                if h == heads - 1:
                    O["m"] = (kb, bank, m)

            def end(n):
                i, h = divmod(n, heads)
                if h == heads - 1:
                    s = slice(i * heads, i * heads + heads)
                    kb, bank, m = O["m"]
                    finish(i, kb, bank, RS[:, s], MX[:, s], m)

            return [(6, end), (5, value), (4, kept), (3, turned), (1, soft), (0, score)]

        def rows_out(c, tag, heads, width, oT, on=None):
            RI = sb("RI" + tag, [128, heads], c=c)
            ON = on or Ring([sb(f"ON{tag}{n}", [128, heads * width], c=c) for n in range(2)])
            kk = heads * width // 128

            def finish(i, kb, bank, rs, mx, m):
                m1 = dve.op(lambda e: e.reciprocal(RI[:, :], rs), act.last())
                ok, on, fr = ON.take()
                o3 = on[:, :].rearrange("p (h w) -> p h w", h=heads)
                b3 = bank[:, 0:heads * width].rearrange("p (h w) -> p h w", h=heads)
                m = dve.op(lambda e: e.tensor_tensor(o3, b3, RI[:, :].unsqueeze(2).to_broadcast([128, heads, width]), ALU.mult), m, m1, fr)
                banks.free(kb, m)
                k2, bk, fr = banks.take()
                m = flips([(bk[:, 128 * j:128 * j + 128], on[:, 128 * j:128 * j + 128]) for j in range(kk)], m, fr)
                ON.free(ok, m)
                src = bk[:, 0:128 * kk].rearrange("p (k t) -> p k t", k=kk)
                banks.free(k2, copy(oT[:, :, 128 * i:128 * i + 128], src, m))
            return finish

        def in_parts(c, tag):
            HTh, YH, YL = (sb(n + tag, [128, 8, 512], c=c) for n in ("HTh", "YH", "YL"))
            WH = Ring([sb(f"WH{tag}{n}", [128, 4096], c=c) for n in range(2)])

            def part(n):
                wk, w, wm = weight()
                hk, wh, fh = WH.take()
                wh, wl = wh[:, 0:n], W2[wk][1][:, 0:n]
                return wk, w, wm, hk, wh, wl, split(w[:, 0:n], wh, wl, wm, fh)

            first_ = part(2048 if tag == "1" else 3072)
            mh = [split(HT[:, k, :], HTh[:, k, :], HTl[:, k, :]) for k in range(8)]
            return HTh, YH, YL, WH, part, first_, mh

        def proj_out(YH, YL, WH, part, cur, marks):
            for half in range(2):
                nxt = part(4096) if half == 0 else None
                wk, w, wm, hk, wh, wl, ms = cur
                for tb in range(4):
                    kb, bank, fr = banks.take()
                    t = slice(128 * tb, 128 * tb + 128)
                    m = mm3(bank, [(bank, (YH[:, k, t], YL[:, k, t]), (wh[:, 512 * k:512 * k + 512], wl[:, 512 * k:512 * k + 512])) for k in range(8)], fr, ms, marks)
                    o = X[:, tb, 512 * half:512 * half + 512]
                    m2 = dve.op(lambda e: e.tensor_tensor(o, o, bank[:, :], ALU.add), m)
                    banks.free(kb, m2)
                done(wk, m)
                WH.free(hk, m)
                ahead()
                cur = nxt

        with ExitStack() as c0:
            with ExitStack() as c1:
                hm = normed(X, HT, 4, "mix", m_x, c1)
            show("hT", HT[:, :, :])
            pe.need(*hm)
            barrier()
            oTa = sb("oTa", [128, 4, 512], c=c0)
            oTb = sb("oTb", [128, 4, 512], c=c0)
            cqT = sb("cqT", [128, 3, 512], c=c0)
            krN = sb("krN", [128, 4, 32], c=c0)
            with ExitStack() as c1:
                qbT = sb("qbT", [128, 4, 512], c=c1)
                kbT = sb("kbT", [128, 4, 512], c=c1)
                vb = sb("vb", [128, 4, 512], c=c1)
                BI = sb("BI", [128, 4, 512], c=c1)
                ckvT = sb("ckvT", [128, 2, 512], c=c1)
                qaT = sb("qaT", [96, 8, 512], c=c1)
                kaT = sb("kaT", [96, 8, 512], c=c1)
                va = sb("va", [128, 4, 512], c=c1)
                c2 = c1.enter_context(ExitStack())
                qiT, kiT = oTa, oTb[:, 3, :]
                ST = Ring([oTb[:, n, :] for n in range(3)])
                SU = Ring([sb(f"SU{n}", [128, 768], c=c2) for n in range(3)])
                wiN = sb("wiN", [128, 4, 8], c=c2)
                t1 = sb("t1", [128, 128], c=c2)
                t2 = sb("t2", [128, 128], c=c2)
                sq = sb("sqc", [128, 384], c=c2)
                st = sb("stc", [128, 8], c=c2)
                kiN = sb("kiN", [128, 4, 128], c=c2)

                def first_work(tb, s, m):
                    dve.op(lambda e: e.tensor_copy(krN[:, tb, :], s[:, 384:416]), m)
                    rope(krN[:, tb, :].unsqueeze(1), tb, 1, 16, "a", t1[:, 0:32], t2[:, 0:32], None)
                    dve.op(lambda e: e.tensor_copy(kiN[:, tb, 0:64], s[:, 416:480]))
                    rope(kiN[:, tb, 0:16].unsqueeze(1), tb, 1, 8, "b", t1[:, 0:16], t2[:, 0:16], None)
                    dve.op(lambda e: e.tensor_copy(kiN[:, tb, 64:128], kiN[:, tb, 0:64]))
                    dve.op(lambda e: e.tensor_scalar(wiN[:, tb, :], s[:, 480:488], float(8 ** -0.5), None, ALU.mult))
                    m = act.op(lambda e: e.activation(sq[:, :], s[:, 0:384], ACT.Square, accum_out=st[:, tb:tb + 1]), m)
                    m = rstd(st[:, tb:tb + 1], st[:, tb:tb + 1], 384, m)
                    return dve.op(lambda e: e.tensor_scalar(s[:, 0:384], s[:, 0:384], st[:, tb:tb + 1], None, ALU.mult), m)

                def first_kept(tb, got):
                    kb, bank, m = got[0]
                    for j in range(3):
                        dve.op(lambda e: e.tensor_scalar(cqT[:, j, 128 * tb:128 * tb + 128], bank[:, 128 * j:128 * j + 128], gg("cq")[:, j:j + 1], None, ALU.mult), m)
                    banks.free(kb, dve.op(lambda e: e.tensor_copy(kiT[:, 128 * tb:128 * tb + 128], bank[:, 384:512])))

                def turn4(srcs, m):
                    kb, bank, fr = banks.take()
                    p = srcs[0].shape[1]
                    return kb, bank, flips([(bank[0:p, 128 * j:128 * j + 128], x) for j, x in enumerate(srcs)], m, fr)

                def by128(s):
                    return [s[:, 128 * j:128 * j + 128] for j in range(4)]

                def keep4(dst, tb, got):
                    kb, bank, m = got[0]
                    banks.free(kb, copy(dst[:, :, 128 * tb:128 * tb + 128], bank[:, :].rearrange("p (k t) -> p k t", k=4), m))

                def keep96(dst, h0, tb, got):
                    for g, (kb, bank, m) in enumerate(got):
                        banks.free(kb, copy(dst[:, h0 + 4 * g:h0 + 4 * g + 4, 128 * tb:128 * tb + 128], bank[0:96, :].rearrange("p (h t) -> p h t", h=4), m))

                def direct(dst):
                    return lambda tb, bank, m: copy(dst[:, tb, :], bank[:, :], m)

                def rows_of(tiles, ring):
                    n_, cur = 4 * len(tiles), {}
                    P0, P1, P2, P3 = ({} for _ in range(4))

                    def product(n):
                        tb = n % 4
                        kk, lhs, width, marks, *_ = tiles[n // 4]
                        if tb == 0:
                            cur["w"] = weight()
                        wk, w, wm = cur["w"]
                        P0[n] = project(w, kk, lhs, tb, width, wm, marks)
                        if tb == 3:
                            done(wk, P0[n][2])
                            ahead()

                    def out_(n):
                        kb, bank, m = P0.pop(n)
                        out, work = tiles[n // 4][4:6]
                        if work is None:
                            banks.free(kb, out(n % 4, bank, m))
                            return
                        sk, s, fr = ring.take()
                        m = out(s, bank, m, fr)
                        banks.free(kb, m)
                        P1[n] = (sk, s, m)

                    def work_(n):
                        if n in P1:
                            sk, s, m = P1.pop(n)
                            P2[n] = (sk, s, tiles[n // 4][5](n % 4, s, m))

                    def turns_(n):
                        if n in P2:
                            sk, s, m = P2.pop(n)
                            P3[n] = [turn4(x, m) for x in tiles[n // 4][6](n % 4, s)]
                            ring.free(sk, P3[n][-1][2])

                    def keep_(n):
                        if n in P3:
                            tiles[n // 4][7](n % 4, P3.pop(n))

                    return staged(n_, (4, keep_), (3, turns_), (2, work_), (1, out_), (0, product))

                def plain(w):
                    return lambda s, bank, m, fr: act.op(lambda e: e.activation(s[:, 0:w], bank[:, 0:w], ACT.Copy), m, fr)

                rope_b = lambda tb, s, m: rope(s[:, 0:512].rearrange("p (h f) -> p h f", h=8)[:, :, 0:16], tb, 8, 8, "b", t1[:, :], t2[:, :], m)
                turned_b = lambda dst: (8, ht, 512, None, plain(512), rope_b, lambda tb, s: [by128(s)], lambda tb, got: keep4(dst, tb, got))
                for _ in rows_of([(8, ht, 488, None, plain(488), first_work, lambda tb, s: [by128(s)[0:3] + [kiN[:, tb, :]]], first_kept)]
                                 + [turned_b(qiT)], ST):
                    pass
                barrier()
                RL = Ring([oTb[:, n, :] for n in range(2)])
                WA, WB = oTb[:, 2, :], kiN.rearrange("p b n -> p (b n)")
                M8 = sb("M8", [128, 8], c=c2)
                L0, L = {}, {}

                def logits(n):
                    i, h = divmod(n, 8)
                    i += 1
                    kn = 128 * i + 128
                    kb, bank, fr = banks.take()
                    o = 64 * (h % 2)
                    L0[n] = (kb, bank, mms(bank, [(bank[:, 0:kn], qiT[o:o + 64, h // 2, 128 * i:128 * i + 128], kiT[o:o + 64, 0:kn])], fr))

                def positive(n):
                    kn = 128 * (n // 8) + 256
                    kb, bank, m = L0.pop(n)
                    rk, r, fr = RL.take()
                    m = act.op(lambda e: e.activation(r[:, 0:kn], bank[:, 0:kn], ACT.Relu, scale=0.125), m, fr)
                    banks.free(kb, m)
                    L[n] = (rk, r, m)

                def summed(n):
                    i, h = divmod(n, 8)
                    i += 1
                    kn = 128 * i + 128
                    rk, r, m = L.pop(n)
                    if h == 0:
                        m = dve.op(lambda e: e.tensor_scalar(WA[:, 0:kn], r[:, 0:kn], wiN[:, i, 0:1], None, ALU.mult), m)
                    else:
                        m = dve.op(lambda e: e.scalar_tensor_tensor(WA[:, 0:kn], r[:, 0:kn], wiN[:, i, h:h + 1], WA[:, 0:kn], ALU.mult, ALU.add), m)
                    RL.free(rk, m)
                    if h == 7:
                        dve.op(lambda e: e.tensor_tensor(WA[:, 0:kn], WA[:, 0:kn], cc("ba")[:, 512 - kn:512], ALU.add))
                        a, b = WA, WB
                        for r_ in range(16):
                            dve.op(lambda e: e.max(M8[:, :], a[:, 0:kn]))
                            dve.op(lambda e: e.match_replace(b[:, 0:kn], M8[:, :], a[:, 0:kn], -2e30))
                            a, b = b, a
                            if r_ % 2:
                                yield
                        dve.op(lambda e: e.tensor_scalar(BI[:, i, 0:kn], a[:, 0:kn], -1.5e30, NEG, ALU.is_gt, ALU.mult))

                def index():
                    for n in range(26):
                        if n < 24:
                            logits(n)
                        if 1 <= n < 25:
                            positive(n - 1)
                        if n >= 2:
                            yield from summed(n - 2)
                        yield

                cql = lambda k, tb: cqT[:, k, 128 * tb:128 * tb + 128]
                ckl = lambda k, tb: ckvT[:, k, 128 * tb:128 * tb + 128]
                CK = []

                def latent_work(tb, s, m):
                    m = act.op(lambda e: e.activation(sq[:, 0:256], s[:, 0:256], ACT.Square, accum_out=st[:, 4 + tb:5 + tb]), m, dve.last())
                    m = rstd(st[:, 4 + tb:5 + tb], st[:, 4 + tb:5 + tb], 256, m)
                    return dve.op(lambda e: e.tensor_scalar(s[:, 0:256], s[:, 0:256], st[:, 4 + tb:5 + tb], None, ALU.mult), m)

                def latent_kept(tb, got):
                    kb, bank, m = got[0]
                    for j in range(2):
                        m = dve.op(lambda e: e.tensor_scalar(ckvT[:, j, 128 * tb:128 * tb + 128], bank[:, 128 * j:128 * j + 128], gg("ckv")[:, j:j + 1], None, ALU.mult), m)
                    banks.free(kb, m)
                    CK.append(m)

                def by96(s, n):
                    return [[s[:, 96 * (4 * g + j):96 * (4 * g + j) + 96] for j in range(4)] for g in range(n)]

                rope_a = lambda tb, s, m: rope(s[:, 0:384].rearrange("p (h f) -> p h f", h=4)[:, :, 64:96], tb, 4, 16, "a", t1[:, 0:128], t2[:, 0:128], m)
                s8 = lambda s: s.rearrange("p (h f) -> p h f", h=8)
                keys_out = lambda s, bank, m, fr: act.op(lambda e: e.activation(s8(s)[:, :, 0:64], bank[:, :].rearrange("p (h f) -> p h f", h=8), ACT.Copy), m, fr)
                keys_work = lambda tb, s, m: dve.op(lambda e: e.tensor_copy(s8(s)[:, :, 64:96], krN[:, tb, :].unsqueeze(1).to_broadcast([128, 8, 32])), m)
                latent = rows_of([turned_b(qbT), turned_b(kbT), (8, ht, 512, None, direct(vb), None, None, None)]
                                 + [(8, ht, 256, None, plain(256), latent_work, lambda tb, s: [by128(s)[0:2]], latent_kept)]
                                 + [(3, cql, 384, None, plain(384), rope_a, lambda tb, s: by96(s, 1), (lambda g: lambda tb, got: keep96(qaT, 4 * g, tb, got))(g)) for g in range(2)]
                                 + [(2, ckl, 512, CK, keys_out, keys_work, lambda tb, s: by96(s, 2), lambda tb, got: keep96(kaT, 0, tb, got)),
                                    (2, ckl, 512, CK, direct(va), None, None, None)], SU)
                weave((index(), 50), (latent, 36))
                show("bi", BI[:, 1:4, :])
                barrier()
                c2.close()
                half = lambda h: slice(64 * (h % 2), 64 * (h % 2) + 64)
                share = (Ring([sb(f"PP{n}", [128, 512], c=c1) for n in range(5)] + [BI[:, 0, :]]),
                         Ring([cqT[:, n, :] for n in range(3)] + [ckvT[:, 0, :]]))
                fin_b = rows_out(c1, "b", 8, 64, oTb, Ring([ckvT[:, 1, :]]))
                fin_a = rows_out(c1, "a", 8, 64, oTa, Ring([sb("ONa", [128, 512], c=c1)]))
                weave((staged(32, *attend(
                    c1, "b", 4, 8, lambda i, h: qbT[half(h), h // 2, 128 * i:128 * i + 128],
                    lambda i, h: kbT[half(h), h // 2, 0:128 * i + 128],
                    lambda i, h, j: vb[:, j, 64 * h:64 * h + 64], lambda i: 128 * i + 128,
                    lambda i, h: ((BI[:, i, 0:128 * i + 128] if i else cc("ba")[:, 384:512]), None), 0.125, 64, fin_b, share)), 38),
                    (staged(32, *attend(
                        c1, "a", 4, 8, lambda i, h: qaT[:, h, 128 * i:128 * i + 128],
                        lambda i, h: kaT[:, h, 0:128 * i + 128],
                        lambda i, h, j: va[:, j, 64 * h:64 * h + 64], lambda i: 128 * i + 128,
                        lambda i, h: (cc("ba")[:, 384 - 128 * i:512], None), float(96 ** -0.5), 64, fin_a, share)), 38))
                show("oTa", oTa[:, :, :])
                barrier()
            with ExitStack() as c1:
                SG = Ring([sb(f"SG{n}", [128, 512], c=c1) for n in range(4)])
                HTh, YH, YL, WH, part, cur, mh = in_parts(c1, "1")
                my = []
                for m_ in range(8):
                    nxt = part(2048 if m_ < 7 else 4096)
                    wk, w, wm, hk, wh, wl, msp = cur
                    wh, wl = (x.rearrange("p (k n) -> p k n", k=8) for x in (wh, wl))
                    parts = []
                    for b, (oT, off) in enumerate(((oTa, 2048), (oTb, 2560))):
                        kb, bank, fr = banks.take()
                        c_ = slice(128 * b, 128 * b + 128)
                        m = mm3(bank, [(bank, (wh[:, k, c_], wl[:, k, c_]), (HTh[:, k, :], HTl[:, k, :])) for k in range(8)], fr, msp, mh)
                        gk, g, fr = SG.take()
                        m = act.op(lambda e: e.activation(g[:, :], bank[:, :], ACT.Sigmoid), m, fr)
                        banks.free(kb, m)
                        kb, bank, fr = banks.take()
                        mw = mms(bank, [(bank[:, :], w[:, off + 128 * k:off + 128 * k + 128], oT[:, k, :]) for k in range(4)], fr, wm)
                        m = dve.op(lambda e: e.tensor_tensor(g[:, :], g[:, :], bank[:, :], ALU.mult), mw, m)
                        banks.free(kb, m)
                        parts.append((gk, g, m))
                    done(wk, mw)
                    WH.free(hk, mw)
                    ahead()
                    (k1, g1, m1), (k2, g2, m2) = parts
                    m = dve.op(lambda e: e.tensor_tensor(g1[:, :], g1[:, :], g2[:, :], ALU.add), m1, m2)
                    m = split(g1[:, :], YH[:, m_, :], YL[:, m_, :], m)
                    my.append(m)
                    SG.free(k1, m)
                    SG.free(k2, m)
                    cur = nxt
                proj_out(YH, YL, WH, part, cur, my)
            show("x1", X[:, :, :])
            barrier()
        if stop == "attn1":
            return finish_program(nc, ctx, (pe, dve, act, pool, sp), dsem)

        NT = 11
        HS, OS = d["hs"], d["os"]
        with ExitStack() as c0:
            XN = sb("XN", [128, 4, 1028], c=c0)
            SL_ = sb("slot", [128, 4], I32, c=c0)
            IX = sb("IX", [128, NT * 4], I32, c=c0)
            with ExitStack() as c1:
                sq = sb("sqe", [128, 1024], c=c1)
                st_ = sb("ste", [128, 4], c=c1)
                r = norm_rows(X, XN[:, :, 0:1024], sq, st_, 4, 1024, dve.last())
                hm = turn(XN[:, :, 0:1024], HT, 4, 8, gg("ffn"), r)
                pe.need(*hm)
                LG = sb("LG", [128, 4, 40], c=c1)
                GO = sb("GO", [128, 4, 8], c=c1)
                wk, w, wm = weight()

                def route(tb):
                    g8, f8, oh, o2, s1, cb = (sb(f"{n}{tb}", [128, k], c=c1) for n, k in (("g8", 8), ("f8", 8), ("oh", 32), ("o2", 32), ("s1", 8), ("cb", 32)))
                    i8 = sb(f"i8{tb}", [128, 8], U32, c=c1)
                    st = Stream(dve)
                    kb, bank, m = project(w, 8, ht, tb, 40, wm)
                    lg = LG[:, tb, :]
                    banks.free(kb, st.op(lambda e: e.tensor_tensor(lg, bank[:, 0:40], gg("br"), ALU.add), m))
                    route.last = m
                    yield
                    st.op(lambda e: e.max(g8, lg[:, 0:8]))
                    yield
                    st.op(lambda e: e.max_index(i8, g8, lg[:, 0:8]))
                    yield
                    st.op(lambda e: e.tensor_copy(f8, i8))
                    yield
                    st.op(lambda e: e.tensor_scalar(GO[:, tb, :], cc("iota")[:, 0:8], f8[:, 0:1], None, ALU.is_equal))
                    yield
                    st.op(lambda e: e.tensor_scalar(s1[:, 0:1], g8[:, 0:1], -1.0, None, ALU.mult))
                    m = act.op(lambda e: e.activation(oh[:, 0:8], lg[:, 0:8], ACT.Exp, bias=s1[:, 0:1], accum_out=s1[:, 1:2]), st.at, alone=True)
                    yield
                    st.op(lambda e: e.reciprocal(s1[:, 1:2], s1[:, 1:2]), m)
                    yield
                    st.op(lambda e: e.tensor_scalar(oh[:, 0:8], cc("iota")[:, 0:8], f8[:, 0:1], NEG, ALU.not_equal, ALU.mult))
                    yield
                    st.op(lambda e: e.tensor_tensor(o2.rearrange("p (g x) -> p g x", g=8), lg[:, 8:40].rearrange("p (g x) -> p g x", g=8), oh[:, 0:8].unsqueeze(2).to_broadcast([128, 8, 4]), ALU.add))
                    yield
                    st.op(lambda e: e.max(g8, o2))
                    yield
                    st.op(lambda e: e.max_index(i8, g8, o2))
                    yield
                    st.op(lambda e: e.tensor_copy(f8, i8))
                    yield
                    st.op(lambda e: e.tensor_tensor(s1[:, 2:3], g8[:, 1:2], g8[:, 0:1], ALU.subtract))
                    m = act.op(lambda e: e.activation(s1[:, 3:4], s1[:, 2:3], ACT.Exp), st.at, alone=True)
                    yield
                    st.op(lambda e: e.tensor_scalar(s1[:, 4:5], s1[:, 3:4], 1.0, None, ALU.add), m)
                    yield
                    st.op(lambda e: e.reciprocal(s1[:, 4:5], s1[:, 4:5]))
                    yield
                    st.op(lambda e: e.tensor_tensor(s1[:, 5:6], s1[:, 4:5], s1[:, 1:2], ALU.mult))
                    yield
                    st.op(lambda e: e.tensor_tensor(s1[:, 6:7], s1[:, 5:6], s1[:, 3:4], ALU.mult))
                    yield
                    st.op(lambda e: e.tensor_scalar(oh, cc("iota")[:, 0:32], f8[:, 0:1], s1[:, 5:6], ALU.is_equal, ALU.mult))
                    yield
                    st.op(lambda e: e.tensor_scalar(o2, cc("iota")[:, 0:32], f8[:, 1:2], s1[:, 6:7], ALU.is_equal, ALU.mult))
                    yield
                    st.op(lambda e: e.tensor_tensor(cb, oh, o2, ALU.add))
                    yield
                    st.op(lambda e: e.tensor_reduce(XN[:, tb, 1024:1028], cb.rearrange("p (g x) -> p x g", g=8), AX.X, ALU.add), r[tb])
                    route.marks.append(st.at)
                    yield

                route.marks = []
                weave(*[(route(tb), 21) for tb in range(4)])
                done(wk, route.last)
                ahead()
                marks = route.marks
                kb, bank, fr = banks.take()
                for tb in range(4):
                    m = mms(bank, [(bank[:, 8 * tb:8 * tb + 8], cc("before") if b_ == tb else cc("ones"), GO[:, b_, :]) for b_ in range(tb + 1)], fr, marks)
                m = mms(bank, [(bank[:, 32:40], cc("ones"), GO[:, b_, :]) for b_ in range(4)])
                RK = sb("RK", [128, 5, 8], c=c1)
                st = Stream(dve)
                m = st.op(lambda e: e.tensor_copy(RK, bank[:, 0:40].rearrange("p (b g) -> p b g", b=5)), m)
                banks.free(kb, m)
                TL, EN, T8 = (sb(n, [128, 8], c=c1) for n in ("TL", "EN", "T8"))
                for j in range(4):
                    st.op(lambda e: e.tensor_scalar(T8 if j else TL, RK[:, 4, :], 128.0 * j, None, ALU.is_gt))
                    if j:
                        st.op(lambda e: e.tensor_tensor(TL, TL, T8, ALU.add))
                st.op(lambda e: e.tensor_tensor_scan(EN, TL, TL, 0.0, ALU.add, ALU.bypass))
                st.op(lambda e: e.tensor_tensor(T8, EN, TL, ALU.subtract))
                st.op(lambda e: e.tensor_scalar(T8, T8, 128.0, None, ALU.mult))
                st.op(lambda e: e.tensor_tensor(RK[:, 0:4, :], RK[:, 0:4, :], T8.unsqueeze(1).to_broadcast([128, 4, 8]), ALU.add))
                st.op(lambda e: e.tensor_tensor(RK[:, 0:4, :], RK[:, 0:4, :], GO, ALU.mult))
                SF = sb("SF", [128, 4], c=c1)
                st.op(lambda e: e.tensor_reduce(SF, RK[:, 0:4, :], AX.X, ALU.add))
                ms = st.op(lambda e: e.tensor_copy(SL_, SF))
                GT = sb("GT", [128, NT, 8], c=c1)
                GI = sb("GI", [128, NT], c=c1)
                IF = sb("IF", [128, NT, 4], c=c1)
                st.op(lambda e: e.tensor_tensor(GT, EN.unsqueeze(1).to_broadcast([128, NT, 8]), cc("iota")[:, 0:NT].unsqueeze(2).to_broadcast([128, NT, 8]), ALU.is_le))
                st.op(lambda e: e.tensor_reduce(GI, GT, AX.X, ALU.add))
                st.op(lambda e: e.tensor_scalar(GI, GI, 7.0, 512.0, ALU.min, ALU.mult))
                st.op(lambda e: e.tensor_tensor(IF, cc("rows").unsqueeze(1).to_broadcast([128, NT, 4]), GI.unsqueeze(2).to_broadcast([128, NT, 4]), ALU.add))
                mi = st.op(lambda e: e.tensor_copy(IX, IF.rearrange("p a b -> p (a b)")))
                sc = [pool.idma(HS[:, :], bass.IndirectOffsetOnAxis(ap=SL_[:, tb:tb + 1], axis=0), XN[:, tb, :], None, ds(f"hs{tb}"), ms, m_zero) for tb in range(4)]
                show("xn", XN)
                barrier()
            UP = Ring([sb(f"UP{n}", [128, 4096], c=c0) for n in range(2)] + [HT.rearrange("p k n -> p (k n)")])
            DN = Ring([sb(f"DN{n}", [128, 2048], c=c0) for n in range(4)])
            HR = Ring([sb(f"HR{n}", [128, 1028], c=c0) for n in range(2)])
            HX = Ring([sb(f"HX{n}", [128, 8, 128], c=c0) for n in range(2)])
            SL = Ring([sb(f"SL{n}", [128, 256], c=c0) for n in range(2)])
            HN = Ring([sb(f"HN{n}", [128, 256], c=c0) for n in range(2)])
            HH = Ring([sb(f"HH{n}", [128, 256], c=c0) for n in range(3)])
            OT = Ring([sb(f"OT{n}", [128, 1024], c=c0) for n in range(2)])
            WT, HM, A, B_, OB_, stored = {}, {}, {}, {}, {}, []

            def fetch_expert(n):
                uk, u, fu = UP.take()
                nk, dn, fn_ = DN.take()
                off = lambda: bass.IndirectOffsetOnAxis(ap=IX[:, n:n + 1], axis=0)
                WT[n] = (uk, u, pool.idma(u, None, d["wup"][:, :], off(), ds(f"up{uk}"), fu, mi),
                         nk, dn, pool.idma(dn, None, d["wdn"][:, :], off(), ds(f"dn{nk}"), fn_))

            def tile_in(j):
                hk, hr, fh = HR.take()
                m = sp.dma(hr, HS[128 * j:128 * j + 128, :], ds(f"hr{hk}"), fh, sc)
                xk, hx, fx = HX.take()
                ms = []
                for half_ in range(2):
                    kb, bank, fr = banks.take()
                    m1 = flips([(bank[:, 128 * q:128 * q + 128], hr[:, 512 * half_ + 128 * q:512 * half_ + 128 * q + 128]) for q in range(4)], m, fr)
                    g4 = gg("ffn")[:, 4 * half_:4 * half_ + 4].unsqueeze(2).to_broadcast([128, 4, 128])
                    m2 = dve.op(lambda e: e.tensor_tensor(hx[:, 4 * half_:4 * half_ + 4, :], bank.rearrange("p (a b) -> p a b", a=4), g4, ALU.mult), m1, fx, alone=True)
                    banks.free(kb, m2)
                    ms.append(m2)
                HM[j] = (hk, hr, m, xk, hx, ms)

            def up(n):
                j, x = divmod(n, 4)
                hk, hr, mr, xk, hx, ms = HM[j]
                uk, u, um, nk, dn, nm = WT[n]
                kb, bank, fr = banks.take()
                m = mms(bank, [(bank, hx[:, k, :], u[:, 512 * k:512 * k + 512]) for k in range(8)], fr, um, ms)
                UP.free(uk, m)
                if x == 3:
                    HX.free(xk, m)
                sk, s, fs = SL.take()
                m = act.op(lambda e: e.activation(s, bank[:, 0:256], ACT.Silu), m, fs, alone=True)
                hk2, hn, fh = HN.take()
                m = dve.op(lambda e: e.scalar_tensor_tensor(hn, s, hr[:, 1024 + x:1025 + x], bank[:, 256:512], ALU.mult, ALU.mult), m, fh, mr, alone=True)
                SL.free(sk, m)
                banks.free(kb, m)
                if x == 3:
                    HR.free(hk, m)
                A[n] = (hk2, hn, m)

            def turn_h(n):
                hk, hn, m = A.pop(n)
                kb, bank, fr = banks.take()
                m = flips([(bank[:, 128 * j:128 * j + 128], hn[:, 128 * j:128 * j + 128]) for j in range(2)], m, fr)
                HN.free(hk, m)
                tk, t, ft = HH.take()
                m = act.op(lambda e: e.activation(t, bank[:, 0:256], ACT.Copy), m, ft, alone=True)
                banks.free(kb, m)
                B_[n] = (tk, t, m)

            def down(n):
                j, x = divmod(n, 4)
                tk, t, m = B_.pop(n)
                nk, dn, nm = WT.pop(n)[3:]
                if x == 0:
                    OB_[j] = [banks.take(), banks.take()]
                for half_ in range(2):
                    kb, bank, fr = OB_[j][half_]
                    pe.need(m, nm, fr)
                    for q in range(2):
                        first_, last_ = x == 0 and q == 0, x == 3 and q == 1
                        a, b = t[:, 128 * q:128 * q + 128], dn[:, 1024 * q + 512 * half_:1024 * q + 512 * half_ + 512]
                        m2 = pe.op(lambda e: e.matmul(bank, a, b, start=first_, stop=last_, skip_group_check=True))
                HH.free(tk, m2)
                DN.free(nk, m2)
                if x == 3:
                    ok, o, fo = OT.take()
                    ms = []
                    for half_ in range(2):
                        kb, bank, _ = OB_[j][half_]
                        o_ = o[:, 512 * half_:512 * half_ + 512]
                        ms.append(act.op(lambda e: e.activation(o_, bank, ACT.Copy), m2, fo, alone=True) if half_ else
                                  dve.op(lambda e: e.tensor_copy(o_, bank), m2, fo, alone=True))
                        banks.free(kb, ms[-1])
                    m = sp.dma(OS[128 * j:128 * j + 128, :], o, ds(f"os{ok}"), ms)
                    OT.free(ok, m)
                    stored.append(m)

            fetch_expert(0)
            fetch_expert(1)
            tile_in(0)

            def more(n):
                if n + 2 < 4 * NT:
                    fetch_expert(n + 2)
                if n % 4 == 2 and n // 4 + 1 < NT:
                    tile_in(n // 4 + 1)

            stages(4 * NT, (0, up), (1, turn_h), (2, down), (0, more))
            YG = [XN[:, n, 0:1024] for n in range(4)]
            for tb in range(4):
                m = pool.idma(YG[tb], None, OS[:, :], bass.IndirectOffsetOnAxis(ap=SL_[:, tb:tb + 1], axis=0), ds(f"yg{tb}"), stored[-2:], sc)
                dve.op(lambda e: e.tensor_tensor(X[:, tb, :], X[:, tb, :], YG[tb], ALU.add), m)
            show("x2", X[:, :, :])
            barrier()
        if stop == "moe":
            return finish_program(nc, ctx, (pe, dve, act, pool, sp), dsem)

        with ExitStack() as c1:
            sq = sb("sqf", [128, 1024], c=c1)
            st = sb("stf", [128, 4], c=c1)
            got = [act.op(lambda e, b=b: e.activation(sq[:, :], X[:, b, :], ACT.Square, accum_out=st[:, b:b + 1])) for b in range(4)]
            m = rstd(st[:, 0:4], st[:, 0:4], 1024, got[-1])
            ms = [dve.op(lambda e, b=b: e.scalar_tensor_tensor(X[:, b, :], X[:, b, :], st[:, b:b + 1], gg("final"), ALU.mult, ALU.mult), m) for b in range(4)]
            show("x3", X[:, :, :])
            hm = normed(X, HT, 4, "mix2", ms, c1)
        barrier()
        with ExitStack() as c0:
            oTs = sb("oTs", [128, 4, 512], c=c0)
            oTd = sb("oTd", [128, 2, 512], c=c0)
            oTm = sb("oTm", [128, 4, 512], c=c0)
            ca = c0.enter_context(ExitStack())
            dqT = sb("dqT", [128, 6, 512], c=ca)
            dkT = sb("dkT", [128, 6, 512], c=ca)
            dvN = sb("dvN", [128, 3, 4, 256], c=ca)

            def cols(a, g, b):
                if g == 0:
                    return a[:, 128 * b:128 * b + 128]
                if g == 1:
                    return a.rearrange("p (t b) -> p b t", b=4)[:, b, :]
                return a.rearrange("p (l b r) -> p b r l", b=4, r=4)[:, b, :, :]

            def headnorm(st3, src, heads, width, gain, scale, sq, ss, m):
                bc = lambda a: a.unsqueeze(2).to_broadcast([128, heads, width])
                m = dve.op(lambda e: e.tensor_tensor(sq, src, src, ALU.mult), m)
                m = dve.op(lambda e: e.tensor_reduce(ss, sq, AX.X, ALU.add), m)
                m = rstd(ss, ss, width, m)
                m = dve.op(lambda e: e.tensor_tensor(st3, src, bc(ss), ALU.mult), m)
                g = gg(gain).unsqueeze(1).to_broadcast([128, heads, width])
                if scale is not None:
                    return dve.op(lambda e: e.scalar_tensor_tensor(st3, st3, scale, g, ALU.mult, ALU.mult), m)
                return dve.op(lambda e: e.tensor_tensor(st3, st3, g, ALU.mult), m)

            with ExitStack() as c1:
                qT = sb("sqT", [128, 4, 512], c=c1)
                kT = sb("skT", [128, 4, 512], c=c1)
                vs = sb("svs", [128, 4, 512], c=c1)
                for dst, sc in ((qT, 0.125), (kT, None)):
                    wk, w, wm = weight()
                    wv = w.rearrange("p (k n) -> p k n", k=8)
                    for j in range(4):
                        kb, bank, fr = banks.take()
                        m = mms(bank, [(bank[:, :], wv[:, k, 128 * j:128 * j + 128], HT[:, k, :]) for k in range(8)], fr, wm)
                        wlast = m
                        banks.free(kb, copy(dst[:, j, :], bank[:, :], m, scale=sc))
                    done(wk, wlast)
                    ahead()
                barrier()
                Z = Ring([sb(f"Z{n}", [128, 512], c=c1) for n in range(4)] + [oTm[:, n, :] for n in (0, 1)])
                A1 = Ring([sb(f"A1{n}", [128, 512], c=c1) for n in range(2)] + [oTm[:, 2, :]])
                SPL = Ring([sb(f"SPL{n}", [128, 512], c=c1) for n in range(2)])
                PT = Ring([sb(f"PTs{n}", [128, 512], c=c1) for n in range(2)])
                ON = Ring([sb(f"ONs{n}", [128, 512], c=c1) for n in range(1)])
                S0, S, E0, E1, E, T0, T, O = ({} for _ in range(8))
                hs = lambda h: slice(64 * (h % 2), 64 * (h % 2) + 64)

                def score(n):
                    i, h = divmod(n, 8)
                    kn = 128 * i + 128
                    kb, bank, fr = banks.take()
                    S0[n] = (kb, bank, mms(bank, [(bank[:, 0:kn], qT[hs(h), h // 2, 128 * i:128 * i + 128], kT[hs(h), h // 2, 0:kn])], fr))

                def masked(n):
                    i, h = divmod(n, 8)
                    kn = 128 * i + 128
                    kb, bank, m = S0.pop(n)
                    zk, z, fr = Z.take()
                    m = dve.op(lambda e: e.tensor_tensor(z[:, 0:kn], bank[:, 0:kn], cc("bs")[:, 512 - kn:512], ALU.add), m, fr)
                    banks.free(kb, m)
                    S[n] = (zk, z, m)

                def keep(n):
                    i, h = divmod(n, 8)
                    kn = 128 * i + 128
                    zk, z, m = S.pop(n)
                    ak, a, fr = A1.take()
                    m1 = act.op(lambda e: e.activation(a[:, 0:kn], z[:, 0:kn], ACT.Abs), m, fr)
                    m1 = act.op(lambda e: e.activation(a[:, 0:kn], a[:, 0:kn], ACT.Exp, scale=-1.0), m1)
                    m1 = act.op(lambda e: e.activation(a[:, 0:kn], a[:, 0:kn], ACT.Ln, bias=1.0), m1)
                    E0[n] = (zk, z, ak, a, m1)

                def sums(n):
                    i, h = divmod(n, 8)
                    kn = 128 * i + 128
                    zk, z, ak, a, m1 = E0.pop(n)
                    pk, p, fr = SPL.take()
                    m1 = dve.op(lambda e: e.scalar_tensor_tensor(a[:, 0:kn], z[:, 0:kn], 0.0, a[:, 0:kn], ALU.max, ALU.add), m1)
                    r = a[:, 0:kn][:, ::-1]
                    m1 = dve.op(lambda e: e.tensor_tensor_scan(p[:, 0:kn][:, ::-1], r, r, 0.0, ALU.add, ALU.bypass), m1, fr)
                    m2 = dve.op(lambda e: e.tensor_tensor(z[:, 0:kn], z[:, 0:kn], p[:, 0:kn], ALU.subtract), m1)
                    A1.free(ak, m1)
                    SPL.free(pk, m2)
                    E1[n] = (zk, z, m2)

                def power(n):
                    i, h = divmod(n, 8)
                    kn = 128 * i + 128
                    zk, z, m2 = E1.pop(n)
                    m = act.op(lambda e: e.activation(z[:, 0:kn], z[:, 0:kn], ACT.Exp), m2)
                    E[n] = (zk, z, m)

                def turned(n):
                    i, h = divmod(n, 8)
                    kn = 128 * i + 128
                    zk, z, m = E.pop(n)
                    kb, bank, fr = banks.take()
                    m = flips([(bank[:, 128 * j:128 * j + 128], z[:, 128 * j:128 * j + 128]) for j in range(i + 1)], m, fr)
                    Z.free(zk, m)
                    T0[n] = (kb, bank, m)

                def turned2(n):
                    i, h = divmod(n, 8)
                    kn = 128 * i + 128
                    kb, bank, m = T0.pop(n)
                    tk, t, fr = PT.take()
                    m = copy(t[:, 0:kn], bank[:, 0:kn], m, fr)
                    banks.free(kb, m)
                    T[n] = (tk, t, m)

                def value(n):
                    i, h = divmod(n, 8)
                    tk, t, m = T.pop(n)
                    if h == 0:
                        O["b"] = banks.take()
                    kb, bank, fr = O["b"]
                    m = mms(bank, [(bank[:, 64 * h:64 * h + 64], t[:, 128 * j:128 * j + 128], vs[:, j, 64 * h:64 * h + 64]) for j in range(i + 1)], m, VM[0:i + 1], fr if h == 0 else None)
                    PT.free(tk, m)
                    if h == 7:
                        O["m"] = (kb, bank, m)

                def rows(n):
                    i, h = divmod(n, 8)
                    if h == 7:
                        kb, bank, m = O["m"]
                        ok, on, fr = ON.take()
                        m = act.op(lambda e: e.activation(on[:, :], bank[:, :], ACT.Copy), m, fr)
                        banks.free(kb, m)
                        kb, bk, fr = banks.take()
                        m = flips([(bk[:, 128 * j:128 * j + 128], on[:, 128 * j:128 * j + 128]) for j in range(4)], m, fr)
                        ON.free(ok, m)
                        banks.free(kb, copy(oTs[:, :, 128 * i:128 * i + 128], bk[:, :].rearrange("p (k t) -> p k t", k=4), m))

                DST = Ring([sb(f"SV{n}", [128, 384], c=c1) for n in range(3)])
                sq = sb("sqh", [128, 6, 64], c=c1)
                ss = sb("ssh", [128, 6], c=c1)
                HP = Ring([oTd.rearrange("p a (b n) -> p (a b) n", b=4)])
                DW, DA, DN_, DP, VM = {}, {}, {}, {}, []

                def dil_rows(n):
                    g, tb = divmod(n, 4)
                    if tb == 0:
                        DW[g] = weight()
                    wk, w, wm = DW[g]
                    kb, bank, m = project(w, 8, ht, tb, 384, wm)
                    if tb == 3:
                        done(wk, m)
                        ahead()
                    DP[n] = (kb, bank, m)

                def dil_out(n):
                    kb, bank, m = DP.pop(n)
                    sk, s, fr = DST.take()
                    m = act.op(lambda e: e.activation(s[:, :], bank[:, 0:384], ACT.Copy), m, fr)
                    banks.free(kb, m)
                    DA[n] = (sk, s, m)

                def dil_norm(n):
                    g, tb = divmod(n, 4)
                    sk, s, m = DA.pop(n)
                    s3 = s.rearrange("p (h f) -> p h f", h=6)
                    DN_[n] = (sk, s, headnorm(s3, s3, 6, 64, ("qd", "kd")[g // 2], (0.125, None)[g // 2], sq, ss, m))

                def dil_turn(n):
                    g, tb = divmod(n, 4)
                    dst = (dqT, dkT)[g // 2]
                    sk, s, m = DN_.pop(n)
                    kb, bank, fr = banks.take()
                    m = flips([(bank[:, 128 * j:128 * j + 128], s[:, 128 * j:128 * j + 128]) for j in range(3)], m, fr)
                    DST.free(sk, m)
                    j0 = 3 * (g % 2)
                    n_ = 1 if j0 else 3
                    ms = [copy(dst[:, j0:j0 + n_, 128 * tb:128 * tb + 128], bank[:, 0:128 * n_].rearrange("p (k t) -> p k t", k=n_), m)]
                    for j in range(n_, 3):
                        src = bank[:, 128 * j:128 * j + 128].rearrange("p (l b r) -> p b r l", b=4, r=4)
                        o = dst[:, j0 + j, :].rearrange("p (b r l) -> p b r l", b=4, r=4)[:, :, :, 8 * tb:8 * tb + 8]
                        ms.append(act.op(lambda e: e.activation(o, src, ACT.Copy), m, ms[0]))
                    banks.free(kb, *ms)

                def dil_columns(n):
                    g, b = divmod(n, 4)
                    if g == 2:
                        k, hp, fr = HP.take()
                        src = HT.rearrange("p k (l b r) -> p b k r l", b=4, r=4)[:, b]
                        DP[n] = (k, hp, dve.op(lambda e: e.tensor_copy(hp.rearrange("p k (r l) -> p k r l", r=4), src), fr))

                def dil_values(n):
                    g, b = divmod(n, 4)
                    if b == 0:
                        DW["v"] = weight()
                    wk, w, wm = DW["v"]
                    k, hp, mp = DP.pop(n) if g == 2 else (None, None, None)
                    kb, bank, fr = banks.take()
                    m = mms(bank, [(bank[:, 0:256], hp[:, k_, :] if g == 2 else cols(HT[:, k_, :], g, b), w[:, 256 * k_:256 * k_ + 256]) for k_ in range(8)], fr, wm, mp)
                    if g == 2:
                        HP.free(k, m)
                    if b == 3:
                        done(wk, m)
                        ahead()
                    DA[n] = (kb, bank, m)

                def dil_kept(n):
                    g, b = divmod(n, 4)
                    kb, bank, m = DA.pop(n)
                    banks.free(kb, copy(dvN[:, g, b, :], bank[:, 0:256], m))

                def stick_values():
                    wk, w, wm = weight()
                    for tb in range(4):
                        kb, bank, m = project(w, 8, ht, tb, 512, wm)
                        if tb == 3:
                            done(wk, m)
                            ahead()
                        yield
                        VM.append(copy(vs[:, tb, :], bank[:, :], m))
                        banks.free(kb, VM[-1])

                def dilated():
                    yield from stick_values()
                    yield from staged(16, (1, dil_out), (0, dil_rows), (2, dil_norm), (3, dil_turn))
                    yield from staged(12, (2, dil_kept), (1, dil_values), (0, dil_columns))

                weave((staged(32, (8, rows), (7, value), (6, turned2), (5, turned), (4, power), (3, sums), (2, keep), (1, masked), (0, score)), 40), (dilated(), 35))
                show("oTs", oTs[:, :, :])
                barrier()

            with ExitStack() as c1:
                oTg = sb("oTg", [128, 3, 2, 512], c=c1)
                LS = sb("LS", [128, 3, 4, 4], c=c1)
                BD = sb("BD", [128, 2048], c=c1)
                dve.need(sp.dma(BD[:, :], d["bd"], ds("bd")))
                bd = BD[:, :]
                ME = sb("ME", [128, 2, 1024], c=c1)
                spare = ME.rearrange("p b n -> p (b n)")
                LT, MM = spare[0:4, 0:1536].rearrange("p (g t) -> p g t", g=3), spare[0:4, 1536:2048]
                share = (Ring([sb(f"Pd{n}", [128, 256], c=c1) for n in range(4)]),
                         Ring([sb(f"PTd{n}", [128, 256], c=c1) for n in range(3)]))

                OG = Ring([sb(f"OG{n}", [128, 256], c=c1) for n in range(2)])

                def dil_attention():
                    for g in range(3):
                        RI = sb(f"RI{g}", [128, 4], c=c1)
                        RL2 = sb(f"RL2{g}", [128, 4], c=c1)

                        def q(i, h, g=g):
                            n = 4 * g + h
                            return cols(dqT[hs(n), n // 2, :], g % 2, i)

                        def k(i, h, g=g):
                            n = 4 * g + h
                            if g == 0:
                                return dkT[hs(n), n // 2, 128 * max(i - 1, 0):128 * i + 128]
                            return cols(dkT[hs(n), n // 2, :], g % 2, i)

                        def keys(i, g=g):
                            return 256 if g == 0 and i > 0 else 128

                        def v(i, h, j, g=g):
                            b = max(i - 1, 0) + j if g == 0 else i
                            return dvN[:, g, b, 64 * h:64 * h + 64]

                        def bias(i, h, g=g):
                            if g == 0:
                                o = 256 * h
                                return (bd[:, o + (0 if i else 128):o + 256], None)
                            o = 512 + 512 * g + 128 * h
                            return (bd[:, o:o + 128], None)

                        def finish(i, kb, bank, rs, mx, m, g=g, RI=RI, RL2=RL2, ON=OG):
                            al = act.last()
                            ml = act.op(lambda e: e.activation(RL2[:, :], rs, ACT.Ln), al, dve.last())
                            dve.op(lambda e: e.tensor_tensor(LS[:, g, i, :], RL2[:, :], mx, ALU.add), ml)
                            m1 = dve.op(lambda e: e.reciprocal(RI[:, :], rs), al)
                            ok, on, fr = ON.take()
                            o3 = on[:, :].rearrange("p (h w) -> p h w", h=4)
                            b3 = bank[:, 0:256].rearrange("p (h w) -> p h w", h=4)
                            m = dve.op(lambda e: e.tensor_tensor(o3, b3, RI[:, :].unsqueeze(2).to_broadcast([128, 4, 64]), ALU.mult), m, m1, fr)
                            banks.free(kb, m)
                            k2, bk, fr = banks.take()
                            m = flips([(bk[:, 128 * j:128 * j + 128], on[:, 128 * j:128 * j + 128]) for j in range(2)], m, fr)
                            ON.free(ok, m)
                            ms = []
                            for j in range(2):
                                src = bk[:, 128 * j:128 * j + 128]
                                if g == 2:
                                    src = src.rearrange("p (r l) -> p r l", r=4)
                                ms.append(dve.op(lambda e, j=j, src=src: e.tensor_copy(cols(oTg[:, g, j, :], g, i), src), m))
                            banks.free(k2, *ms)

                        yield from staged(16, *attend(c1, f"d{g}", 4, 4, q, k, v, keys, bias, 1.0, 64, finish, share))
                    dve.need(MW["mt"])
                    for g in range(3):
                        kb, bank, fr = banks.take()
                        m = flips([(bank[0:4, 128 * b:128 * b + 128], LS[:, g, b, :]) for b in range(4)], fr, dve.last())
                        ms = []
                        for b in range(4):
                            src = bank[0:4, 128 * b:128 * b + 128]
                            if g == 2:
                                src = src.rearrange("p (r l) -> p r l", r=4)
                            ms.append(dve.op(lambda e, g=g, b=b, src=src: e.tensor_copy(cols(LT[:, g, :], g, b), src), m))
                        banks.free(kb, *ms)
                        yield
                    dv(lambda e: e.tensor_tensor(MM[:, :], LT[:, 0, :], LT[:, 1, :], ALU.max))
                    dv(lambda e: e.tensor_tensor(MM[:, :], MM[:, :], LT[:, 2, :], ALU.max))
                    dv(lambda e: e.tensor_tensor(LT[:, :, :], LT[:, :, :], MM[:, :].unsqueeze(1).to_broadcast([4, 3, 512]), ALU.subtract))
                    yield
                    m = act.op(lambda e: e.activation(LT[:, :, :], LT[:, :, :], ACT.Exp), dve.last())
                    dv(lambda e: e.tensor_tensor(MM[:, :], LT[:, 0, :], LT[:, 1, :], ALU.add), m)
                    dv(lambda e: e.tensor_tensor(MM[:, :], MM[:, :], LT[:, 2, :], ALU.add))
                    dv(lambda e: e.reciprocal(MM[:, :], MM[:, :]))
                    yield
                    dv(lambda e: e.tensor_tensor(LT[:, :, :], LT[:, :, :], MM[:, :].unsqueeze(1).to_broadcast([4, 3, 512]), ALU.mult))
                    for j in range(2):
                        for g in range(3):
                            kb, bank, fr = banks.take()
                            m = mms(bank, [(bank[:, :], cc("sel")[0:4, 128 * j:128 * j + 128], LT[:, g, :])], fr, dve.last())
                            dst = oTd[:, j, :] if g == 0 else oTg[:, g, j, :]
                            m = dve.op(lambda e, g=g, j=j, bank=bank, dst=dst: e.tensor_tensor(dst, oTg[:, g, j, :], bank[:, :], ALU.mult), m)
                            banks.free(kb, m)
                            yield
                            if g:
                                dv(lambda e, g=g, j=j: e.tensor_tensor(oTd[:, j, :], oTd[:, j, :], oTg[:, g, j, :], ALU.add))

                mqT = sb("mqT", [128, 4, 512], c=c1)
                MT = sb("MT", [128, 8, 256], c=c1)
                m_me = sp.dma(ME[:, :, :], d["mem"].rearrange("(b p) n -> p b n", p=128), ds("mem"))
                msq = oTm[:, 0:2, :].rearrange("p a b -> p (a b)")
                ss = sb("ssm", [128, 4], c=c1)
                sm = sb("sm2", [128, 2], c=c1)
                MS = Ring([oTm[:, 2, :], oTm[:, 3, :], oTd[:, 0, :]])
                sq = msq[:, 0:512].rearrange("p (h f) -> p h f", h=4)
                MW, MA, MN, MP = {}, {}, {}, {}
                mt = lambda k, tb: MT[:, k, 128 * tb:128 * tb + 128]

                def mem_rows(n):
                    if n in (0, 4):
                        MW["w"] = weight()
                    wk, w, wm = MW["w"]
                    kb, bank, m = project(w, 8, mt if n >= 4 else ht, n % 4, 512, wm, MW["mt"])
                    if n == 3:
                        f = state["ring"].bufs[wk]
                        MW["kept"] = (wk, m, f[:, 0:1024].rearrange("p (h t) -> p h t", h=4), f[:, 1024:2048].rearrange("p (b n) -> p b n", b=2), f[:, 2048:4096])
                    if n == 5:
                        done(wk, m)
                        ahead()
                    MP[n] = (kb, bank, m)

                def mem_out(n):
                    kb, bank, m = MP.pop(n)
                    sk, s, fr = MS.take()
                    m = act.op(lambda e: e.activation(s[:, :], bank[:, :], ACT.Copy), m, fr)
                    banks.free(kb, m)
                    MA[n] = (sk, s, m)

                def mem_norm(n):
                    sk, s, m = MA.pop(n)
                    s3 = s.rearrange("p (h f) -> p h f", h=4)
                    MN[n] = (sk, s, headnorm(s3, s3, 4, 128, "km" if n >= 4 else "qm", None, sq, ss, m))

                def mem_turn(n):
                    dst, tb = (MW["kept"][2] if n >= 4 else mqT), n % 4
                    sk, s, m = MN.pop(n)
                    kb, bank, fr = banks.take()
                    m = flips([(bank[:, 128 * j:128 * j + 128], s[:, 128 * j:128 * j + 128]) for j in range(4)], m, fr)
                    MS.free(sk, m)
                    banks.free(kb, copy(dst[:, :, 128 * tb:128 * tb + 128], bank[:, :].rearrange("p (k t) -> p k t", k=4), m, MW["kept"][1] if n >= 4 else None))

                def memory():
                    r = norm_rows(ME, ME, msq, sm, 2, 1024, m_me)
                    yield
                    MW["mt"] = turn(ME, MT, 2, 8, gg("mem2"), r)
                    yield
                    yield from staged(6, (1, mem_out), (0, mem_rows), (2, mem_norm), (3, mem_turn))
                    wk, w, wm = weight()
                    mkT, mv = MW["kept"][2:4]
                    for tb in range(2):
                        kb, bank, m = project(w, 8, mt, tb, 512, wm)
                        banks.free(kb, copy(mv[:, tb, :], bank[:, :], m))
                        yield
                    done(wk, m)
                    ahead()
                    pe.need(act.last(), dve.last())
                    m, f = MW["kept"][1], MW["kept"][4]
                    P, PT, on = (Ring([f[:, a + w * n:a + w * n + w] for n in range(k)]) for a, w, k in ((0, 256, 3), (768, 256, 3), (1536, 512, 1)))
                    for r in (P, PT, on):
                        r.idle = [(k, [m]) for k, _ in r.idle]
                    fin = rows_out(c1, "m", 4, 128, oTm, on=on)
                    yield from staged(16, *attend(
                        c1, "m", 4, 4, lambda i, h: mqT[:, h, 128 * i:128 * i + 128], lambda i, h: mkT[:, h, :],
                        lambda i, h, j: mv[:, j, 128 * h:128 * h + 128], lambda i: 256, lambda i, h: None,
                        float(128 ** -0.5), 128, fin, (P, PT)))

                weave((dil_attention(), 72), (memory(), 32))
                show("oTd", oTd[:, :, :])
                show("oTm", oTm[:, :, :])
                barrier()
                done(MW["kept"][0])
                sp.need(pe.last(), act.last(), dve.last())
                ahead()
            ca.close()
            with ExitStack() as c1:
                SG = Ring([sb(f"SH{n}", [128, 512], c=c1) for n in range(6)])
                HTh, YH, YL, WH, part, cur, mh = in_parts(c1, "2")
                my = []
                for m_ in range(8):
                    ok, wo, om = weight()
                    nxt = part(3072 if m_ < 7 else 4096)
                    wk, w, wm, hk, wh, wl, msp = cur
                    wh, wl = (x.rearrange("p (k n) -> p k n", k=8) for x in (wh, wl))
                    parts = []
                    for b, (oT, off, kk) in enumerate(((oTs, 0, 4), (oTd, 512, 2), (oTm, 768, 4))):
                        kb, bank, fr = banks.take()
                        c_ = slice(128 * b, 128 * b + 128)
                        mg = mm3(bank, [(bank, (wh[:, k, c_], wl[:, k, c_]), (HTh[:, k, :], HTl[:, k, :])) for k in range(8)], fr, msp, mh)
                        gk, g, fr = SG.take()
                        m = act.op(lambda e: e.activation(g[:, :], bank[:, :], ACT.Sigmoid, bias=gg("bg2")[:, 8 * b + m_:8 * b + m_ + 1]), mg, fr)
                        banks.free(kb, m)
                        kb, bank, fr = banks.take()
                        mw = mms(bank, [(bank[:, :], wo[:, off + 128 * k:off + 128 * k + 128], oT[:, k, :]) for k in range(kk)], fr, om)
                        m = dve.op(lambda e: e.tensor_tensor(g[:, :], g[:, :], bank[:, :], ALU.mult), mw, m)
                        banks.free(kb, m)
                        parts.append((gk, g, m))
                    done(wk, mw)
                    done(ok, mw)
                    WH.free(hk, mw)
                    ahead()
                    (k1, g1, m1), (k2, g2, m2), (k3, g3, m3) = parts
                    m = dve.op(lambda e: e.tensor_tensor(g1[:, :], g1[:, :], g2[:, :], ALU.add), m1, m2)
                    m = dve.op(lambda e: e.tensor_tensor(g1[:, :], g1[:, :], g3[:, :], ALU.add), m, m3)
                    m = split(g1[:, :], YH[:, m_, :], YL[:, m_, :], m)
                    my.append(m)
                    for kx in (k1, k2, k3):
                        SG.free(kx, m)
                    cur = nxt
                proj_out(YH, YL, WH, part, cur, my)
            show("x4", X[:, :, :])
            barrier()
        if stop == "attn2":
            return finish_program(nc, ctx, (pe, dve, act, pool, sp), dsem)

        WD, AD = d["wspill"], d["aspill"]
        K1 = 28
        cw.close()
        with ExitStack() as c0:
            HH_, HL_ = (sb(n, [128, 8, 512], c=c0) for n in ("HTh", "HTl"))
            ur2 = [sb2(f"Q{n}", [128, 2048], c0) for n in range(3)]
            state["ring"] = Ring([a for a, _ in ur2])
            UR = Ring(ur2)
            del state["stop"]
            ahead()
            with ExitStack() as c1:
                hs_ = normed(X, (HH_, HL_), 4, "ffn2", dve.last(), c1)
            barrier()
            h3 = lambda k, s=slice(0, 512): (HH_[:, k, s], HL_[:, k, s])
            uh2 = [sb2(f"UH{n}", [128, 2, 8, 128], c0) for n in range(2)]
            UH = Ring([b for _, b in uh2])
            VR = Ring([sb2(f"VR{n}", [128, 4, 1024], c0) for n in range(2)])
            order = list(range(K1, 32)) + list(range(K1))
            E2 = {}

            def take_u2(n):
                uk, ub, fu = UR.take()
                return uk, [x.rearrange("p (a k n) -> p a k n", a=2, k=8) for x in ub], sp.dma(ub[0], d["u"][n // 2][:, 2 * (n % 2):2 * (n % 2) + 2].rearrange("p a k n -> p (a k n)"), ds(f"u{uk}"), fu)

            def load_u(g):
                if g >= K1:
                    E2["u", g] = [take_u2(2 * g), take_u2(2 * g + 1)]

            def load_v(g):
                vk, vb_, fv = VR.take()
                E2["v", g] = (vk, vb_, sp.dma(vb_[0], d["v"][g], ds(f"v{vk}"), fv))

            with ExitStack() as cx:
                IA = sb("IA", [128, 3, 512], c=cx)
                TS = sb("TS", [128, 4, 8, 2, 16], c=cx)
                TF = sb("TF", [128, 4, 8, 2, 16], c=cx)
                with ExitStack() as c1:
                    TI = sb("TI", [128, 4, 8, 2, 16], U32, c=c1)
                    QT = Ring([sb(f"QT{n}", [128, 2, 512], c=c1) for n in range(2)])
                    QH = Ring([sb(f"QH{n}", [128, 8, 256], c=c1) for n in range(2)])
                    SC = Ring([sb(f"SC{n}", [128, 2, 128], c=c1) for n in range(4)])
                    Qm, Wq = {}, {}
                    for n in range(3):
                        ur2.append(sb2(f"QX{n}", [128, 2048], c1))
                        state["ring"].bufs.append(ur2[-1][0])
                        state["ring"].idle.append((3 + n, []))
                    ahead()

                    def parts(h):
                        wk, w, wm = weight()
                        sk, sub, sm = weight()
                        v8 = lambda a: a.rearrange("p (k n) -> p k n", k=8)
                        wv = v8(ur2[wk][1])
                        hk, wh, hf = QH.take()
                        Wq[h] = (wk, wv, hk, wh, split(v8(w), wh, wv, wm, hf), sk, sub, sm)

                    def queries(h):
                        wk, wv, hk, wh, mw, sk, sub, sm = Wq.pop(h)
                        qk, q, qf = QT.take()
                        ms = []
                        for p in range(2):
                            kb, bank, fr = banks.take()
                            s = slice(128 * p, 128 * p + 128)
                            m = mm3(bank, [(bank[:, :], (wh[:, k, s], wv[:, k, s]), h3(k)) for k in range(8)], fr, mw, *hs_)
                            m2 = act.op(lambda e: e.activation(q[:, p, :], bank[:, :], ACT.Copy), m, qf, alone=True)
                            banks.free(kb, m2)
                            ms.append(m2)
                        done(wk, m)
                        QH.free(hk, m)
                        ahead()
                        Qm[h] = (qk, q, ms, sk, sub, sm)

                    def tops(h):
                        qk, q, ms, sk, sub, sm = Qm.pop(h)
                        for tb in range(4):
                            kb, bank, fr = banks.take()
                            pe.need(fr, sm, *ms)
                            for p in range(2):
                                m = mms(bank, [(bank[:, 128 * p:128 * p + 128], q[:, p, 128 * tb:128 * tb + 128], sub[:, 128 * p:128 * p + 128])])
                            ck, s, fr = SC.take()
                            mc = act.op(lambda e: e.activation(s.rearrange("p a b -> p (a b)"), bank[:, 0:256], ACT.Copy), m, fr, alone=True)
                            banks.free(kb, mc)
                            two = (0, 1)
                            m1 = [dve.op(lambda e: e.max(TS[:, tb, h, p, 0:8], s[:, p, :]), mc, alone=True) for p in two]
                            m1 = [dve.op(lambda e: e.max_index(TI[:, tb, h, p, 0:8], TS[:, tb, h, p, 0:8], s[:, p, :]), m1[p], alone=True) for p in two]
                            m1 = [dve.op(lambda e: e.match_replace(s[:, p, :], TS[:, tb, h, p, 0:8], s[:, p, :], -3e38), m1[p], alone=True) for p in two]
                            m1 = [dve.op(lambda e: e.max(TS[:, tb, h, p, 8:16], s[:, p, :]), m1[p], alone=True) for p in two]
                            m1 = [dve.op(lambda e: e.max_index(TI[:, tb, h, p, 8:16], TS[:, tb, h, p, 8:16], s[:, p, :]), m1[p], alone=True) for p in two]
                            SC.free(ck, *m1)
                        QT.free(qk, m)
                        done(sk, m)
                        ahead()

                    stages(8, (0, parts), (1, queries), (2, tops))
                    dv(lambda e: e.tensor_copy(TF, TI))
                    barrier()
                CD = sb("CD", [128, 8, 256], c=cx)
                C2 = sb("C2", [128, 8, 256], c=cx)
                S16 = sb("S16", [128, 8, 16], c=cx)
                P16 = sb("P16", [128, 8, 16], U32, c=cx)
                A16 = sb("A16", [128, 8, 16], U32, c=cx)
                PF = sb("PF", [128, 2, 8, 16], c=cx)
                SM = sb("SM", [128, 8], c=cx)
                SEL = sb("SEL", [128, 3, 8, 16], c=cx)
                OA = Ring([sb(f"OA{n}", [128, 4, 128], c=cx) for n in range(2)])
                OB = Ring([sb(f"OB{n}", [128, 4, 128], c=cx) for n in range(2)])
                GA = Ring([sb(f"GA{n}", [128, 512], c=cx) for n in range(4)])
                TW = 32
                WS = Ring([sb("WS", [128, 128, TW], c=cx), VR.bufs[1][0].rearrange("p a n -> p (a n)").rearrange("p (i t) -> p i t", t=TW)])
                iota16 = cc("iota")[:, 0:16].unsqueeze(1).to_broadcast([128, 16, 16])
                spilled = {}

                def chosen(tb):
                    st = Stream(dve)
                    ms = []
                    for h in range(8):
                        c3 = CD[:, h, :].rearrange("p (a b) -> p a b", a=16)
                        a_ = TS[:, tb, h, 0, :].unsqueeze(2).to_broadcast([128, 16, 16])
                        b_ = TS[:, tb, h, 1, :].unsqueeze(1).to_broadcast([128, 16, 16])
                        ms.append(dve.op(lambda e: e.tensor_tensor(c3, a_, b_, ALU.add), chosen.last, alone=True))
                    yield
                    ms = [dve.op(lambda e: e.max(S16[:, h, 0:8], CD[:, h, :]), ms[h], alone=True) for h in range(8)]
                    yield
                    mi = [dve.op(lambda e: e.max_index(P16[:, h, 0:8], S16[:, h, 0:8], CD[:, h, :]), ms[h], alone=True) for h in range(8)]
                    yield
                    ms = [dve.op(lambda e: e.match_replace(C2[:, h, :], S16[:, h, 0:8], CD[:, h, :], -3e38), ms[h], alone=True) for h in range(8)]
                    yield
                    ms = [dve.op(lambda e: e.max(S16[:, h, 8:16], C2[:, h, :]), ms[h], alone=True) for h in range(8)]
                    yield
                    ms = [dve.op(lambda e: e.max_index(P16[:, h, 8:16], S16[:, h, 8:16], C2[:, h, :]), ms[h], alone=True) for h in range(8)]
                    yield
                    st.op(lambda e: e.tensor_scalar(A16, P16, 4, None, ALU.logical_shift_right), *ms, *mi)
                    st.op(lambda e: e.tensor_copy(PF[:, 0], A16))
                    st.op(lambda e: e.tensor_scalar(A16, P16, 15, None, ALU.bitwise_and))
                    mp = st.op(lambda e: e.tensor_copy(PF[:, 1], A16))
                    yield
                    for p, buf in ((0, CD), (1, C2)):
                        ms = []
                        for h in range(8):
                            c3 = buf[:, h, :].rearrange("p (a b) -> p a b", a=16)
                            pos = PF[:, p, h, :].unsqueeze(2).to_broadcast([128, 16, 16])
                            ms.append(dve.op(lambda e: e.tensor_tensor(c3, pos, iota16, ALU.is_equal), mp, alone=True))
                        yield
                        for h in range(8):
                            c3 = buf[:, h, :].rearrange("p (a b) -> p a b", a=16)
                            f_ = TF[:, tb, h, p, :].unsqueeze(1).to_broadcast([128, 16, 16])
                            ms[h] = dve.op(lambda e: e.tensor_tensor(c3, c3, f_, ALU.mult), ms[h], alone=True)
                        yield
                        ml = st.op(lambda e: e.tensor_reduce(SEL[:, p], buf.rearrange("p h (a b) -> p h a b", a=16), AX.X, ALU.add), *ms)
                        yield
                    m = st.op(lambda e: e.tensor_tensor(PF[:, 0], S16, S16[:, :, 0:1].to_broadcast([128, 8, 16]), ALU.subtract))
                    m = act.op(lambda e: e.activation(PF[:, 1], PF[:, 0], ACT.Exp), m, alone=True)
                    st.op(lambda e: e.tensor_reduce(SM, PF[:, 1], AX.X, ALU.add), m)
                    st.op(lambda e: e.reciprocal(SM, SM))
                    m = st.op(lambda e: e.tensor_tensor(SEL[:, 2], PF[:, 1], SM.unsqueeze(2).to_broadcast([128, 8, 16]), ALU.mult))
                    yield
                    kb, bank, fr = banks.take()
                    m = flips([(bank[:, 128 * a:128 * a + 128], SEL[:, a].rearrange("p h s -> p (h s)")) for a in range(3)], fr, m)
                    m = act.op(lambda e: e.activation(IA[:, :, 128 * tb:128 * tb + 128], bank[:, 0:384].rearrange("p (a t) -> p a t", a=3), ACT.Copy), m, alone=True)
                    banks.free(kb, m)
                    chosen.last = [st.at, m]
                    chosen.ready = m
                    yield

                chosen.last = None
                cur, H4 = {}, {}

                def hot(n):
                    ak, a, fa = OA.take()
                    bk, b, fb = OB.take()
                    ms = []
                    for j in range(4):
                        t = 4 * n + j
                        ms.append(dve.op(lambda e: e.tensor_scalar(a[:, j, :], cc("iota"), IA[:, 0, t:t + 1], None, ALU.is_equal), fa, chosen.ready, alone=True))
                        ms.append(dve.op(lambda e: e.tensor_scalar(b[:, j, :], cc("iota"), IA[:, 1, t:t + 1], IA[:, 2, t:t + 1], ALU.is_equal, ALU.mult), fb, alone=True))
                    H4[n] = (ak, a, bk, b, ms)

                def outer(n):
                    ak, a, bk, b, ms = H4.pop(n)
                    if (4 * n) % TW == 0:
                        cur["w"] = WS.take()
                    wk, ws, fw = cur["w"]
                    kb, bank, fr = banks.take()
                    pe.need(ms, fr)
                    for j in range(4):
                        m = mms(bank, [(bank[:, 128 * j:128 * j + 128], a[:, j, :], b[:, j, :])])
                    OA.free(ak, m)
                    OB.free(bk, m)
                    t0 = (4 * n) % TW
                    o = ws[:, :, t0:t0 + 4].rearrange("p i t -> p t i")
                    mc = act.op(lambda e: e.activation(o, bank.rearrange("p (t i) -> p t i", t=4), ACT.Copy), m, fw, alone=True)
                    banks.free(kb, mc)
                    cur.setdefault("m", []).append(mc)
                    if t0 + 4 == TW:
                        c = 4 * n // TW
                        m = act.dma(WD[:, :, c * TW:(c + 1) * TW].rearrange("i p t -> p i t"), ws, ds(f"ws{wk}"), cur.pop("m"))
                        WS.free(wk, m)
                        spilled[wk] = m

                def matrix():
                    for tb in range(4):
                        yield from chosen(tb)
                        for n in range(33):
                            if n < 32:
                                hot(32 * tb + n)
                            if n >= 1:
                                outer(32 * tb + n - 1)
                            yield

                def acts(uh, ul, j, *marks):
                    kb, bank, fr = banks.take()
                    return kb, bank, mm3(bank, [(bank, (uh[:, j, k, :], ul[:, j, k, :]), h3(k)) for k in range(8)], fr, *marks)

                def take_u(n):
                    uk, ub, fu = UR.take()
                    return uk, [x.rearrange("p (a k n) -> p a k n", a=2, k=8) for x in ub], sp.dma(ub[0], d["u"][n // 2][:, 2 * (n % 2):2 * (n % 2) + 2].rearrange("p a k n -> p (a k n)"), ds(f"u{uk}"), fu)

                def prep_u(u):
                    uk, ub, um = u
                    hk, uh, fh = UH.take()
                    return uk, ub[1], hk, uh, split(ub[0], uh, ub[1], um, fh)

                def firsts():
                    us = [take_u(n) for n in range(2)]
                    pr = [prep_u(us.pop(0))]
                    for n in range(2 * K1):
                        if n + 2 < 2 * K1:
                            us.append(take_u(n + 2))
                        if us:
                            pr.append(prep_u(us.pop(0)))
                        uk, ub, hk, uh, um = pr.pop(0)
                        for j in range(2):
                            kb, bank, m = acts(uh, ub, j, um)
                            ak, ga, fa = GA.take()
                            m2 = act.op(lambda e: e.activation(ga, bank, ACT.Gelu), m, fa, alone=True)
                            banks.free(kb, m2)
                            m3 = act.dma(AD[n // 2, :, 2 * (n % 2) + j, :], ga, ds(f"ga{ak}"), m2)
                            GA.free(ak, m3)
                            spilled["a%d" % ak] = m3
                            if j:
                                UR.free(uk, m)
                                UH.free(hk, m)
                            yield

                weave((firsts(), 4 * K1), (matrix(), 4 * (13 + 33)))
                load_u(order[0])
                load_v(order[0])
                sp.need(*spilled.values())
                barrier()
            with ExitStack() as c1:
                GA = Ring([sb(f"GB{n}", [128, 512], c=c1) for n in range(2)])
                VH = Ring([sb(f"VH{n}", [128, 4, 512], c=c1) for n in range(2)])
                GL = Ring([sb(f"GL{n}", [128, 4, 512], c=c1) for n in range(2)])
                GH = Ring([sb(f"GH{n}", [128, 4, 512], c=c1) for n in range(2)])
                WW = Ring([sb(f"WW{n}", [128, 4, 512], c=c1) for n in range(2)])
                Vs = {}
                L, Gs, U = {}, {}, {}

                def load_w(g):
                    wk, wb, fw = WW.take()
                    L["w", g] = (wk, wb, sp.dma(wb, WD[4 * g:4 * g + 4, :, :].rearrange("i p t -> p i t"), ds(f"ww{wk}"), fw))

                def load_a(g):
                    if g < K1 and ("a", g) not in L and UH.idle:
                        ak, a, fa = UH.take()
                        a = uh2[ak][0].rearrange("p a k n -> p (a k n)").rearrange("p (a n) -> p a n", a=4)
                        L["a", g] = (ak, a, sp.dma(a, AD[g], ds(f"al{ak}"), fa))

                def parts_u(g):
                    if g >= K1:
                        U[g] = []
                        for uk, ub, um in E2.pop(("u", g)):
                            k2, uh, f2 = UH.take()
                            U[g].append((uk, ub[1], k2, uh, split(ub[0], uh, ub[1], um, f2)))

                def first(g):
                    wk, wb, wm = L.pop(("w", g))
                    gk, gl, fg = GL.take()
                    hk, gh, fh = GH.take()
                    if g < K1:
                        ak, a, am = L.pop(("a", g))
                        m3 = dve.op(lambda e: e.tensor_tensor(wb, a, wb, ALU.mult), am, wm, alone=True)
                        UH.free(ak, m3)
                        gm = [split(wb, gh, gl, m3, fh, fg)]
                    else:
                        gm = []
                        for i, (uk, ub, k2, uh, um) in enumerate(U.pop(g)):
                            for j in range(2):
                                kb, bank, fr = banks.take()
                                m = mm3(bank, [(bank, (uh[:, j, k, :], ub[:, j, k, :]), h3(k)) for k in range(8)], fr, um)
                                a = 2 * i + j
                                ak, ga, fa = GA.take()
                                m2 = act.op(lambda e: e.activation(ga, bank, ACT.Gelu), m, fa, alone=True)
                                banks.free(kb, m2)
                                m3 = dve.op(lambda e: e.tensor_tensor(wb[:, a, :], ga, wb[:, a, :], ALU.mult), m2, wm, alone=True)
                                GA.free(ak, m3)
                                gm.append(split(wb[:, a, :], gh[:, a, :], gl[:, a, :], m3, fh, fg))
                            UR.free(uk, m)
                            UH.free(k2, m)
                    WW.free(wk, gm)
                    Gs[g] = (gk, gl, hk, gh, gm)

                def prep_v(n):
                    g, half_ = order[n // 2], n % 2
                    vk, vb_, vm = E2["v", g]
                    k, vh, fv = VH.take()
                    c = slice(512 * half_, 512 * half_ + 512)
                    Vs[n] = (k, vh, vb_[1][:, :, c], split(vb_[0][:, :, c], vh, vb_[1][:, :, c], vm, fv))

                def second(n):
                    g, half_ = order[n // 2], n % 2
                    gk, gl, hk, gh, gm = Gs[g]
                    vk = E2["v", g][0]
                    k, vh, vl, vs_ = Vs.pop(n)
                    for tb in range(4):
                        kb, bank, fr = banks.take()
                        t = slice(128 * tb, 128 * tb + 128)
                        m = mm3(bank, [(bank, (gh[:, a, t], gl[:, a, t]), (vh[:, a, :], vl[:, a, :])) for a in range(4)], fr, gm, vs_)
                        o = X[:, tb, 512 * half_:512 * half_ + 512]
                        ma = dve.op(lambda e: e.tensor_tensor(o, o, bank, ALU.add), m, xm[2 * tb + half_], alone=True)
                        xm[2 * tb + half_] = ma
                        banks.free(kb, ma)
                    VH.free(k, m)
                    if half_:
                        GL.free(gk, m)
                        GH.free(hk, m)
                        VR.free(vk, m)

                xm = [None] * 8
                load_w(order[0])
                parts_u(order[0])
                first(order[0])
                load_u(order[1])
                load_w(order[1])
                load_a(order[1])
                load_v(order[1])
                prep_v(0)
                for n in range(64):
                    k = n // 2
                    if n % 2 == 0:
                        prep_v(n + 1)
                        if k + 1 < 32:
                            parts_u(order[k + 1])
                        second(n)
                        if k + 2 < 32:
                            load_w(order[k + 2])
                            load_a(order[k + 2])
                        continue
                    if k + 1 < 32:
                        first(order[k + 1])
                    if k + 2 < 32:
                        load_a(order[k + 2])
                        load_u(order[k + 2])
                    if n + 1 < 64:
                        prep_v(n + 1)
                    second(n)
                    if k + 2 < 32:
                        load_v(order[k + 2])
            m = sp.dma(out.rearrange("(b p) n -> p b n", p=128), X, ds("out"), *xm)
            sp.need(m)
        finish_program(nc, ctx, (pe, dve, act, pool, sp), dsem)


def finish_program(nc, ctx, queues, dsem):
    pe, dve, act, pool, sp = queues
    for s, n in dsem.values():
        sp.need((s, n))
    with nc.Block() as block:
        block.tensor(lambda e: pe.run(e))
        block.vector(lambda e: dve.run(e))
        block.scalar(lambda e: act.run(e))
        block.gpsimd(lambda e: pool.run(e))
        block.sync(lambda e: sp.run(e))


def kernel(**inputs):
    import concourse.bacc as bacc
    from concourse.bass_utils import run_bass_kernel_spmd

    nc = bacc.Bacc("TRN2", target_bir_lowering=False, num_devices=1)
    arrays, sizes = lay({k: np.asarray(v) for k, v in inputs.items()})
    d = {n: nc.dram_tensor("in_" + n, a.shape, F32, kind="ExternalInput").ap() for n, a in arrays.items()}
    d["aspill"] = nc.dram_tensor("aspill", (32, 128, 4, 512), F32, kind="Internal").ap()
    d["hs"] = nc.dram_tensor("hs", (1408, 1028), F32, kind="Internal").ap()
    d["os"] = nc.dram_tensor("os", (1408, 1024), F32, kind="Internal").ap()
    d["wspill"] = nc.dram_tensor("wspill", (128, 128, 512), F32, kind="Internal").ap()
    out = nc.dram_tensor("out_0", (512, 1024), F32, kind="ExternalOutput").ap()
    program(nc, d, out, sizes)
    r = run_bass_kernel_spmd(nc, [{"in_" + n: a for n, a in arrays.items()}], core_ids=[0])
    return r.results[0]["out_0"].reshape(1, 512, 1024)
```
